# Optimizing a Trainium2 kernel written in Bass

```python
import math
import jax, jax.numpy as jnp
from jax import lax
import numpy as np

D_MODEL = 1024
BATCH = 1
SEQ = 1024
DEPTH = 1
DEC_BATCH = 8
DEC_SEQ = 8
PAST_LEN = 2048
PAGE_SIZE = 128

GLA_HEADS = 4
GLA_DK = 128
GLA_DV = 256
GLA_RANK = 16
GLA_TAU = 16.0
GLA_CHUNK = 64
SWA_HEADS = 16
SWA_KV_HEADS = 2
SWA_GROUP = SWA_HEADS // SWA_KV_HEADS
SWA_HEAD_DIM = 64
WINDOW = 128
SWA_BLOCK = WINDOW
PEER_HEADS = 8
PEER_NKEYS = 128
PEER_N_EXPERTS = PEER_NKEYS * PEER_NKEYS
PEER_QDIM = 256
PEER_HALF = PEER_QDIM // 2
PEER_TOPK = 16
PEER_BLOCK = 256
EPS = 1e-6

GLA_QK = GLA_HEADS * GLA_DK
GLA_V = GLA_HEADS * GLA_DV
SWA_Q = SWA_HEADS * SWA_HEAD_DIM
SWA_KV = SWA_KV_HEADS * SWA_HEAD_DIM
IN_SIZES = (GLA_QK, GLA_QK, GLA_V, GLA_V, GLA_RANK, SWA_Q, SWA_KV, SWA_KV, D_MODEL, D_MODEL)
IN_WIDTH = sum(IN_SIZES)

kernel_name = "gla_swa_sink_peer_hybrid_step"

def rmsnorm(x, g):
    xf = x.astype(jnp.float32)
    y = xf * lax.rsqrt(jnp.mean(xf * xf, axis=-1, keepdims=True) + EPS) * g.astype(jnp.float32)
    return y.astype(x.dtype)

def gla_chunked(q, k, v, log_a, s0):
    B, T, H, _ = q.shape
    dv = v.shape[-1]
    c = math.gcd(T, GLA_CHUNK)
    n = T // c

    def to_chunks(t):
        return t.astype(jnp.float32).reshape(B, n, c, H, t.shape[-1]).transpose(1, 0, 3, 2, 4)

    qc, kc, vc, ac = to_chunks(q), to_chunks(k), to_chunks(v), to_chunks(log_a)
    causal = jnp.tril(jnp.ones((c, c), dtype=bool))[:, :, None]

    def step(S, inp):
        qi, ki, vi, ai = inp
        b = jnp.cumsum(ai, axis=-2)
        o_inter = jnp.einsum('bhid,bhde->bhie', qi * jnp.exp(b), S)
        rel = jnp.where(causal, b[:, :, :, None, :] - b[:, :, None, :, :], -jnp.inf)
        scores = jnp.einsum('bhid,bhjd,bhijd->bhij', qi, ki, jnp.exp(rel))
        o = o_inter + jnp.einsum('bhij,bhje->bhie', scores, vi)
        b_last = b[:, :, -1:, :]
        S_new = jnp.exp(b_last[:, :, 0, :])[..., None] * S + jnp.einsum(
            'bhjd,bhje->bhde', ki * jnp.exp(b_last - b), vi)
        return S_new, o

    S, o = lax.scan(step, s0.astype(jnp.float32), (qc, kc, vc, ac))
    o = o.transpose(1, 0, 3, 2, 4).reshape(B, T, H, dv)
    return o, S

def banded_sink_attention(q, k, v, q_pos, k_pos, sinks):
    s = jnp.einsum('bnqhgd,bnkhd->bnhgqk', q, k).astype(jnp.float32) * (SWA_HEAD_DIM ** -0.5)
    diff = q_pos[:, :, None] - k_pos[:, None, :]
    mask = (diff >= 0) & (diff < WINDOW) & (k_pos[:, None, :] >= 0)
    s = jnp.where(mask[None, :, None, None], s, -jnp.inf)
    sink = sinks.astype(jnp.float32)[:, :, None, None]
    m = jnp.maximum(jnp.max(s, axis=-1, keepdims=True), sink)
    e = jnp.exp(s - m)
    p = e / (jnp.sum(e, axis=-1, keepdims=True) + jnp.exp(sink - m))
    return jnp.einsum('bnhgqk,bnkhd->bnqhgd', p.astype(v.dtype), v)

def swa_prompt(q, k, v, sinks):
    B, T = q.shape[:2]
    nb = T // SWA_BLOCK
    qb = q.reshape(B, nb, SWA_BLOCK, SWA_KV_HEADS, SWA_GROUP, SWA_HEAD_DIM)
    kb = k.reshape(B, nb, SWA_BLOCK, SWA_KV_HEADS, SWA_HEAD_DIM)
    vb = v.reshape(B, nb, SWA_BLOCK, SWA_KV_HEADS, SWA_HEAD_DIM)
    prev = lambda t: jnp.concatenate([jnp.zeros_like(t[:, :1]), t[:, :-1]], axis=1)
    kk = jnp.concatenate([prev(kb), kb], axis=2)
    vv = jnp.concatenate([prev(vb), vb], axis=2)
    pos = jnp.arange(T, dtype=jnp.int32).reshape(nb, SWA_BLOCK)
    k_pos = jnp.concatenate([pos - SWA_BLOCK, pos], axis=1)
    o = banded_sink_attention(qb, kk, vv, pos, k_pos, sinks).reshape(B, T, SWA_Q)
    L = min(WINDOW, T)
    return o, k[:, T - L:], v[:, T - L:]

def swa_sample(q, k, v, win_k, win_v, sinks):
    B, T = q.shape[:2]
    L = win_k.shape[1]
    kk = jnp.concatenate([win_k.astype(k.dtype), k], axis=1)
    vv = jnp.concatenate([win_v.astype(v.dtype), v], axis=1)
    q_pos = (PAST_LEN + jnp.arange(T, dtype=jnp.int32))[None]
    k_pos = (PAST_LEN - L + jnp.arange(L + T, dtype=jnp.int32))[None]
    o = banded_sink_attention(q[:, None], kk[:, None], vv[:, None], q_pos, k_pos, sinks)
    return o.reshape(B, T, SWA_Q), kk[:, -L:], vv[:, -L:]

def peer_ffn(xn, w_q, keys1, keys2, u, v):
    shp = xn.shape
    xt = xn.reshape(-1, D_MODEL)
    n = xt.shape[0]
    q = (xt @ w_q).astype(jnp.float32).reshape(n, PEER_HEADS, 2, PEER_HALF)
    s1 = jnp.einsum('nhd,hkd->nhk', q[:, :, 0], keys1.astype(jnp.float32))
    s2 = jnp.einsum('nhd,hkd->nhk', q[:, :, 1], keys2.astype(jnp.float32))
    v1, i1 = lax.top_k(s1, PEER_TOPK)
    v2, i2 = lax.top_k(s2, PEER_TOPK)
    cand = (v1[..., :, None] + v2[..., None, :]).reshape(n, PEER_HEADS, PEER_TOPK * PEER_TOPK)
    cand_idx = (i1[..., :, None] * PEER_NKEYS + i2[..., None, :]).reshape(n, PEER_HEADS, PEER_TOPK * PEER_TOPK)
    top_s, sel = lax.top_k(cand, PEER_TOPK)
    idx = jnp.take_along_axis(cand_idx, sel, axis=-1)
    g = jax.nn.softmax(top_s, axis=-1)
    hk = PEER_HEADS * PEER_TOPK
    pad = (-n) % PEER_BLOCK
    nb = (n + pad) // PEER_BLOCK
    xp = jnp.pad(xt, ((0, pad), (0, 0))).reshape(nb, PEER_BLOCK, D_MODEL)
    ip = jnp.pad(idx.reshape(n, hk), ((0, pad), (0, 0))).reshape(nb, PEER_BLOCK, hk)
    gp = jnp.pad(g.reshape(n, hk), ((0, pad), (0, 0))).astype(xt.dtype).reshape(nb, PEER_BLOCK, hk)

    def block(args):
        xb, ib, gb = args
        ub = jnp.take(u, ib, axis=0)
        act = jax.nn.gelu(jnp.einsum('pd,ped->pe', xb, ub), approximate=False)
        vb = jnp.take(v, ib, axis=0)
        return jnp.einsum('pe,ped->pd', gb * act, vb)

    out = lax.map(block, (xp, ip, gp))
    return out.reshape(-1, D_MODEL)[:n].reshape(shp)

def hybrid_layer(x, gla_s0, win_k, win_v, is_prompt, norm_mix, w_in, gla_w_decay, gla_b_decay,
                 gla_norm, swa_sinks, w_branch_a, w_branch_b, w_out, norm_ffn,
                 peer_w_q, peer_keys1, peer_keys2, peer_u, peer_v):
    B, T, _ = x.shape
    xn = rmsnorm(x, norm_mix)
    z = xn @ w_in
    splits = [int(s) for s in np.cumsum(IN_SIZES)[:-1]]
    gq, gk, gv, gg, glr, sq, sk, sv, gate_a, gate_b = jnp.split(z, splits, axis=-1)
    log_a = jax.nn.log_sigmoid((glr @ gla_w_decay + gla_b_decay).astype(jnp.float32)) / GLA_TAU
    o_a, s_new = gla_chunked(
        (gq * (GLA_DK ** -0.5)).reshape(B, T, GLA_HEADS, GLA_DK),
        gk.reshape(B, T, GLA_HEADS, GLA_DK),
        gv.reshape(B, T, GLA_HEADS, GLA_DV),
        log_a.reshape(B, T, GLA_HEADS, GLA_DK),
        gla_s0)
    o_a = rmsnorm(o_a, gla_norm).astype(x.dtype) * jax.nn.silu(gg.reshape(B, T, GLA_HEADS, GLA_DV))
    o_a = o_a.reshape(B, T, GLA_V)
    q = sq.reshape(B, T, SWA_KV_HEADS, SWA_GROUP, SWA_HEAD_DIM)
    k = sk.reshape(B, T, SWA_KV_HEADS, SWA_HEAD_DIM)
    v = sv.reshape(B, T, SWA_KV_HEADS, SWA_HEAD_DIM)
    sinks = swa_sinks.reshape(SWA_KV_HEADS, SWA_GROUP)
    if is_prompt:
        o_b, new_k, new_v = swa_prompt(q, k, v, sinks)
    else:
        o_b, new_k, new_v = swa_sample(q, k, v, win_k, win_v, sinks)
    merged = jax.nn.sigmoid(gate_a) * (o_a @ w_branch_a) + jax.nn.sigmoid(gate_b) * (o_b @ w_branch_b)
    h = x + merged @ w_out
    h = h + peer_ffn(rmsnorm(h, norm_ffn), peer_w_q, peer_keys1, peer_keys2, peer_u, peer_v)
    return h, new_k, new_v, s_new.astype(x.dtype)

def setup_inputs(seed: int = 0) -> dict:
    key = jax.random.key(seed)
    ks = jax.random.split(key, 24)
    f32 = jnp.float32
    nrm = lambda k, shp, s: jax.random.normal(k, shp, f32) * s
    win_buf = min(WINDOW, PAST_LEN)
    return {
        "x_prompt": nrm(ks[0], (BATCH, SEQ, D_MODEL), 1.0),
        "x_sample": nrm(ks[1], (DEC_BATCH, DEC_SEQ, D_MODEL), 1.0),
        "cache_win_k": nrm(ks[2], (DEPTH, DEC_BATCH, win_buf, SWA_KV_HEADS, SWA_HEAD_DIM), 1.0),
        "cache_win_v": nrm(ks[3], (DEPTH, DEC_BATCH, win_buf, SWA_KV_HEADS, SWA_HEAD_DIM), 1.0),
        "state_gla": nrm(ks[4], (DEPTH, DEC_BATCH, GLA_HEADS, GLA_DK, GLA_DV), 1.0),
        "norm_mix": 1.0 + nrm(ks[5], (DEPTH, D_MODEL), 0.02),
        "w_in": nrm(ks[6], (DEPTH, D_MODEL, IN_WIDTH), D_MODEL ** -0.5),
        "gla_w_decay": nrm(ks[7], (DEPTH, GLA_RANK, GLA_QK), GLA_RANK ** -0.5),
        "gla_b_decay": nrm(ks[8], (DEPTH, GLA_QK), 0.1),
        "gla_norm": 1.0 + nrm(ks[9], (DEPTH, GLA_DV), 0.02),
        "swa_sinks": nrm(ks[10], (DEPTH, SWA_HEADS), 0.5),
        "w_branch_a": nrm(ks[11], (DEPTH, GLA_V, D_MODEL), GLA_V ** -0.5),
        "w_branch_b": nrm(ks[12], (DEPTH, SWA_Q, D_MODEL), SWA_Q ** -0.5),
        "w_out": nrm(ks[13], (DEPTH, D_MODEL, D_MODEL), D_MODEL ** -0.5),
        "norm_ffn": 1.0 + nrm(ks[14], (DEPTH, D_MODEL), 0.02),
        "peer_w_q": nrm(ks[15], (DEPTH, D_MODEL, PEER_HEADS * PEER_QDIM), D_MODEL ** -0.5),
        "peer_keys1": nrm(ks[16], (DEPTH, PEER_HEADS, PEER_NKEYS, PEER_HALF), PEER_HALF ** -0.5),
        "peer_keys2": nrm(ks[17], (DEPTH, PEER_HEADS, PEER_NKEYS, PEER_HALF), PEER_HALF ** -0.5),
        "peer_u": nrm(ks[18], (DEPTH, PEER_N_EXPERTS, D_MODEL), D_MODEL ** -0.5),
        "peer_v": nrm(ks[19], (DEPTH, PEER_N_EXPERTS, D_MODEL), PEER_HEADS ** -0.5),
        "norm_final": 1.0 + nrm(ks[20], (D_MODEL,), 0.02),
    }

def reference(x_prompt, x_sample, cache_win_k, cache_win_v, state_gla, norm_mix, w_in, gla_w_decay,
              gla_b_decay, gla_norm, swa_sinks, w_branch_a, w_branch_b, w_out, norm_ffn,
              peer_w_q, peer_keys1, peer_keys2, peer_u, peer_v, norm_final):
    hp, hs = x_prompt, x_sample
    pk, pv, ps, sk, sv, ss = [], [], [], [], [], []
    for l in range(DEPTH):
        params = (norm_mix[l], w_in[l], gla_w_decay[l], gla_b_decay[l], gla_norm[l], swa_sinks[l],
                  w_branch_a[l], w_branch_b[l], w_out[l], norm_ffn[l],
                  peer_w_q[l], peer_keys1[l], peer_keys2[l], peer_u[l], peer_v[l])
        s0 = jnp.zeros((hp.shape[0], GLA_HEADS, GLA_DK, GLA_DV), jnp.float32)
        hp, k1, v1, s1 = hybrid_layer(hp, s0, None, None, True, *params)
        hs, k2, v2, s2 = hybrid_layer(hs, state_gla[l], cache_win_k[l], cache_win_v[l], False, *params)
        pk.append(k1); pv.append(v1); ps.append(s1)
        sk.append(k2); sv.append(v2); ss.append(s2)
    y_prompt = rmsnorm(hp, norm_final)
    y_sample = rmsnorm(hs, norm_final)
    return (y_prompt, y_sample, jnp.stack(pk), jnp.stack(pv), jnp.stack(ps),
            jnp.stack(sk), jnp.stack(sv), jnp.stack(ss))


_drawn_inputs = setup_inputs


def setup_inputs(seed=0):
    import zlib

    import numpy as np

    out = dict(_drawn_inputs(seed))
    spreads = {}
    factors = {'gla_norm': 3.549, 'swa_sinks': 8.0, 'norm_final': 8.688, 'norm_ffn': 3.212}
    for name, (base, spread) in spreads.items():
        noise = np.random.default_rng([zlib.crc32(name.encode()), seed]).standard_normal(out[name].shape)
        drawn = base * np.exp(spread * noise) if base else spread * noise
        out[name] = __import__('jax').numpy.asarray(drawn.astype(out[name].dtype))
    for name, factor in factors.items():
        out[name] = (out[name] * factor).astype(out[name].dtype)
    return out
```

```python
from contextlib import ExitStack

import concourse.bass as bass
from concourse import mybir

F32 = mybir.dt.float32
U32 = mybir.dt.uint32
ALU = mybir.AluOpType
ACT = mybir.ActivationFunctionType
AX_X = mybir.AxisListType.X

P = 128
D = 1024
KT = D // P
SEQ = 1024
SEQS = 8
STEPS = 8
NSAMP = SEQS * STEPS
TOK = SEQ + NSAMP
TILES = SEQ // P
BANK = 512

GLA_HEADS, DK, DV, RANK = 4, 128, 256, 16
SUB = 16
SUBS = P // SUB
CLAMP = 60.0
SWA_HEADS, KV_HEADS, HD, WINDOW = 16, 2, 64, 128
GROUP = SWA_HEADS // KV_HEADS
MASKED = -1e30

HEADS, NKEYS, HALF, TOPK = 8, 128, 128, 16
QD = HEADS * 2 * HALF
LOWEST = -3.0e38
EPS = 1e-6


def wait(eng, sem, value):
    if not isinstance(value, int) or value > 0:
        eng.wait_ge(sem, value)


def wait_alone(eng, sem, value, tick):
    if not isinstance(value, int) or value > 0:
        eng.wait_ge(sem, value)
        eng.sem_inc(tick, 1)


class Chain:

    def __init__(self, eng, sem):
        self.eng, self.sem, self.n = eng, sem, 0

    def step(self, ins):
        ins.then_inc(self.sem, 1)
        self.n += 1

    def link(self, ins):
        self.step(ins)
        self.eng.wait_ge(self.sem, self.n)

    def settle(self):
        self.eng.wait_ge(self.sem, self.n)

    def restart(self):
        if self.n:
            self.settle()
            self.eng.sem_clear(self.sem)
            self.n = 0


CHUNK = 512
GROUPS = [(0, BANK), (BANK, BANK), (2 * BANK, NSAMP)]
SMALL = 2 * KV_HEADS * HD + RANK
KV = KV_HEADS * HD


def project_stage(nc, sem, x_dram, g_mix_dram, w_big_dram, w_small_dram, w_decay_dram, b_decay_dram,
                  z_tok, z_feat, z_kv, z_kT, z_b):
    SLOTS = 3
    TOK_CHUNKS, FEAT_CHUNKS = 8, 4
    NT = TILES + 1
    NF = CHUNK // P * len(GROUPS)
    with ExitStack() as ctx:
        def sb(name, shape, dt=F32):
            return ctx.enter_context(nc.sbuf_tensor(name, shape, dt))

        def pb(name, shape):
            return ctx.enter_context(nc.psum_tensor(name, shape, F32))

        xnT = sb("j_xnT", [P, KT, TOK])
        w = sb("j_w", [P, 2, KT * CHUNK])
        w_small = sb("j_w_small", [P, KT, SMALL])
        w_decay = sb("j_w_decay", [RANK, GLA_HEADS * DK])
        b_decay = sb("j_b_decay", [P, GLA_HEADS])
        g_mix = sb("j_g_mix", [P, D])
        x = sb("j_x", [P, 3, D])
        xn = sb("j_xn", [P, 2, D])
        ident = sb("j_ident", [P, P])
        keep = sb("j_keep", [P, TOK])
        stat = sb("j_stat", [P, NT, 4])
        stage = sb("j_stage", [P, SLOTS, CHUNK])
        low = sb("j_low", [RANK, TOK])
        z = sb("j_z", [P, TOK])
        la = sb("j_la", [P, 2, TOK])
        t_ps = [pb(f"j_t{i}", [P, 4, P]) for i in range(2)]
        m_ps = [pb(f"j_m{i}", [P, BANK]) for i in range(SLOTS)]
        z_ps = [pb(f"j_z{i}", [P, BANK]) for i in range(3)]

        consts = sem("j_consts")
        made = sem("j_made")
        x_in = [sem(f"j_x{i}") for i in range(3)]
        sq_done = sem("j_sq")
        rt_in = sem("j_rt_in")
        rt_done = sem("j_rt")
        xn_ready = sem("j_xn")
        xnT_ps = sem("j_xnT_ps")
        xnT_ready = sem("j_xnT")
        w_in = [sem(f"j_w{i}") for i in range(2)]
        chunk_used = sem("j_chunk_used")
        m_done = sem("j_m_done")
        staged = sem("j_staged")
        stored = [sem(f"j_stored{i}") for i in range(SLOTS)]
        z_done = sem("j_z_done")
        z_taken = sem("j_z_taken")
        abs_done = sem("j_abs")
        log_done = sem("j_log")
        b_ready = sem("j_b")
        b_stored = sem("j_b_stored")
        vstep = sem("j_vstep")
        astep = sem("j_astep")
        pstep = sem("j_pstep")
        block = ctx.enter_context(nc.Block())

        def n_of(t):
            return NSAMP if t == TILES else P

        @block.sync
        def _(sp):
            sp.dma_start(g_mix[:, :], g_mix_dram.to_broadcast([P, D])).then_inc(consts, 16)
            sp.dma_start(w_small[:, :, :], w_small_dram).then_inc(consts, 16)
            sp.dma_start(w_decay[:, :], w_decay_dram).then_inc(consts, 16)
            sp.dma_start(b_decay[:, :], b_decay_dram).then_inc(consts, 16)
            for t in range(NT):
                wait(sp, xn_ready, t - 2)
                sp.dma_start(x[0:n_of(t), t % 3, :], x_dram[t * P:t * P + n_of(t), :]).then_inc(x_in[t % 3], 16)
                if t < 2:
                    sp.dma_start(w[:, t, :], w_big_dram[t]).then_inc(w_in[t], 16)
            with sp.Fori(1, (TOK_CHUNKS + FEAT_CHUNKS) // 2) as i:
                for s in range(2):
                    sp.wait_ge(chunk_used, 2 * i + s - 1)
                    sp.dma_start(w[:, s, :], w_big_dram[bass.ds(2 * i + s, 1), :, :].rearrange("o p n -> p (o n)")
                                 ).then_inc(w_in[s], 16)
            for j in range(GLA_HEADS):
                sp.wait_ge(b_ready, j + 1)
                sp.dma_start(z_b[j], la[:, 1, :]).then_inc(b_stored, 16)
            sp.wait_ge(b_stored, 16 * GLA_HEADS)

        @block.gpsimd
        def _(pool):
            pool.memset(ident[:, :], 0.0).then_inc(pstep, 1)
            pool.wait_ge(pstep, 1)
            pool.affine_select(out=ident[:, :], in_=ident[:, :], compare_op=ALU.not_equal, fill=1.0,
                               base=0, pattern=[[-1, P]], channel_multiplier=1).then_inc(made, 1)
            pool.memset(keep[:, :], 1.0).then_inc(pstep, 1)
            pool.wait_ge(pstep, 2)
            pool.memset(keep[:, 0:SEQ:P], 0.0).then_inc(made, 1)
            pool.memset(keep[:, SEQ:TOK:STEPS], 0.0).then_inc(made, 1)

        @block.scalar
        def _(act):
            act.wait_ge(made, 3)

            def transposed(t):
                n = n_of(t)
                for i in range(2):
                    act.wait_ge(xnT_ps, 2 * t + i + 1)
                    act.activation(xnT[:, 4 * i:4 * i + 4, t * P:t * P + n], t_ps[i][:, :, 0:n],
                                   ACT.Copy).then_inc(xnT_ready, 1)

            for t in range(NT):
                n = n_of(t)
                act.wait_ge(x_in[t % 3], 16 * (t // 3 + 1))
                if t >= 2:
                    act.wait_ge(xnT_ps, 2 * (t - 1))
                act.activation(xn[0:n, t % 2, :], x[0:n, t % 3, :], ACT.Square,
                               accum_out=stat[0:n, t, 0:1]).then_inc(sq_done, 1)
                act.wait_ge(rt_in, t + 1)
                act.activation(stat[0:n, t, 2:3], stat[0:n, t, 1:2], ACT.Sqrt).then_inc(rt_done, 1)
                if t:
                    transposed(t - 1)
            transposed(NT - 1)

            def take(item, slot, use, n, width, func, dst):
                act.wait_ge(m_done, item + 1)
                wait(act, stored[slot], 16 * use)
                act.activation(stage[0:n, slot, 0:width], m_ps[slot][0:n, 0:width], func).then_inc(staged, 1)
                act.wait_ge(staged, item + 1)
                act.dma_start(dst, stage[0:n, slot, 0:width]).then_inc(stored[slot], 16)

            def tokens(c, func):
                for t in range(NT):
                    take(c * NT + t, t % SLOTS, c * (NT // SLOTS) + t // SLOTS, n_of(t), CHUNK, func,
                         z_tok[t * P:t * P + n_of(t), bass.ds(c * CHUNK, CHUNK)])

            for c in range(2):
                tokens(c, ACT.Copy)
            for c in range(2, 4):
                tokens(c, ACT.Silu)
            with act.Fori(4, TOK_CHUNKS) as c:
                tokens(c, ACT.Sigmoid)
            base, uses = TOK_CHUNKS * NT, TOK_CHUNKS * NT // SLOTS

            def features(c):
                for b in range(CHUNK // P):
                    for g, (g0, gn) in enumerate(GROUPS):
                        take(base + c * NF + b * 3 + g, g, uses + c * 4 + b, P, gn, ACT.Copy,
                             z_feat[bass.ds(c * 4 + b, 1), :, g0:g0 + gn].rearrange("o p n -> p (o n)"))

            with act.Fori(0, FEAT_CHUNKS) as c:
                features(c)
            base, uses = base + FEAT_CHUNKS * NF, uses + FEAT_CHUNKS * NF // SLOTS
            for t in range(NT):
                take(base + t, t % SLOTS, uses + t // SLOTS, n_of(t), 2 * KV, ACT.Copy, z_kv[t * P:t * P + n_of(t), :])
            base, uses = base + NT, uses + NT // SLOTS
            for g, (g0, gn) in enumerate(GROUPS):
                take(base + g, g, uses, P, gn, ACT.Copy, z_kT[:, g0:g0 + gn])
            for g, (g0, gn) in enumerate(GROUPS):
                act.wait_ge(m_done, base + 3 + g + 1)
                act.activation(low[:, g0:g0 + gn], m_ps[g][0:RANK, 0:gn], ACT.Copy).then_inc(staged, 1)
            for j in range(GLA_HEADS):
                act.wait_ge(z_taken, 3 * (j + 1))
                wait(act, b_ready, j)
                act.activation(la[:, 0, :], z[:, :], ACT.Abs).then_inc(abs_done, 1)
                act.wait_ge(abs_done, 3 * j + 1)
                act.activation(la[:, 0, :], la[:, 0, :], ACT.Exp, scale=-1.0).then_inc(abs_done, 1)
                act.wait_ge(abs_done, 3 * j + 2)
                act.activation(la[:, 0, :], la[:, 0, :], ACT.Ln, bias=1.0).then_inc(abs_done, 1)
            for slot in range(SLOTS):
                act.wait_ge(stored[slot], 16 * (uses + 1))

        @block.vector
        def _(dve):
            chain = Chain(dve, vstep)
            dve.wait_ge(consts, 64)
            for t in range(NT):
                n = n_of(t)
                dve.wait_ge(sq_done, t + 1)
                dve.tensor_scalar(stat[0:n, t, 1:2], stat[0:n, t, 0:1], 1.0 / D, EPS, ALU.mult,
                                  ALU.add).then_inc(rt_in, 1)
                dve.wait_ge(rt_done, t + 1)
                chain.link(dve.reciprocal(stat[0:n, t, 3:4], stat[0:n, t, 2:3]))
                dve.scalar_tensor_tensor(out=xn[0:n, t % 2, :], in0=x[0:n, t % 3, :], scalar=stat[0:n, t, 3:4],
                                         in1=g_mix[0:n, :], op0=ALU.mult, op1=ALU.mult).then_inc(xn_ready, 1)
            for j in range(GLA_HEADS):
                wait(dve, abs_done, 3 * j)
                for g, (g0, gn) in enumerate(GROUPS):
                    dve.wait_ge(z_done, 3 * j + g + 1)
                    if g == 0 and j:
                        dve.wait_ge(b_ready, j)
                    dve.tensor_scalar(z[:, g0:g0 + gn], z_ps[g][:, 0:gn], b_decay[:, j:j + 1], None,
                                      ALU.add).then_inc(z_taken, 1)
                dve.wait_ge(abs_done, 3 * (j + 1))
                chain.link(dve.scalar_tensor_tensor(out=z[:, :], in0=z[:, :], scalar=0.0, in1=la[:, 0, :],
                                                    op0=ALU.min, op1=ALU.subtract))
                wait(dve, b_stored, 16 * j)
                chain.link(dve.tensor_tensor_scan(la[:, 1, :], keep[:, :], z[:, :], 0.0, ALU.mult, ALU.add))
                dve.tensor_scalar(la[:, 1, :], la[:, 1, :], 1.0 / 16.0, None, ALU.mult).then_inc(b_ready, 1)

        @block.tensor
        def _(pe):
            pe.wait_ge(made, 3)
            pe.wait_ge(consts, 64)
            for t in range(NT):
                n = n_of(t)
                pe.wait_ge(xn_ready, t + 1)
                for i in range(2):
                    wait(pe, xnT_ready, 2 * (t - 1) + i + 1)
                    for j in range(4):
                        k = 4 * i + j
                        last = pe.transpose(t_ps[i][:, j, 0:n], xn[0:n, t % 2, k * P:(k + 1) * P], ident[0:n, 0:n])
                    last.then_inc(xnT_ps, 1)
            pe.wait_ge(xnT_ready, 2 * NT)

            def product(item, slot, m, width, lhs, rhs):
                wait(pe, staged, item - SLOTS + 1)
                for k in range(KT):
                    last = pe.matmul(m_ps[slot][0:m, 0:width], lhs(k), rhs(k), start=(k == 0), stop=(k == KT - 1))
                last.then_inc(m_done, 1)
                return last

            def tokens(i, s):
                c = 2 * i + s
                pe.wait_ge(w_in[s], 16 * (i + 1))
                for t in range(NT):
                    product(c * NT + t, t % SLOTS, n_of(t), CHUNK,
                            lambda k: xnT[:, k, t * P:t * P + n_of(t)],
                            lambda k: w[:, s, k * CHUNK:(k + 1) * CHUNK])
                pe.wait_ge(m_done, (c + 1) * NT)
                pe.sem_inc(chunk_used, 1)

            for s in range(2):
                tokens(0, s)
            with pe.Fori(1, TOK_CHUNKS // 2) as i:
                for s in range(2):
                    tokens(i, s)
            base = TOK_CHUNKS * NT
            with pe.Fori(0, FEAT_CHUNKS // 2) as i:
                for s in range(2):
                    c = 2 * i + s
                    pe.wait_ge(w_in[s], 16 * (i + TOK_CHUNKS // 2 + 1))
                    for b in range(CHUNK // P):
                        for g, (g0, gn) in enumerate(GROUPS):
                            product(base + c * NF + b * 3 + g, g, P, gn,
                                    lambda k: w[:, s, k * CHUNK + b * P:k * CHUNK + (b + 1) * P],
                                    lambda k: xnT[:, k, g0:g0 + gn])
                    pe.wait_ge(m_done, base + (c + 1) * NF)
                    pe.sem_inc(chunk_used, 1)
            base += FEAT_CHUNKS * NF
            for t in range(NT):
                product(base + t, t % SLOTS, n_of(t), 2 * KV, lambda k: xnT[:, k, t * P:t * P + n_of(t)],
                        lambda k: w_small[:, k, 0:2 * KV])
            base += NT
            for g, (g0, gn) in enumerate(GROUPS):
                product(base + g, g, P, gn, lambda k: w_small[:, k, 0:KV], lambda k: xnT[:, k, g0:g0 + gn])
            for g, (g0, gn) in enumerate(GROUPS):
                product(base + 3 + g, g, RANK, gn, lambda k: w_small[:, k, 2 * KV:SMALL],
                        lambda k: xnT[:, k, g0:g0 + gn])
            pe.wait_ge(staged, base + 6)
            for j in range(GLA_HEADS):
                for g, (g0, gn) in enumerate(GROUPS):
                    wait(pe, z_taken, 3 * (j - 1) + g + 1)
                    pe.matmul(z_ps[g][:, 0:gn], w_decay[:, j * DK:(j + 1) * DK], low[:, g0:g0 + gn],
                              start=True, stop=True).then_inc(z_done, 1)


class Tail:

    def __init__(self, sb, sem, name):
        self.v_gate = sb(name + "gate", [P, D])
        self.ga = sb(name + "ga", [P, D])
        self.gb = sb(name + "gb", [P, D])
        self.x = sb(name + "x", [P, D])
        self.oa = sb(name + "oa", [P, D])
        self.oaT = sb(name + "oaT", [P, KT, P])
        self.obT = sb(name + "obT", [P, KT, P])
        self.mT = sb(name + "mT", [P, KT, P])
        self.h = sb(name + "h", [P, D])
        self.stat = sb(name + "stat", [P, 4, GLA_HEADS])
        self.gates_in = sem(name + "gates_in")
        self.gate_ready = sem(name + "gate_ready")
        self.o_done = sem(name + "o_done")
        self.sq_done = sem(name + "sq_done")
        self.rt_in = sem(name + "rt_in")
        self.rt_done = sem(name + "rt_done")
        self.oa_ready = sem(name + "oa_ready")
        self.turned = sem(name + "turned")
        self.oaT_ready = sem(name + "oaT_ready")
        self.ob_done = sem(name + "ob_done")
        self.obT_ready = sem(name + "obT_ready")
        self.a_done = sem(name + "a_done")
        self.b_done = sem(name + "b_done")
        self.m_ready = sem(name + "m_ready")
        self.mT_ready = sem(name + "mT_ready")
        self.y_done = sem(name + "y_done")
        self.h_ready = sem(name + "h_ready")
        self.h_stored = sem(name + "h_stored")


def mix_stage(nc, sem, x_dram, wa_dram, wb_dram, wo_dram, gla_norm_dram, sinks_dram, sink_rows_dram, mask_dram,
              causal_dram, samp_mask_dram, samp_causal_dram, seg_cols_dram, seg_rows_dram, cache_kT_dram,
              cache_v_dram, cache_k_rows, cache_v_rows, state_dram, z_tok, z_feat, z_kv, z_kT, z_b, h_dram,
              pk_dram, pv_dram, ps_dram, sk_dram, sv_dram, ss_dram):
    QSCALE = DK ** -0.5
    with ExitStack() as outer:
        def sbo(name, shape, dt=F32):
            return outer.enter_context(nc.sbuf_tensor(name, shape, dt))

        wa = sbo("wa", [P, KT, D])
        wb = sbo("wb", [P, KT, D])
        wo = sbo("wo", [P, KT, D])
        gn = sbo("gn", [P, DV])
        ident = sbo("m_ident", [P, P])
        X = outer.enter_context(nc.psum_tensor("X", [P, D], F32))
        O = outer.enter_context(nc.psum_tensor("O", [P, D], F32))
        U = outer.enter_context(nc.psum_tensor("U", [P, D], F32))
        R = outer.enter_context(nc.psum_tensor("R", [P, 2, BANK], F32))


        def tail_norm_act(act, T, t, n, after_head=None):
            for h in range(GLA_HEADS):
                if h == 0:
                    act.wait_ge(T.o_done, GLA_HEADS * (t + 1))
                    wait(act, T.turned, 4 * t - 2)
                act.activation(T.oa[0:n, h * DV:(h + 1) * DV], O[0:n, h * DV:(h + 1) * DV], ACT.Square,
                               accum_out=T.stat[0:n, 0, h:h + 1]).then_inc(T.sq_done, 1)
            act.wait_ge(T.rt_in, t + 1)
            act.activation(T.stat[0:n, 2, :], T.stat[0:n, 1, :], ACT.Sqrt).then_inc(T.rt_done, 1)

        def tail_oa_dve(dve, chain, T, t, n):
            dve.wait_ge(T.sq_done, GLA_HEADS * (t + 1))
            dve.tensor_scalar(T.stat[0:n, 1, :], T.stat[0:n, 0, :], 1.0 / DV, EPS, ALU.mult, ALU.add).then_inc(T.rt_in, 1)
            dve.wait_ge(T.rt_done, t + 1)
            chain.link(dve.reciprocal(T.stat[0:n, 3, :], T.stat[0:n, 2, :]))
            dve.wait_ge(T.gate_ready, t + 1)
            for h in range(GLA_HEADS):
                cols = slice(h * DV, (h + 1) * DV)
                last = dve.scalar_tensor_tensor(out=T.oa[0:n, cols], in0=O[0:n, cols], scalar=T.stat[0:n, 3, h:h + 1],
                                                in1=T.v_gate[0:n, cols], op0=ALU.mult, op1=ALU.mult)
                if h < GLA_HEADS - 1:
                    chain.step(last)
            last.then_inc(T.oa_ready, 1)

        def tail_merge_dve(dve, chain, T, t, n):
            for i in range(2):
                dve.wait_ge(T.turned, 4 * t + i + 1)
                dve.tensor_copy(T.oaT[:, 4 * i:4 * i + 4, 0:n], R[:, i, :].rearrange("p (k n) -> p k n", k=4)[:, :, 0:n]
                                ).then_inc(T.oaT_ready, 1)
            dve.wait_ge(T.gates_in, 64 * (t + 1))
            dve.wait_ge(T.a_done, t + 1)
            chain.link(dve.tensor_tensor(T.ga[0:n, :], O[0:n, :], T.ga[0:n, :], ALU.mult))
            dve.wait_ge(T.b_done, t + 1)
            chain.link(dve.tensor_tensor(T.gb[0:n, :], X[0:n, :], T.gb[0:n, :], ALU.mult))
            dve.tensor_tensor(T.ga[0:n, :], T.ga[0:n, :], T.gb[0:n, :], ALU.add).then_inc(T.m_ready, 1)
            dve.wait_ge(T.y_done, t + 1)
            wait(dve, T.h_stored, 16 * t)
            dve.tensor_tensor(T.h[0:n, :], U[0:n, :], T.x[0:n, :], ALU.add).then_inc(T.h_ready, 1)

        def tail_act(act, T, t, n):
            act.wait_ge(T.ob_done, t + 1)
            act.activation(T.obT[:, :, 0:n], U[:, 0:KT * n].rearrange("p (k n) -> p k n", k=KT),
                           ACT.Copy).then_inc(T.obT_ready, 1)
            for i in range(2):
                act.wait_ge(T.turned, 4 * t + 3 + i)
                act.activation(T.mT[:, 4 * i:4 * i + 4, 0:n], R[:, i, :].rearrange("p (k n) -> p k n", k=4)[:, :, 0:n],
                               ACT.Copy).then_inc(T.mT_ready, 1)

        def turn(pe, T, src, n):
            for i in range(2):
                for j in range(4):
                    k = 4 * i + j
                    last = pe.transpose(R[:, i, j * P:j * P + n], src[0:n, k * P:(k + 1) * P], ident[0:n, 0:n])
                last.then_inc(T.turned, 1)

        def product(pe, out, lhsT, w, n, done):
            for c in range(D // BANK):
                for k in range(KT):
                    last = pe.matmul(out[0:n, c * BANK:(c + 1) * BANK], lhsT[:, k, 0:n], w[:, k, c * BANK:(c + 1) * BANK],
                                     start=(k == 0), stop=(k == KT - 1))
            last.then_inc(done, 1)

        def tail_pe(pe, T, t, n):
            pe.wait_ge(T.obT_ready, t + 1)
            product(pe, X, T.obT, wb, n, T.b_done)
            pe.wait_ge(T.oa_ready, t + 1)
            turn(pe, T, T.oa, n)
            pe.wait_ge(T.oaT_ready, 2 * (t + 1))
            product(pe, O, T.oaT, wa, n, T.a_done)
            pe.wait_ge(T.m_ready, t + 1)
            turn(pe, T, T.ga, n)
            pe.wait_ge(T.mT_ready, 2 * (t + 1))
            product(pe, U, T.mT, wo, n, T.y_done)

        def tail_load(sp, T, t, n):
            r0 = t * P
            for i, dst in ((1, T.v_gate), (2, T.ga), (3, T.gb)):
                sp.dma_start(dst[0:n, :], z_tok[bass.ds(r0, n), i * D:(i + 1) * D]).then_inc(T.gates_in, 16)
            sp.dma_start(T.x[0:n, :], x_dram[bass.ds(r0, n), :]).then_inc(T.gates_in, 16)

        def gate_norm(pool, T, t, n):
            pool.wait_ge(T.gates_in, 64 * (t + 1))
            pool.tensor_tensor(T.v_gate[0:n, :].rearrange("p (h e) -> p h e", h=GLA_HEADS),
                               T.v_gate[0:n, :].rearrange("p (h e) -> p h e", h=GLA_HEADS),
                               gn[0:n, :].unsqueeze(1).to_broadcast([n, GLA_HEADS, DV]), ALU.mult
                               ).then_inc(T.gate_ready, 1)


        with ExitStack() as ctx:
            def sb(name, shape, dt=F32):
                return ctx.enter_context(nc.sbuf_tensor(name, shape, dt))

            T = Tail(sb, sem, "p_")
            q = sb("q", [P, GLA_HEADS, P])
            k = sb("k", [P, GLA_HEADS, P])
            b = sb("b", [P, GLA_HEADS, P])
            v = sb("v", [P, D])
            sq = sb("sq", [P, KT, P])
            kk = sb("kk", [P, KV_HEADS, 2, P])
            vv = sb("vv", [P, 2, KV])
            mask = sb("mask", [P, 2, 2 * P])
            causal = sb("causal", [P, P])
            sinks = sb("sinks", [P, SWA_HEADS])
            rel = sb("rel", [P, 2, SUBS, P])
            qt = sb("qt", [P, 2, P])
            qb = sb("qb", [P, 2, P])
            eb = sb("eb", [P, 2, P])
            kp = sb("kp", [P, 2, P])
            kpT = sb("kpT", [P, 2, P])
            scm = sb("scm", [P, 2, P])
            S = sb("S", [P, GLA_HEADS, DV])
            s = sb("s", [P, SWA_HEADS, 2 * P])
            m = sb("m", [P, 4, SWA_HEADS])
            e_sum = sb("e_sum", [P, SWA_HEADS])
            pT = sb("pT", [P, 2, 4, P])

            consts = sem("m_consts")
            zeroed = sem("zeroed")
            gla_in = sem("gla_in")
            swa_in = sem("swa_in")
            s_done = sem("m_s_done")
            s_taken = sem("m_s_taken")
            neg_ready = sem("neg_ready")
            e_done = sem("m_e_done")
            p_ready = sem("p_ready")
            pT_ps = sem("pT_ps")
            pT_ready = sem("pT_ready")
            rel_ready = sem("rel_ready")
            ex_done = sem("ex_done")
            kq_ready = sem("kq_ready")
            sc_done = sem("sc_done")
            kpT_ready = sem("kpT_ready")
            scm_ready = sem("scm_ready")
            su_done = sem("su_done")
            S_ready = sem("S_ready")
            out_copied = sem("out_copied")
            vstep = sem("m_vstep")
            vtick = sem("m_vtick")
            astep = sem("m_astep")
            pstep = sem("m_pstep")
            block = ctx.enter_context(nc.Block())

            def score_pair(i, j):
                return R[:, j, 0:2 * P] if i % 2 == 0 else X[:, j * BANK:j * BANK + 2 * P]

            def update(h):
                at = (h % 2) * BANK + (h // 2) * DV
                return U[:, at:at + DV]

            @block.sync
            def _(sp):
                def load_gla(t):
                    wait(sp, su_done, GLA_HEADS * t)
                    cols = bass.ds(t * P, P)
                    for dst, src in ((b, z_b[:, :, cols]), (k, z_feat[4:8, :, cols]), (q, z_feat[0:4, :, cols])):
                        sp.dma_start(dst[:, :, :], src.rearrange("h p n -> p h n")).then_inc(gla_in, 16)
                    sp.dma_start(v[:, :], z_tok[cols, 0:D]).then_inc(gla_in, 16)

                def load_swa(t):
                    wait(sp, T.ob_done, t)
                    first = isinstance(t, int) and t == 0
                    sp.dma_start(sq[:, :, :], z_feat[8:16, :, bass.ds(t * P, P)].rearrange("h p n -> p h n")
                                 ).then_inc(swa_in, 16)
                    old = 1 if first else 0
                    start, width = (0, P) if first else (t * P - P, 2 * P)
                    for half in range(2):
                        sp.dma_start(kk[half * HD:(half + 1) * HD, :, :, :].rearrange("d g a n -> d g (a n)")[:, :, old * P:],
                                     z_kT[:, bass.ds(start, width)].rearrange("(g d) n -> d g n", g=KV_HEADS)
                                     ).then_inc(swa_in, 16)
                    sp.dma_start(vv[:, old:, :], z_kv[bass.ds(start, width), KV:2 * KV].rearrange("(a p) c -> p a c", p=P)
                                 ).then_inc(swa_in, 16)

                def load_gates(t):
                    wait(sp, T.h_ready, t)
                    tail_load(sp, T, t, P)

                sp.dma_start(mask[:, :, :], mask_dram).then_inc(consts, 16)
                sp.dma_start(causal[:, :], causal_dram).then_inc(consts, 16)
                sp.dma_start(sinks[:, :], sinks_dram.to_broadcast([P, SWA_HEADS])).then_inc(consts, 16)
                load_swa(0)
                load_gla(0)
                load_gates(0)
                sp.dma_start(gn[:, :], gla_norm_dram.to_broadcast([P, DV])).then_inc(consts, 16)
                for dst, src in ((wb, wb_dram), (wa, wa_dram), (wo, wo_dram)):
                    sp.dma_start(dst[:, :, :], src).then_inc(consts, 16)
                for dst, src in ((pk_dram, z_kv[SEQ - WINDOW:SEQ, 0:KV]), (pv_dram, z_kv[SEQ - WINDOW:SEQ, KV:2 * KV])):
                    sp.dma_start(dst, src).then_inc(out_copied, 16)
                for dst, src, new in ((sk_dram, cache_k_rows, 0), (sv_dram, cache_v_rows, KV)):
                    sp.dma_start(dst[:, 0:WINDOW - STEPS, :], src[:, STEPS:WINDOW, :]).then_inc(out_copied, 16)
                    sp.dma_start(dst[:, WINDOW - STEPS:WINDOW, :],
                                 z_kv[SEQ:TOK, new:new + KV].rearrange("(b s) c -> b s c", s=STEPS)).then_inc(out_copied, 16)

                def tile(t):
                    more = not (isinstance(t, int) and t == TILES - 1)
                    if more:
                        load_gla(t + 1)
                        load_swa(t + 1)
                    sp.wait_ge(T.h_ready, t + 1)
                    sp.dma_start(h_dram[bass.ds(t * P, P), :], T.h[:, :]).then_inc(T.h_stored, 16)
                    if more:
                        load_gates(t + 1)

                tile(0)
                with sp.Fori(1, TILES - 1) as t:
                    tile(t)
                tile(TILES - 1)
                sp.wait_ge(S_ready, GLA_HEADS * TILES)
                sp.dma_start(ps_dram.rearrange("h d e -> d h e"), S[:, :, :]).then_inc(out_copied, 16)
                sp.wait_ge(out_copied, 16 * 7)
                sp.wait_ge(T.h_stored, 16 * TILES)

            @block.gpsimd
            def _(pool):
                pool.memset(ident[:, :], 0.0).then_inc(pstep, 1)
                pool.wait_ge(pstep, 1)
                pool.affine_select(out=ident[:, :], in_=ident[:, :], compare_op=ALU.not_equal, fill=1.0,
                                   base=0, pattern=[[-1, P]], channel_multiplier=1).then_inc(zeroed, 1)
                pool.memset(S[:, :, :], 0.0).then_inc(zeroed, 1)
                pool.memset(kk[:, :, 0, :], 0.0).then_inc(zeroed, 1)
                pool.memset(vv[:, 0, :], 0.0).then_inc(zeroed, 1)
                pool.wait_ge(consts, 16 * 7)
                gate_norm(pool, T, 0, P)
                with pool.Fori(1, TILES) as t:
                    gate_norm(pool, T, t, P)

            @block.scalar
            def _(act):
                chain = Chain(act, astep)
                act.wait_ge(zeroed, 4)

                def gla_exp(t, h):
                    i = GLA_HEADS * t + h
                    act.wait_ge(rel_ready, i + 1)
                    wait(act, T.o_done, i - 1)
                    chain.step(act.activation(rel[:, h % 2, :, :], rel[:, h % 2, :, :], ACT.Exp, scale=-1.0))
                    chain.step(act.activation(qt[:, h % 2, :], qt[:, h % 2, :], ACT.Exp))
                    chain.step(act.activation(eb[:, h % 2, :], b[:, h, :], ACT.Exp))
                    act.activation(kp[:, h % 2, :], b[:, h, :], ACT.Exp, bias=b[:, h, P - 1:P], scale=-1.0).then_inc(ex_done, 1)

                def tile(t):
                    gla_exp(t, 0)
                    gla_exp(t, 1)
                    act.wait_ge(neg_ready, t + 1)
                    for h in range(SWA_HEADS):
                        chain.step(act.activation(s[:, h, :], s[:, h, :], ACT.Exp, bias=m[:, 1, h:h + 1],
                                                  accum_out=e_sum[:, h:h + 1]))
                    act.activation(m[:, 2, :], m[:, 2, :], ACT.Exp).then_inc(e_done, 1)
                    for h in range(GLA_HEADS):
                        act.wait_ge(sc_done, GLA_HEADS * t + h + 1)
                        wait(act, su_done, GLA_HEADS * t + h - 1)
                        act.activation(kpT[:, h % 2, :], X[:, BANK + h * P:BANK + (h + 1) * P],
                                       ACT.Copy).then_inc(kpT_ready, 1)
                        if h < 2:
                            gla_exp(t, h + 2)
                    tail_norm_act(act, T, t, P)
                    for i in range(SWA_HEADS // 2):
                        act.wait_ge(pT_ps, 8 * t + i + 1)
                        act.activation(pT[:, i % 2, :, :], X[:, (i % 2) * BANK:(i % 2 + 1) * BANK].rearrange("p (a n) -> p a n", a=4),
                                       ACT.Copy).then_inc(pT_ready, 1)
                    tail_act(act, T, t, P)
                    chain.restart()

                tile(0)
                with act.Fori(1, TILES) as t:
                    tile(t)

            @block.vector
            def _(dve):
                chain = Chain(dve, vstep)
                dve.wait_ge(consts, 16 * 7)
                dve.wait_ge(zeroed, 4)

                def exponents(t, h):
                    i = GLA_HEADS * t + h
                    if h == 0:
                        dve.wait_ge(gla_in, 64 * (t + 1))
                    wait(dve, sc_done, i - 1)
                    for j in range(SUBS):
                        ref = b[:, h, j * SUB + SUB // 2:j * SUB + SUB // 2 + 1]
                        chain.step(dve.tensor_scalar(rel[:, h % 2, j, :], b[:, h, :], ref, -CLAMP, ALU.subtract, ALU.max))
                    blocks = b[:, h, :].rearrange("p (j i) -> p j i", j=SUBS)
                    view = qt[:, h % 2, :].rearrange("p (j i) -> p j i", j=SUBS)
                    chain.link(dve.tensor_tensor(view, blocks, blocks[:, :, SUB // 2:SUB // 2 + 1].to_broadcast([P, SUBS, SUB]),
                                                 ALU.subtract))
                    dve.tensor_scalar(qt[:, h % 2, :], qt[:, h % 2, :], CLAMP, None, ALU.min).then_inc(rel_ready, 1)

                def rescale(t, h):
                    i = GLA_HEADS * t + h
                    dve.wait_ge(ex_done, i + 1)
                    chain.step(dve.tensor_tensor(rel[:, h % 2, :, :], rel[:, h % 2, :, :],
                                                 k[:, h, :].unsqueeze(1).to_broadcast([P, SUBS, P]), ALU.mult))
                    wait(dve, T.o_done, i - 1)
                    chain.step(dve.scalar_tensor_tensor(out=qt[:, h % 2, :], in0=q[:, h, :], scalar=QSCALE,
                                                        in1=qt[:, h % 2, :], op0=ALU.mult, op1=ALU.mult))
                    chain.step(dve.scalar_tensor_tensor(out=qb[:, h % 2, :], in0=q[:, h, :], scalar=QSCALE,
                                                        in1=eb[:, h % 2, :], op0=ALU.mult, op1=ALU.mult))
                    dve.tensor_tensor(kp[:, h % 2, :], k[:, h, :], kp[:, h % 2, :], ALU.mult).then_inc(kq_ready, 1)

                def masked(t, h):
                    i = GLA_HEADS * t + h
                    dve.wait_ge(sc_done, i + 1)
                    dve.tensor_tensor(scm[:, h % 2, :], X[:, h * P:(h + 1) * P], causal[:, :], ALU.mult).then_inc(scm_ready, 1)

                def advance(t, h):
                    i = GLA_HEADS * t + h
                    dve.wait_ge(su_done, i + 1)
                    dve.scalar_tensor_tensor(out=S[:, h, :], in0=S[:, h, :], scalar=eb[:, h % 2, P - 1:P],
                                             in1=update(h), op0=ALU.mult, op1=ALU.add).then_inc(S_ready, 1)

                def tile(t):
                    first = isinstance(t, int) and t == 0
                    exponents(t, 0)
                    exponents(t, 1)
                    for i in range(SWA_HEADS // 2):
                        wait_alone(dve, s_done, 8 * t + i + 1, vtick)
                        for j in range(2):
                            h = 2 * i + j
                            last = dve.tensor_tensor_reduce(s[:, h, :], score_pair(i, j),
                                                            mask[:, 0 if first else 1, :], HD ** -0.5, sinks[:, h:h + 1],
                                                            ALU.add, ALU.max, m[:, 0, h:h + 1])
                            if j == 0:
                                chain.step(last)
                        last.then_inc(s_taken, 1)
                        if i == 3:
                            rescale(t, 0)
                    dve.wait_ge(s_taken, 8 * (t + 1))
                    chain.step(dve.tensor_scalar(m[:, 1, :], m[:, 0, :], -1.0, None, ALU.mult))
                    dve.tensor_tensor(m[:, 2, :], sinks[:, :], m[:, 0, :], ALU.subtract).then_inc(neg_ready, 1)
                    rescale(t, 1)
                    for h in range(GLA_HEADS):
                        masked(t, h)
                        if h < 2:
                            advance(t, h)
                            exponents(t, h + 2)
                            rescale(t, h + 2)
                        else:
                            advance(t, h)
                    dve.wait_ge(e_done, t + 1)
                    chain.link(dve.tensor_tensor(m[:, 3, :], e_sum[:, :], m[:, 2, :], ALU.add))
                    chain.link(dve.reciprocal(m[:, 3, :], m[:, 3, :]))
                    dve.tensor_tensor(s[:, :, :], s[:, :, :], m[:, 3, :].unsqueeze(2).to_broadcast([P, SWA_HEADS, 2 * P]),
                                      ALU.mult).then_inc(p_ready, 1)
                    tail_oa_dve(dve, chain, T, t, P)
                    tail_merge_dve(dve, chain, T, t, P)
                    chain.restart()

                tile(0)
                with dve.Fori(1, TILES) as t:
                    tile(t)

            @block.tensor
            def _(pe):
                pe.wait_ge(zeroed, 4)

                def gla_scores(t, h):
                    i = GLA_HEADS * t + h
                    pe.wait_ge(kq_ready, i + 1)
                    for j in range(SUBS):
                        pe.matmul(X[:, h * P + j * SUB:h * P + (j + 1) * SUB], rel[:, h % 2, j, :],
                                  qt[:, h % 2, j * SUB:(j + 1) * SUB], start=True, stop=True)
                    pe.transpose(X[:, BANK + h * P:BANK + (h + 1) * P], kp[:, h % 2, :], ident[:, :]).then_inc(sc_done, 1)

                def gla_out(t, h):
                    i = GLA_HEADS * t + h
                    vh = v[:, h * DV:(h + 1) * DV]
                    pe.wait_ge(scm_ready, i + 1)
                    wait(pe, S_ready, i - GLA_HEADS + 1)
                    pe.matmul(O[:, h * DV:(h + 1) * DV], scm[:, h % 2, :], vh, start=True, stop=False)
                    pe.matmul(O[:, h * DV:(h + 1) * DV], qb[:, h % 2, :], S[:, h, :], start=False, stop=True
                              ).then_inc(T.o_done, 1)
                    pe.wait_ge(kpT_ready, i + 1)
                    pe.wait_ge(T.o_done, i + 1)
                    if h >= 2:
                        pe.wait_ge(S_ready, i - 1)
                    pe.matmul(update(h), kpT[:, h % 2, :], vh, start=True, stop=True).then_inc(su_done, 1)

                def tile(t):
                    pe.wait_ge(swa_in, 64 * (t + 1))
                    for i in range(SWA_HEADS // 2):
                        if i == 0:
                            wait(pe, T.mT_ready, 2 * t)
                        wait(pe, s_taken, 8 * t + i - 1)
                        for j in range(2):
                            half = j * HD
                            last = pe.matmul(score_pair(i, j), sq[half:half + HD, i, :],
                                             kk[half:half + HD, 2 * i // GROUP, :, :].rearrange("d a n -> d (a n)"),
                                             start=True, stop=True)
                        last.then_inc(s_done, 1)
                    pe.wait_ge(gla_in, 64 * (t + 1))
                    pe.wait_ge(s_taken, 8 * (t + 1))
                    wait(pe, T.h_ready, t)
                    for h in range(GLA_HEADS):
                        gla_scores(t, h)
                        gla_out(t, h)
                    pe.wait_ge(p_ready, t + 1)
                    pe.wait_ge(S_ready, GLA_HEADS * (t + 1))
                    for i in range(SWA_HEADS // 2 + 1):
                        if i < SWA_HEADS // 2:
                            wait(pe, pT_ready, 8 * t + i - 1)
                            for j in range(4):
                                last = pe.transpose(X[:, (i % 2) * BANK + j * P:(i % 2) * BANK + (j + 1) * P],
                                                    s[:, 2 * i + j // 2, (j % 2) * P:(j % 2 + 1) * P], ident[:, :])
                            last.then_inc(pT_ps, 1)
                        if i:
                            i -= 1
                            pe.wait_ge(pT_ready, 8 * t + i + 1)
                            g = 2 * i // GROUP
                            for j in range(2):
                                for a in range(2):
                                    last = pe.matmul(U[j * HD:(j + 1) * HD, i * P:(i + 1) * P], vv[:, a, g * HD:(g + 1) * HD],
                                                     pT[:, i % 2, 2 * j + a, :], start=(a == 0), stop=(a == 1))
                    last.then_inc(T.ob_done, 1)
                    pe.wait_ge(consts, 16 * 7)
                    tail_pe(pe, T, t, P)

                tile(0)
                with pe.Fori(1, TILES) as t:
                    tile(t)


        with ExitStack() as ctx:
            def sb(name, shape, dt=F32):
                return ctx.enter_context(nc.sbuf_tensor(name, shape, dt))

            N = NSAMP
            KEYS = WINDOW + STEPS
            T = Tail(sb, sem, "n_")
            q = sb("n_q", [P, GLA_HEADS, N])
            k = sb("n_k", [P, GLA_HEADS, N])
            b = sb("n_b", [P, GLA_HEADS, N])
            v = sb("n_v", [P, D])
            sq = sb("n_sq", [HD, SWA_HEADS, N])
            sq_seq = sb("n_sq_seq", [HD, SEQS, SWA_HEADS, STEPS])
            kk = sb("n_kk", [HD, SEQS, KV_HEADS, KEYS])
            vv = sb("n_vv", [P, SEQS, KV])
            v_new = sb("n_vnew", [STEPS, SEQS, KV])
            mask = sb("n_mask", [P, KEYS])
            causal = sb("n_causal", [N, N])
            seg_cols = sb("n_seg_cols", [P, SEQS, N])
            seg_rows = sb("n_seg_rows", [N, SEQS])
            sink = sb("n_sink", [P, 1])
            st = sb("n_st", [P, SEQS, DV])
            kt = sb("n_kt", [P, N])
            qt = sb("n_qt", [P, N])
            kp = sb("n_kp", [P, N])
            last_e = sb("n_last_e", [P, SEQS])
            qm = sb("n_qm", [P, SEQS, N])
            kpm = sb("n_kpm", [N, SEQS, P])
            scm = sb("n_scm", [N, N])
            s = sb("n_s", [P, SEQS, KEYS])
            m = sb("n_m", [P, 4, SEQS])
            e_sum = sb("n_e_sum", [P, SEQS])
            pT = sb("n_pT", [P, SEQS, P])
            pT_new = sb("n_pT_new", [STEPS, SEQS, P])

            ins = sem("n_ins")
            sq_ready = sem("n_sq_ready")
            st_in = sem("n_st_in")
            st_out = sem("n_st_out")
            ex_in = sem("n_ex_in")
            ex_done = sem("n_ex_done")
            kq_ready = sem("n_kq_ready")
            sc_done = sem("n_sc_done")
            m_ready = sem("n_scm_ready")
            su_done = sem("n_su_done")
            su_used = sem("n_su_used")
            st_ready = sem("n_st_ready")
            s_done = sem("n_s_done")
            neg_ready = sem("n_neg_ready")
            e_done = sem("n_e_done")
            p_ready = sem("n_p_ready")
            pT_ps = sem("n_pT_ps")
            pT_ready = sem("n_pT_ready")
            pad_done = sem("n_pad_done")
            vstep = sem("n_vstep")
            astep = sem("n_astep")
            pstep = sem("n_pstep")
            block = ctx.enter_context(nc.Block())
            PER_BANK = BANK // KEYS

            def score_place(seq):
                bank, at = seq // PER_BANK, (seq % PER_BANK) * KEYS
                tensor, base = ((X, 0), (X, BANK), (U, 0))[bank]
                return tensor, base + at

            @block.sync
            def _(sp):
                cols = slice(SEQ, TOK)
                for dst, src in ((b, z_b[:, :, cols]), (k, z_feat[4:8, :, cols]), (q, z_feat[0:4, :, cols])):
                    sp.dma_start(dst[:, :, :], src.rearrange("h p n -> p h n")).then_inc(ins, 16)
                sp.dma_start(v[0:N, :], z_tok[cols, 0:D]).then_inc(ins, 16)
                for half in range(2):
                    sp.dma_start(sq[:, half:SWA_HEADS:2, :],
                                 z_feat[8:16, half * HD:(half + 1) * HD, cols].rearrange("c d n -> d c n")).then_inc(ins, 16)
                for g in range(KV_HEADS):
                    sp.dma_start(kk[:, :, g, 0:WINDOW], cache_kT_dram[:, :, g, :]).then_inc(ins, 16)
                    sp.dma_start(kk[:, :, g, WINDOW:KEYS],
                                 z_kT[g * HD:(g + 1) * HD, cols].rearrange("d (b s) -> d b s", s=STEPS)).then_inc(ins, 16)
                sp.dma_start(vv[:, :, :], cache_v_dram).then_inc(ins, 16)
                sp.dma_start(v_new[:, :, :], z_kv[cols, KV:2 * KV].rearrange("(b s) c -> s b c", s=STEPS)).then_inc(ins, 16)
                for dst, src in ((mask[:, :], samp_mask_dram), (causal[:, :], samp_causal_dram),
                                 (seg_cols[:, :, :], seg_cols_dram), (seg_rows[:, :], seg_rows_dram),
                                 (sink[:, :], sink_rows_dram)):
                    sp.dma_start(dst, src).then_inc(ins, 16)
                for i, dst in ((1, T.v_gate), (2, T.ga), (3, T.gb)):
                    sp.dma_start(dst[0:N, :], z_tok[cols, i * D:(i + 1) * D]).then_inc(T.gates_in, 16)
                sp.dma_start(T.x[0:N, :], x_dram[cols, :]).then_inc(T.gates_in, 16)
                for h in range(GLA_HEADS):
                    wait(sp, st_out, 16 * h)
                    sp.dma_start(st[:, :, :], state_dram[:, h, :, :].rearrange("b d e -> d b e")).then_inc(st_in, 16)
                    sp.wait_ge(st_ready, SEQS * (h + 1))
                    sp.dma_start(ss_dram[:, h, :, :].rearrange("b d e -> d b e"), st[:, :, :]).then_inc(st_out, 16)
                sp.wait_ge(pad_done, 1)
                sp.dma_start(h_dram[TOK:(TILES + 1) * P, :], pT[0:P - N, :, :].rearrange("p a b -> p (a b)")).then_inc(T.h_stored, 16)
                sp.wait_ge(T.h_ready, 1)
                sp.dma_start(h_dram[cols, :], T.h[0:N, :]).then_inc(T.h_stored, 16)
                sp.wait_ge(T.h_stored, 32)
                sp.wait_ge(st_out, 16 * GLA_HEADS)

            @block.gpsimd
            def _(pool):
                pool.wait_ge(ins, 16 * 17)
                pool.tensor_copy(sq_seq[:, :, :, :], sq[:, :, :].rearrange("d h (b s) -> d b h s", s=STEPS)).then_inc(sq_ready, 1)
                gate_norm(pool, T, 0, N)
                pool.wait_ge(T.ob_done, 1)
                pool.memset(pT[:, :, :], 0.0).then_inc(pad_done, 1)

            @block.scalar
            def _(act):
                chain = Chain(act, astep)
                for h in range(GLA_HEADS):
                    act.wait_ge(ex_in, h + 1)
                    wait(act, T.o_done, h)
                    chain.step(act.activation(kt[:, :], kt[:, :], ACT.Exp, scale=-1.0))
                    chain.step(act.activation(qt[:, :], b[:, h, :], ACT.Exp))
                    chain.step(act.activation(kp[:, :], kp[:, :], ACT.Exp))
                    act.activation(last_e[:, :], b[:, h, STEPS - 1:N:STEPS], ACT.Exp).then_inc(ex_done, 1)
                act.wait_ge(neg_ready, 1)
                for seq in range(SEQS):
                    chain.step(act.activation(s[:, seq, :], s[:, seq, :], ACT.Exp, bias=m[:, 1, seq:seq + 1],
                                              accum_out=e_sum[:, seq:seq + 1]))
                act.activation(m[:, 2, :], m[:, 2, :], ACT.Exp).then_inc(e_done, 1)
                tail_norm_act(act, T, 0, N)
                for seq in range(SEQS):
                    r = seq % 2
                    act.wait_ge(pT_ps, seq + 1)
                    chain.step(act.activation(pT[:, seq, :], R[:, r, 0:P], ACT.Copy))
                    act.activation(pT_new[:, seq, :], R[0:STEPS, r, P:2 * P], ACT.Copy).then_inc(pT_ready, 1)
                tail_act(act, T, 0, N)

            @block.vector
            def _(dve):
                chain = Chain(dve, vstep)
                dve.wait_ge(ins, 16 * 17)
                for h in range(GLA_HEADS):
                    blocks = b[:, h, :].rearrange("p (s i) -> p s i", s=SEQS)
                    wait(dve, sc_done, h)
                    chain.step(dve.tensor_scalar(kt[:, :], b[:, h, :], -CLAMP, None, ALU.max))
                    dve.tensor_tensor(kp[:, :].rearrange("p (s i) -> p s i", s=SEQS),
                                      blocks[:, :, STEPS - 1:STEPS].to_broadcast([P, SEQS, STEPS]), blocks,
                                      ALU.subtract).then_inc(ex_in, 1)
                    dve.wait_ge(ex_done, h + 1)
                    chain.step(dve.tensor_tensor(kt[:, :], kt[:, :], k[:, h, :], ALU.mult))
                    chain.step(dve.tensor_tensor(kp[:, :], kp[:, :], k[:, h, :], ALU.mult))
                    chain.link(dve.scalar_tensor_tensor(out=qt[:, :], in0=q[:, h, :], scalar=QSCALE, in1=qt[:, :],
                                                        op0=ALU.mult, op1=ALU.mult))
                    dve.tensor_tensor(qm[:, :, :], qt[:, :].unsqueeze(1).to_broadcast([P, SEQS, N]), seg_cols[:, :, :],
                                      ALU.mult).then_inc(kq_ready, 1)
                    dve.wait_ge(sc_done, h + 1)
                    wait(dve, su_done, SEQS * h)
                    chain.step(dve.tensor_tensor(scm[:, :], R[0:N, 0, 0:N], causal[:, :], ALU.mult))
                    dve.tensor_tensor(kpm[:, :, :], R[0:N, 1, 0:P].unsqueeze(1).to_broadcast([N, SEQS, P]),
                                      seg_rows[:, :].unsqueeze(2).to_broadcast([N, SEQS, P]), ALU.mult).then_inc(m_ready, 1)
                    dve.wait_ge(T.o_done, h + 1)
                    for seq in range(SEQS):
                        dve.wait_ge(su_done, SEQS * h + seq + 1)
                        at = (seq % 2) * BANK
                        dve.scalar_tensor_tensor(out=st[:, seq, :], in0=st[:, seq, :], scalar=last_e[:, seq:seq + 1],
                                                 in1=U[:, at:at + DV], op0=ALU.mult, op1=ALU.add).then_inc(st_ready, 1)
                dve.wait_ge(s_done, 1)
                for seq in range(SEQS):
                    tensor, at = score_place(seq)
                    chain.step(dve.tensor_tensor_reduce(s[:, seq, :], tensor[:, at:at + KEYS], mask[:, :], HD ** -0.5, sink[:, :],
                                                        ALU.add, ALU.max, m[:, 0, seq:seq + 1]))
                chain.settle()
                chain.step(dve.tensor_scalar(m[:, 1, :], m[:, 0, :], -1.0, None, ALU.mult))
                dve.tensor_tensor(m[:, 2, :], sink[:, :].to_broadcast([P, SEQS]), m[:, 0, :], ALU.subtract).then_inc(neg_ready, 1)
                dve.wait_ge(e_done, 1)
                chain.link(dve.tensor_tensor(m[:, 3, :], e_sum[:, :], m[:, 2, :], ALU.add))
                chain.link(dve.reciprocal(m[:, 3, :], m[:, 3, :]))
                dve.tensor_tensor(s[:, :, :], s[:, :, :], m[:, 3, :].unsqueeze(2).to_broadcast([P, SEQS, KEYS]),
                                  ALU.mult).then_inc(p_ready, 1)
                tail_oa_dve(dve, chain, T, 0, N)
                tail_merge_dve(dve, chain, T, 0, N)

            @block.tensor
            def _(pe):
                for h in range(GLA_HEADS):
                    vh = v[0:N, h * DV:(h + 1) * DV]
                    pe.wait_ge(kq_ready, h + 1)
                    wait(pe, m_ready, h)
                    pe.matmul(R[0:N, 0, 0:N], kt[:, :], qt[:, :], start=True, stop=True)
                    pe.transpose(R[0:N, 1, 0:P], kp[:, :], ident[:, :]).then_inc(sc_done, 1)
                    pe.wait_ge(m_ready, h + 1)
                    pe.wait_ge(st_in, 16 * (h + 1))
                    pe.matmul(O[0:N, h * DV:(h + 1) * DV], scm[:, :], vh, start=True, stop=False)
                    for seq in range(SEQS):
                        last = pe.matmul(O[0:N, h * DV:(h + 1) * DV], qm[:, seq, :], st[:, seq, :],
                                         start=False, stop=(seq == SEQS - 1))
                    last.then_inc(T.o_done, 1)
                    for seq in range(SEQS):
                        at = (seq % 2) * BANK
                        wait(pe, st_ready, SEQS * h + seq - 1)
                        pe.matmul(U[:, at:at + DV], kpm[:, seq, :], vh, start=True, stop=True).then_inc(su_done, 1)
                pe.wait_ge(st_ready, SEQS * GLA_HEADS)
                pe.wait_ge(sq_ready, 1)
                for seq in range(SEQS):
                    tensor, at = score_place(seq)
                    for g in range(KV_HEADS):
                        last = pe.matmul(tensor[g * HD:(g + 1) * HD, at:at + KEYS],
                                         sq_seq[:, seq, g * GROUP:(g + 1) * GROUP, :].rearrange("d h s -> d (h s)"),
                                         kk[:, seq, g, :], start=True, stop=True)
                last.then_inc(s_done, 1)
                pe.wait_ge(p_ready, 1)
                for seq in range(SEQS):
                    r = seq % 2
                    wait(pe, pT_ready, seq - 1)
                    pe.transpose(R[:, r, 0:P], s[:, seq, 0:WINDOW], ident[:, :])
                    pe.transpose(R[0:STEPS, r, P:2 * P], s[:, seq, WINDOW:KEYS], ident[:, :]).then_inc(pT_ps, 1)
                    pe.wait_ge(pT_ready, seq + 1)
                    for g in range(KV_HEADS):
                        for j in range(2):
                            rows = lambda t: t[:, seq, g * HD:(g + 1) * HD].rearrange("k (h s) -> k h s", s=STEPS)[:, j:GROUP:2, :]
                            out = U[j * HD:(j + 1) * HD, 0:KT * N].rearrange("d (c n) -> d c n", c=KT)[
                                :, g * (GROUP // 2):(g + 1) * (GROUP // 2), seq * STEPS:(seq + 1) * STEPS]
                            pe.matmul(out, vv[:, seq, g * HD:(g + 1) * HD], rows(pT), start=True, stop=False)
                            last = pe.matmul(out, v_new[:, seq, g * HD:(g + 1) * HD], rows(pT_new), start=False, stop=True)
                last.then_inc(T.ob_done, 1)
                tail_pe(pe, T, 0, N)


def peer_stage(nc, sem, h_dram, wq_dram, keys_dram, u_dram, v_dram, g_ffn_dram, g_final_dram, y_dram):
    RING = 8
    IDX = 4
    with ExitStack() as ctx:
        def sb(name, shape, dt=F32):
            return ctx.enter_context(nc.sbuf_tensor(name, shape, dt))

        def pb(name, shape):
            return ctx.enter_context(nc.psum_tensor(name, shape, F32))

        wq = sb("e_wq", [P, KT, QD])
        keys = sb("e_keys", [P, 2 * HEADS, NKEYS])
        g_ffn = sb("e_g_ffn", [P, D])
        g_final = sb("e_g_final", [P, D])
        ident = sb("e_ident", [P, P])
        iota16 = sb("e_iota16", [P, TOPK])
        u_rows = sb("e_u_rows", [P, RING, D])
        v_rows = sb("e_v_rows", [P, RING, D])
        h_next = sb("e_h_next", [P, D])
        xn_next = sb("e_xn_next", [P, D])
        xn = sb("e_xn", [P, D])
        xnT = sb("e_xnT", [P, KT, P])
        h_out = sb("e_h_out", [P, D])
        acc = sb("e_acc", [P, D])
        y = sb("e_y", [P, D])
        q_sb = sb("e_q_sb", [P, 2, P])
        s_sb = sb("e_s_sb", [P, 2, NKEYS])
        s_rest = sb("e_s_rest", [P, 2, NKEYS])
        top_val = sb("e_top_val", [P, 2, TOPK])
        top_idx = sb("e_top_idx", [P, 2, TOPK], U32)
        top_idxf = sb("e_top_idxf", [P, 2, TOPK])
        cand = sb("e_cand", [P, TOPK, TOPK])
        cand_rest = sb("e_cand_rest", [P, TOPK, TOPK])
        best = sb("e_best", [P, IDX, TOPK])
        pos = sb("e_pos", [P, TOPK], U32)
        pos_ab = sb("e_pos_ab", [P, 2, TOPK], U32)
        pos_abf = sb("e_pos_abf", [P, 2, TOPK])
        hot = sb("e_hot", [P, 2, TOPK, TOPK])
        picked = sb("e_picked", [P, 2, TOPK])
        expert = sb("e_expert", [P, IDX, TOPK], U32)
        neg_best = sb("e_neg_best", [P, IDX])
        e_top = sb("e_e_top", [P, IDX, TOPK])
        e_sum = sb("e_e_sum", [P, IDX])
        e_rec = sb("e_e_rec", [P, IDX])
        dots = sb("e_dots", [P, 2, TOPK])
        gelus = sb("e_gelus", [P, 2, TOPK])
        weight = sb("e_weight", [P, 2, TOPK])
        diag = sb("e_diag", [P, TOPK, P])
        stat = sb("e_stat", [P, 8])
        q_ps = pb("e_q_ps", [P, 2, P])
        s_ps = pb("e_s_ps", [P, 2, NKEYS])
        t_ps = [pb(f"e_t_ps{i}", [P, 4, P]) for i in range(2)]
        o_ps = pb("e_o_ps", [P, D])

        consts = sem("e_consts")
        made = sem("e_made")
        h_loaded = sem("e_h_loaded")
        h_again = sem("e_h_again")
        sq_done = sem("e_sq_done")
        rt_in = sem("e_rt_in")
        rt_done = sem("e_rt_done")
        xn_ready = sem("e_xn_ready")
        xnT_ps = sem("e_xnT_ps")
        xnT_ready = sem("e_xnT_ready")
        q_done = sem("e_q_done")
        q_ready = sem("e_q_ready")
        s_done = sem("e_s_done")
        s_taken = sem("e_s_taken")
        picked_ready = sem("e_picked_ready")
        e_done = sem("e_e_done")
        u_got = [sem(f"e_u_got{i}") for i in range(RING)]
        v_got = [sem(f"e_v_got{i}") for i in range(RING)]
        u_used = sem("e_u_used")
        v_used = sem("e_v_used")
        gelu_done = sem("e_gelu_done")
        w_ready = sem("e_w_ready")
        diag_ready = sem("e_diag_ready")
        acc_ready = sem("e_acc_ready")
        out_sq = sem("e_out_sq")
        out_rt = sem("e_out_rt")
        y_ready = sem("e_y_ready")
        y_stored = sem("e_y_stored")
        vstep = sem("e_vstep")
        astep = sem("e_astep")
        ptick = sem("e_ptick")
        pstep = sem("e_pstep")
        block = ctx.enter_context(nc.Block())
        LAST = TILES

        def rows(t):
            return NSAMP if isinstance(t, int) and t == LAST else P

        def before(t, h):
            return rows(t) if h else P

        @block.sync
        def _(sp):
            sp.dma_start(wq[:, :, :], wq_dram).then_inc(consts, 16)
            sp.dma_start(keys[:, :, :], keys_dram).then_inc(consts, 16)
            sp.dma_start(g_ffn[:, :], g_ffn_dram.to_broadcast([P, D])).then_inc(consts, 16)
            sp.dma_start(g_final[:, :], g_final_dram.to_broadcast([P, D])).then_inc(consts, 16)

            def load_next(t):
                wait(sp, xn_ready, t)
                wait(sp, sq_done, t)
                sp.dma_start(h_next[:, :], h_dram[bass.ds(t * P, P), :]).then_inc(h_loaded, 16)

            def load_again(t):
                wait(sp, out_sq, t)
                sp.dma_start(h_out[0:rows(t), :], h_dram[bass.ds(t * P, rows(t)), :]).then_inc(h_again, 16)

            def store(t):
                sp.wait_ge(y_ready, t + 1)
                sp.dma_start(y_dram[bass.ds(t * P, rows(t)), :], y[0:rows(t), :]).then_inc(y_stored, 16)

            load_next(0)

            def tile(t):
                if not (isinstance(t, int) and t == LAST):
                    load_next(t + 1)
                if not (isinstance(t, int) and t == 0):
                    store(t - 1)
                load_again(t)

            tile(0)
            with sp.Fori(1, LAST) as t:
                tile(t)
            tile(LAST)
            store(LAST)
            sp.wait_ge(y_stored, 16 * (LAST + 1))

        @block.gpsimd
        def _(pool):
            pool.memset(ident[:, :], 0.0).then_inc(pstep, 1)
            pool.wait_ge(pstep, 1)
            pool.affine_select(out=ident[:, :], in_=ident[:, :], compare_op=ALU.not_equal, fill=1.0,
                               base=0, pattern=[[-1, P]], channel_multiplier=1).then_inc(made, 1)
            pool.iota(iota16[:, :], [[1, TOPK]], base=0, channel_multiplier=0,
                      allow_small_or_imprecise_dtypes=True).then_inc(made, 1)

            def gather(table, ring, got, used, unit, h, k, n):
                wait_alone(pool, used, unit * TOPK + k - RING + 1, ptick)
                b = h % IDX
                pool.indirect_dma_start(ring[0:n, k % RING, :], None, table,
                                        bass.IndirectOffsetOnAxis(ap=expert[0:n, b, k:k + 1], axis=0)
                                        ).then_inc(got[k % RING], 16)

            def v_gather(t, h, k):
                gather(v_dram, v_rows, v_got, v_used, t * HEADS + h - 1, h - 1, k, before(t, h))

            def tile(t):
                for h in range(HEADS):
                    unit = t * HEADS + h
                    wait_alone(pool, picked_ready, unit + 1, ptick)
                    for k in range(TOPK):
                        gather(u_dram, u_rows, u_got, u_used, unit, h, k, rows(t))
                        if not (isinstance(t, int) and t == 0 and h == 0):
                            v_gather(t, h, k)

            tile(0)
            with pool.Fori(1, LAST) as t:
                tile(t)
            tile(LAST)
            for k in range(TOPK):
                gather(v_dram, v_rows, v_got, v_used, LAST * HEADS + HEADS - 1, HEADS - 1, k, NSAMP)

        @block.scalar
        def _(act):
            chain = Chain(act, astep)

            def norm(t):
                act.wait_ge(h_loaded, 16 * (t + 1))
                wait(act, xnT_ps, 2 * t)
                wait(act, xn_ready, t)
                act.activation(xn_next[:, :], h_next[:, :], ACT.Square, accum_out=stat[:, 0:1]).then_inc(sq_done, 1)
                act.wait_ge(rt_in, t + 1)
                act.activation(stat[:, 2:3], stat[:, 1:2], ACT.Sqrt).then_inc(rt_done, 1)
                for i in range(2):
                    act.wait_ge(xnT_ps, 2 * t + i + 1)
                    act.activation(xnT[:, 4 * i:4 * i + 4, :], t_ps[i][:, :, :], ACT.Copy).then_inc(xnT_ready, 1)

            def queries(unit):
                act.wait_ge(q_done, unit + 1)
                wait(act, s_done, unit)
                act.activation(q_sb[:, :, :], q_ps[:, :, :], ACT.Copy).then_inc(q_ready, 1)

            def exponentials(unit, h):
                b = h % IDX
                act.wait_ge(picked_ready, unit + 1)
                act.activation(e_top[:, b, :], best[:, b, :], ACT.Exp, bias=neg_best[:, b:b + 1],
                               accum_out=e_sum[:, b:b + 1]).then_inc(e_done, 1)

            def gelu(unit, h, n):
                act.wait_ge(u_used, (unit + 1) * TOPK)
                wait(act, w_ready, unit - 1)
                act.activation(gelus[0:n, h % 2, :], dots[0:n, h % 2, :], ACT.Gelu).then_inc(gelu_done, 1)

            def diagonals(unit, h, n):
                act.wait_ge(w_ready, unit + 1)
                for k in range(TOPK):
                    wait(act, v_used, (unit - 1) * TOPK + k + 1)
                    act.activation(diag[0:n, k, 0:n], ident[0:n, 0:n], ACT.Copy,
                                   scale=weight[0:n, h % 2, k:k + 1]).then_inc(diag_ready, 1)

            def evacuate(t):
                act.wait_ge(v_used, (t + 1) * HEADS * TOPK)
                wait(act, out_sq, t)
                act.activation(acc[0:rows(t), :], o_ps[0:rows(t), :], ACT.Copy).then_inc(acc_ready, 1)

            def out_root(t):
                act.wait_ge(out_sq, t + 1)
                act.activation(stat[0:rows(t), 6:7], stat[0:rows(t), 5:6], ACT.Sqrt).then_inc(out_rt, 1)

            act.wait_ge(made, 2)
            norm(0)
            queries(0)
            queries(1)
            exponentials(0, 0)
            exponentials(1, 1)

            def tile(t):
                first = isinstance(t, int) and t == 0
                last = isinstance(t, int) and t == LAST
                for h in range(HEADS):
                    unit = t * HEADS + h
                    if h == HEADS - 2 and not last:
                        norm(t + 1)
                    if h < HEADS - 2 or not last:
                        queries(unit + 2)
                    if not (first and h == 0):
                        diagonals(unit - 1, (h - 1) % HEADS, before(t, h))
                    gelu(unit, h, rows(t))
                    if h < HEADS - 2 or not last:
                        exponentials(unit + 2, (h + 2) % HEADS)
                    if h == 0 and not first:
                        evacuate(t - 1)
                    if h == 1 and not first:
                        out_root(t - 1)

            tile(0)
            with act.Fori(1, LAST) as t:
                tile(t)
            tile(LAST)
            diagonals(LAST * HEADS + HEADS - 1, HEADS - 1, NSAMP)
            evacuate(LAST)
            out_root(LAST)

        @block.vector
        def _(dve):
            chain = Chain(dve, vstep)

            def norm(t):
                dve.wait_ge(sq_done, t + 1)
                dve.tensor_scalar(stat[:, 1:2], stat[:, 0:1], 1.0 / D, EPS, ALU.mult, ALU.add).then_inc(rt_in, 1)
                dve.wait_ge(rt_done, t + 1)
                chain.link(dve.reciprocal(stat[:, 3:4], stat[:, 2:3]))
                dve.scalar_tensor_tensor(out=xn_next[:, :], in0=h_next[:, :], scalar=stat[:, 3:4],
                                         in1=g_ffn[:, :], op0=ALU.mult, op1=ALU.mult).then_inc(xn_ready, 1)

            def take(t):
                dve.wait_ge(xn_ready, t + 1)
                wait(dve, u_used, t * HEADS * TOPK)
                chain.link(dve.tensor_copy(xn[:, :], xn_next[:, :]))

            def top16(values, indices, source, rest):
                chain.link(dve.max(values[:, 0:8], source))
                chain.step(dve.max_index(indices[:, 0:8], values[:, 0:8], source))
                chain.link(dve.match_replace(rest, values[:, 0:8], source, LOWEST))
                chain.link(dve.max(values[:, 8:16], rest))
                chain.step(dve.max_index(indices[:, 8:16], values[:, 8:16], rest))

            def select(unit, h):
                b = h % IDX
                dve.wait_ge(s_done, unit + 1)
                dve.tensor_copy(s_sb[:, :, :], s_ps[:, :, :]).then_inc(s_taken, 1)
                dve.wait_ge(s_taken, unit + 1)
                wait(dve, v_used, (unit - IDX + 1) * TOPK)
                chain.step(dve.tensor_copy(stat[:, 7:8], stat[:, 3:4]))
                for half in range(2):
                    top16(top_val[:, half, :], top_idx[:, half, :], s_sb[:, half, :], s_rest[:, half, :])
                chain.settle()
                chain.step(dve.tensor_copy(top_idxf[:, :, :], top_idx[:, :, :]))
                chain.link(dve.tensor_tensor(cand[:, :, :],
                                             top_val[:, 0, :].unsqueeze(2).to_broadcast([P, TOPK, TOPK]),
                                             top_val[:, 1, :].unsqueeze(1).to_broadcast([P, TOPK, TOPK]), ALU.add))
                flat = cand[:, :, :].rearrange("p a b -> p (a b)")
                rest = cand_rest[:, :, :].rearrange("p a b -> p (a b)")
                top16(best[:, b, :], pos[:, :], flat, rest)
                chain.settle()
                chain.step(dve.tensor_scalar(pos_ab[:, 0, :], pos[:, :], 4, None, ALU.logical_shift_right))
                chain.step(dve.tensor_scalar(pos_ab[:, 1, :], pos[:, :], TOPK - 1, None, ALU.bitwise_and))
                chain.link(dve.tensor_scalar(neg_best[:, b:b + 1], best[:, b, 0:1], -1.0, None, ALU.mult))
                chain.link(dve.tensor_copy(pos_abf[:, :, :], pos_ab[:, :, :]))
                chain.link(dve.tensor_tensor(
                    hot[:, :, :, :].rearrange("p s a b -> p (s a) b"),
                    pos_abf[:, :, :].rearrange("p s a -> p (s a)").unsqueeze(2).to_broadcast([P, 2 * TOPK, TOPK]),
                    iota16[:, :].unsqueeze(1).to_broadcast([P, 2 * TOPK, TOPK]), ALU.is_equal))
                chain.link(dve.tensor_tensor(hot[:, :, :, :], hot[:, :, :, :],
                                             top_idxf[:, :, :].unsqueeze(2).to_broadcast([P, 2, TOPK, TOPK]), ALU.mult))
                chain.link(dve.tensor_reduce(picked[:, :, :], hot[:, :, :, :], AX_X, ALU.add))
                dve.scalar_tensor_tensor(out=expert[:, b, :], in0=picked[:, 0, :], scalar=float(NKEYS),
                                         in1=picked[:, 1, :], op0=ALU.mult, op1=ALU.add).then_inc(picked_ready, 1)

            def u_dots(unit, h, n):
                wait(dve, gelu_done, unit - 1)
                for k in range(TOPK):
                    dve.wait_ge(u_got[k % RING], 16 * (unit * (TOPK // RING) + k // RING + 1))
                    dve.tensor_tensor_reduce(u_rows[0:n, k % RING, :], u_rows[0:n, k % RING, :], xn[0:n, :], 1.0, 0.0,
                                             ALU.mult, ALU.add, dots[0:n, h % 2, k:k + 1]).then_inc(u_used, 1)

            def weights(unit, h, n):
                b = h % IDX
                dve.wait_ge(e_done, unit + 1)
                chain.link(dve.reciprocal(e_rec[0:n, b:b + 1], e_sum[0:n, b:b + 1]))
                dve.wait_ge(gelu_done, unit + 1)
                wait(dve, diag_ready, (unit - 1) * TOPK)
                dve.scalar_tensor_tensor(out=weight[0:n, h % 2, :], in0=gelus[0:n, h % 2, :],
                                         scalar=e_rec[0:n, b:b + 1], in1=e_top[0:n, b, :],
                                         op0=ALU.mult, op1=ALU.mult).then_inc(w_ready, 1)

            def out_square(t):
                n = rows(t)
                dve.wait_ge(acc_ready, t + 1)
                dve.wait_ge(h_again, 16 * (t + 1))
                chain.link(dve.tensor_tensor(h_out[0:n, :], h_out[0:n, :], acc[0:n, :], ALU.add))
                wait(dve, y_stored, 16 * t)
                chain.link(dve.tensor_tensor_reduce(y[0:n, :], h_out[0:n, :], h_out[0:n, :], 1.0, 0.0,
                                                    ALU.mult, ALU.add, stat[0:n, 4:5]))
                chain.link(dve.tensor_copy(acc[0:n, :], h_out[0:n, :]))
                dve.tensor_scalar(stat[0:n, 5:6], stat[0:n, 4:5], 1.0 / D, EPS, ALU.mult, ALU.add).then_inc(out_sq, 1)

            def out_norm(t):
                n = rows(t)
                dve.wait_ge(out_rt, t + 1)
                chain.link(dve.reciprocal(stat[0:n, 6:7], stat[0:n, 6:7]))
                dve.scalar_tensor_tensor(out=y[0:n, :], in0=acc[0:n, :], scalar=stat[0:n, 6:7],
                                         in1=g_final[0:n, :], op0=ALU.mult, op1=ALU.mult).then_inc(y_ready, 1)

            dve.wait_ge(consts, 64)
            dve.wait_ge(made, 2)
            norm(0)
            take(0)
            select(0, 0)
            select(1, 1)
            chain.restart()

            def tile(t):
                first = isinstance(t, int) and t == 0
                last = isinstance(t, int) and t == LAST
                for h in range(HEADS):
                    unit = t * HEADS + h
                    if h == HEADS - 2 and not last:
                        norm(t + 1)
                    u_dots(unit, h, rows(t))
                    if h == HEADS - 1 and not last:
                        take(t + 1)
                    if h < HEADS - 2 or not last:
                        select(unit + 2, (h + 2) % HEADS)
                    weights(unit, h, rows(t))
                    if h == 1 and not first:
                        out_square(t - 1)
                    if h == 2 and not first:
                        out_norm(t - 1)
                chain.restart()

            tile(0)
            with dve.Fori(1, LAST) as t:
                tile(t)
            tile(LAST)
            out_square(LAST)
            out_norm(LAST)

        @block.tensor
        def _(pe):
            def transposes(t):
                pe.wait_ge(xn_ready, t + 1)
                for i in range(2):
                    wait(pe, xnT_ready, 2 * (t - 1) + i + 1)
                    for j in range(4):
                        k = 4 * i + j
                        last = pe.transpose(t_ps[i][:, j, :], xn_next[:, k * P:(k + 1) * P], ident[:, :])
                    last.then_inc(xnT_ps, 1)

            def queries(unit, h, t):
                pe.wait_ge(xnT_ready, 2 * (t + 1))
                wait(pe, q_ready, unit)
                for half in range(2):
                    j = 2 * h + half
                    for k in range(KT):
                        last = pe.matmul(q_ps[:, half, :], wq[:, k, j * P:(j + 1) * P], xnT[:, k, :],
                                         start=(k == 0), stop=(k == KT - 1))
                last.then_inc(q_done, 1)

            def scores(unit, h):
                pe.wait_ge(q_ready, unit + 1)
                wait(pe, s_taken, unit)
                for half in range(2):
                    last = pe.matmul(s_ps[:, half, :], q_sb[:, half, :], keys[:, 2 * h + half, :],
                                     start=True, stop=True)
                last.then_inc(s_done, 1)

            def v_sum(unit, h, n, ks):
                for k in ks:
                    pe.wait_ge(diag_ready, unit * TOPK + k + 1)
                    pe.wait_ge(v_got[k % RING], 16 * (unit * (TOPK // RING) + k // RING + 1))
                    for c in range(D // BANK):
                        last = pe.matmul(o_ps[0:n, c * BANK:(c + 1) * BANK], diag[0:n, k, 0:n],
                                         v_rows[0:n, k % RING, c * BANK:(c + 1) * BANK],
                                         start=(h == 0 and k == 0), stop=(h == HEADS - 1 and k == TOPK - 1))
                    last.then_inc(v_used, 1)

            pe.wait_ge(consts, 64)
            pe.wait_ge(made, 2)
            transposes(0)
            for h in range(2):
                queries(h, h, 0)
                scores(h, h)

            def tile(t):
                first = isinstance(t, int) and t == 0
                last = isinstance(t, int) and t == LAST
                for h in range(HEADS):
                    unit = t * HEADS + h
                    if h == HEADS - 2 and not last:
                        transposes(t + 1)
                    ahead = h < HEADS - 2 or not last
                    if ahead:
                        queries(unit + 2, (h + 2) % HEADS, t + (h + 2) // HEADS)
                    if not first or h:
                        if h == 1:
                            wait(pe, acc_ready, t)
                        v_sum(unit - 1, (h - 1) % HEADS, before(t, h), range(TOPK // 2))
                    if ahead:
                        scores(unit + 2, (h + 2) % HEADS)
                    if not first or h:
                        v_sum(unit - 1, (h - 1) % HEADS, before(t, h), range(TOPK // 2, TOPK))

            tile(0)
            with pe.Fori(1, LAST) as t:
                tile(t)
            tile(LAST)
            v_sum(LAST * HEADS + HEADS - 1, HEADS - 1, NSAMP, range(TOPK))


def build(nc, i, o):
    with ExitStack() as ctx:
        stages(nc, lambda name: ctx.enter_context(nc.semaphore(name)), i, o)


def stages(nc, sem, i, o):
    scratch = lambda name, shape: nc.dram_tensor(name, shape, F32, kind="Internal").ap()
    z_tok = scratch("z_tok", (TOK, 4 * D))
    z_feat = scratch("z_feat", (16, P, TOK))
    z_kv = scratch("z_kv", (TOK, 2 * KV))
    z_kT = scratch("z_kT", (KV, TOK))
    z_b = scratch("z_b", (GLA_HEADS, P, TOK))
    h = scratch("h_mid", ((TILES + 1) * P, D))
    project_stage(nc, sem, i("x"), i("g_mix"), i("w_big"), i("w_small"), i("w_decay"), i("b_decay"),
                  z_tok, z_feat, z_kv, z_kT, z_b)
    mix_stage(nc, sem, i("x"), i("wa"), i("wb"), i("wo"), i("gla_norm"), i("sinks"), i("sink_rows"), i("mask"),
              i("causal"), i("samp_mask"), i("samp_causal"), i("seg_cols"), i("seg_rows"), i("cache_kT"),
              i("cache_v"), i("cache_k_rows"), i("cache_v_rows"), i("state"), z_tok, z_feat, z_kv, z_kT, z_b, h,
              o["pk"], o["pv"], o["ps"], o["sk"], o["sv"], o["ss"])
    peer_stage(nc, sem, h, i("wq"), i("keys"), i("u"), i("v"), i("g_ffn"), i("g_final"), o["y"])


OUTPUTS = [("y", (TOK, D)), ("pk", (WINDOW, KV)), ("pv", (WINDOW, KV)), ("ps", (GLA_HEADS, DK, DV)),
           ("sk", (SEQS, WINDOW, KV)), ("sv", (SEQS, WINDOW, KV)), ("ss", (SEQS, GLA_HEADS, DK, DV))]


def kernel(**inputs):
    import numpy as np
    import concourse.bacc as bacc
    from concourse.bass_utils import run_bass_kernel_spmd as run

    a = {name: np.asarray(value) for name, value in inputs.items()}
    w_in = a["w_in"][0]

    def tiled(w):
        return w.reshape(-1, P, w.shape[1]).transpose(1, 0, 2)

    gq, gk, gv, gg, glr, sq, sk, ga, gb = 0, 512, 1024, 2048, 3072, 3088, 4112, 4368, 5392
    starts = [c + d for c in (gv, gg, ga, gb) for d in (0, CHUNK)] + [gq, gk, sq, sq + CHUNK]
    token, key = np.arange(P)[:, None], np.arange(P)[None, :]
    window = np.concatenate([np.where(key > token, 0.0, MASKED), np.where(key <= token, 0.0, MASKED)], 1)
    first = np.concatenate([np.full((P, P), MASKED), window[:, P:]], 1)
    step = np.arange(P)[:, None] % STEPS
    late = np.arange(WINDOW + STEPS)[None, :]
    samp = np.where((late > step) & (late <= WINDOW + step), 0.0, MASKED)
    row, col = np.arange(NSAMP)[:, None], np.arange(NSAMP)[None, :]
    same = row // STEPS == col // STEPS
    seg = np.arange(SEQS)[:, None] == col // STEPS
    f32 = np.float32
    arrays = {
        "x": np.concatenate([a["x_prompt"].reshape(SEQ, D), a["x_sample"].reshape(NSAMP, D)]),
        "g_mix": a["norm_mix"], "g_ffn": a["norm_ffn"], "g_final": a["norm_final"][None],
        "w_big": np.stack([tiled(w_in[:, c:c + CHUNK]).reshape(P, KT * CHUNK) for c in starts]),
        "w_small": tiled(np.concatenate([w_in[:, sk:sk + 2 * KV], w_in[:, glr:glr + RANK]], 1)),
        "w_decay": a["gla_w_decay"][0], "b_decay": a["gla_b_decay"].reshape(GLA_HEADS, DK).T,
        "wa": tiled(a["w_branch_a"][0]), "wb": tiled(a["w_branch_b"][0]), "wo": tiled(a["w_out"][0]),
        "gla_norm": a["gla_norm"], "sinks": a["swa_sinks"],
        "sink_rows": np.repeat(a["swa_sinks"][0], STEPS)[:, None],
        "mask": np.stack([first, window], 1).astype(f32), "causal": (token <= key).astype(f32),
        "samp_mask": samp.astype(f32), "samp_causal": (same & (row <= col)).astype(f32),
        "seg_cols": np.broadcast_to(seg, (P, SEQS, NSAMP)).astype(f32), "seg_rows": seg.T.astype(f32),
        "cache_kT": a["cache_win_k"][0].transpose(3, 0, 2, 1),
        "cache_v": a["cache_win_v"][0].transpose(1, 0, 2, 3).reshape(WINDOW, SEQS, KV),
        "cache_k_rows": a["cache_win_k"][0].reshape(SEQS, WINDOW, KV),
        "cache_v_rows": a["cache_win_v"][0].reshape(SEQS, WINDOW, KV),
        "state": a["state_gla"][0],
        "wq": tiled(a["peer_w_q"][0]),
        "keys": np.stack([a["peer_keys1"][0], a["peer_keys2"][0]], 1).reshape(2 * HEADS, NKEYS, HALF).transpose(2, 0, 1),
        "u": a["peer_u"][0], "v": a["peer_v"][0],
    }
    nc = bacc.Bacc("TRN2", target_bir_lowering=False, num_devices=1)
    given, feeds = {}, {}
    for name, value in arrays.items():
        feeds[f"in_{name}"] = np.ascontiguousarray(value)
        given[name] = nc.dram_tensor(f"in_{name}", value.shape, F32, kind="ExternalInput").ap()
    outs = {name: nc.dram_tensor(f"out_{name}", shape, F32, kind="ExternalOutput").ap() for name, shape in OUTPUTS}
    build(nc, given.__getitem__, outs)
    result = run(nc, [feeds], core_ids=[0]).results[0]
    r = {name: result[f"out_{name}"] for name, _ in OUTPUTS}
    win = (1, 1, WINDOW, KV_HEADS, HD)
    return (r["y"][:SEQ].reshape(1, SEQ, D), r["y"][SEQ:].reshape(SEQS, STEPS, D),
            r["pk"].reshape(win), r["pv"].reshape(win), r["ps"].reshape(1, 1, GLA_HEADS, DK, DV),
            r["sk"].reshape(1, SEQS, WINDOW, KV_HEADS, HD), r["sv"].reshape(1, SEQS, WINDOW, KV_HEADS, HD),
            r["ss"].reshape(1, SEQS, GLA_HEADS, DK, DV))
```

```python
from contextlib import ExitStack

import concourse.bass as bass
from concourse import mybir

F32 = mybir.dt.float32
F32R = mybir.dt.float32r
U32 = mybir.dt.uint32
ALU = mybir.AluOpType
ACT = mybir.ActivationFunctionType
AX_X = mybir.AxisListType.X

P = 128
D = 1024
KT = D // P
SEQ = 1024
SEQS = 8
STEPS = 8
NSAMP = SEQS * STEPS
TOK = SEQ + NSAMP
TILES = SEQ // P
BANK = 512

GLA_HEADS, DK, DV, RANK = 4, 128, 256, 16
SUB = 16
SUBS = P // SUB
CLAMP = 60.0
SWA_HEADS, KV_HEADS, HD, WINDOW = 16, 2, 64, 128
GROUP = SWA_HEADS // KV_HEADS
MASKED = -1e30

HEADS, NKEYS, HALF, TOPK = 8, 128, 128, 16
QD = HEADS * 2 * HALF
LOWEST = -3.0e38
EPS = 1e-6


def wait(eng, sem, value):
    if not isinstance(value, int) or value > 0:
        eng.wait_ge(sem, value)


def wait_alone(eng, sem, value, tick):
    if not isinstance(value, int) or value > 0:
        eng.wait_ge(sem, value)
        eng.sem_inc(tick, 1)


class Chain:

    def __init__(self, eng, sem):
        self.eng, self.sem, self.n = eng, sem, 0

    def step(self, ins):
        ins.then_inc(self.sem, 1)
        self.n += 1

    def link(self, ins):
        self.step(ins)
        self.eng.wait_ge(self.sem, self.n)

    def settle(self):
        self.eng.wait_ge(self.sem, self.n)

    def restart(self):
        if self.n:
            self.settle()
            self.eng.sem_clear(self.sem)
            self.n = 0


CHUNK = 512
GROUPS = [(0, BANK), (BANK, BANK), (2 * BANK, NSAMP)]
KV = KV_HEADS * HD
SMALL = RANK + 2 * KV
PAD = (TILES + 1) * P


def project_stage(nc, sem, x_dram, g_mix_dram, w_big_dram, w_small_dram, w_decay_dram, b_decay_dram,
                  z_tok, z_feat, z_kv, z_kT, z_b):
    SLOTS = 3
    TOK_CHUNKS, FEAT_CHUNKS = 8, 4
    NT = TILES + 1
    NF = CHUNK // P * len(GROUPS)
    with ExitStack() as ctx:
        def sb(name, shape, dt=F32):
            return ctx.enter_context(nc.sbuf_tensor(name, shape, dt))

        def pb(name, shape):
            return ctx.enter_context(nc.psum_tensor(name, shape, F32))

        xh = sb("j_xh", [P, KT, PAD], F32R)
        xl = sb("j_xl", [P, KT, PAD], F32R)
        w = sb("j_w", [P, KT * CHUNK])
        wh = sb("j_wh", [P, 2, KT * CHUNK], F32R)
        wl = sb("j_wl", [P, 2, KT * CHUNK], F32R)
        w_decay = sb("j_w_decay", [RANK, GLA_HEADS * DK])
        b_decay = sb("j_b_decay", [P, GLA_HEADS])
        room = sb("j_room", [P, 6 * D])
        x = room[:, 0:3 * D].rearrange("p (s n) -> p s n", s=3)
        xn = room[:, 3 * D:5 * D].rearrange("p (s n) -> p s n", s=2)
        g_mix = room[:, 5 * D:6 * D]
        z = room[:, 0:TOK]
        la = room[:, TOK:3 * TOK].rearrange("p (s n) -> p s n", s=2)
        low = room[0:RANK, 3 * TOK:4 * TOK]
        ident = sb("j_ident", [P, P])
        keep = sb("j_keep", [P, TOK])
        stat = sb("j_stat", [P, NT, 4])
        stage = sb("j_stage", [P, SLOTS, CHUNK])
        t_ps = [pb(f"j_t{i}", [P, 4, P]) for i in range(2)]
        m_ps = [pb(f"j_m{i}", [P, BANK]) for i in range(SLOTS)]
        z_ps = [pb(f"j_z{i}", [P, BANK]) for i in range(3)]

        consts = sem("j_consts")
        made = sem("j_made")
        x_in = [sem(f"j_x{i}") for i in range(3)]
        sq_done = sem("j_sq")
        rt_in = sem("j_rt_in")
        rt_done = sem("j_rt")
        xn_ready = sem("j_xn")
        xnT_ps = sem("j_xnT_ps")
        xh_ready = sem("j_xh_ready")
        xl_ready = sem("j_xl_ready")
        w_in = sem("j_w_in")
        wh_ready = sem("j_wh_ready")
        wl_ready = sem("j_wl_ready")
        chunk_used = sem("j_chunk_used")
        m_done = sem("j_m_done")
        staged = sem("j_staged")
        stored = [sem(f"j_stored{i}") for i in range(SLOTS)]
        z_done = sem("j_z_done")
        z_taken = sem("j_z_taken")
        abs_done = sem("j_abs")
        b_ready = sem("j_b")
        b_stored = sem("j_b_stored")
        vstep = sem("j_vstep")
        pstep = sem("j_pstep")
        block = ctx.enter_context(nc.Block())

        def n_of(t):
            return NSAMP if t == TILES else P

        @block.sync
        def _(sp):
            sp.dma_start(g_mix[:, :], g_mix_dram.to_broadcast([P, D])).then_inc(consts, 16)
            sp.dma_start(w_decay[:, :], w_decay_dram).then_inc(consts, 16)
            sp.dma_start(b_decay[:, :], b_decay_dram).then_inc(consts, 16)
            for t in range(NT):
                wait(sp, xn_ready, t - 2)
                sp.dma_start(x[0:n_of(t), t % 3, :], x_dram[t * P:t * P + n_of(t), :]).then_inc(x_in[t % 3], 16)
                if t == 1:
                    sp.dma_start(w[:, :], w_big_dram[0]).then_inc(w_in, 16)
            with sp.Fori(1, TOK_CHUNKS + FEAT_CHUNKS) as c:
                sp.wait_ge(wl_ready, c)
                sp.dma_start(w[:, :], w_big_dram[bass.ds(c, 1), :, :].rearrange("o p n -> p (o n)")).then_inc(w_in, 16)
            sp.wait_ge(wl_ready, TOK_CHUNKS + FEAT_CHUNKS)
            sp.dma_start(w[:, 0:KT * SMALL], w_small_dram.rearrange("p k n -> p (k n)")).then_inc(w_in, 16)
            for j in range(GLA_HEADS):
                sp.wait_ge(b_ready, j + 1)
                sp.dma_start(z_b[j], la[:, 1, :]).then_inc(b_stored, 16)
            sp.wait_ge(b_stored, 16 * GLA_HEADS)

        @block.gpsimd
        def _(pool):
            pool.memset(ident[:, :], 0.0).then_inc(pstep, 1)
            pool.wait_ge(pstep, 1)
            pool.affine_select(out=ident[:, :], in_=ident[:, :], compare_op=ALU.not_equal, fill=1.0,
                               base=0, pattern=[[-1, P]], channel_multiplier=1).then_inc(made, 1)
            pool.memset(keep[:, :], 1.0).then_inc(pstep, 1)
            pool.wait_ge(pstep, 2)
            pool.memset(keep[:, 0:SEQ:P], 0.0).then_inc(made, 1)
            pool.memset(keep[:, SEQ:TOK:STEPS], 0.0).then_inc(made, 1)
            for half in (xh, xl):
                pool.memset(half[:, :, TOK:PAD].bitcast(F32), 0.0).then_inc(made, 1)

        @block.scalar
        def _(act):
            act.wait_ge(made, 5)

            def transposed(t):
                n = n_of(t)
                for i in range(2):
                    act.wait_ge(xnT_ps, 2 * t + i + 1)
                    act.activation(xh[:, 4 * i:4 * i + 4, t * P:t * P + n], t_ps[i][:, :, 0:n],
                                   ACT.Copy).then_inc(xh_ready, 1)

            for t in range(NT):
                n = n_of(t)
                act.wait_ge(x_in[t % 3], 16 * (t // 3 + 1))
                if t >= 2:
                    act.wait_ge(xnT_ps, 2 * (t - 1))
                act.activation(xn[0:n, t % 2, :], x[0:n, t % 3, :], ACT.Square,
                               accum_out=stat[0:n, t, 0:1]).then_inc(sq_done, 1)
                act.wait_ge(rt_in, t + 1)
                act.activation(stat[0:n, t, 2:3], stat[0:n, t, 1:2], ACT.Sqrt).then_inc(rt_done, 1)
                if t:
                    transposed(t - 1)
            transposed(NT - 1)

            def high(c, s, width=KT * CHUNK):
                act.wait_ge(w_in, 16 * (c + 1))
                wait(act, chunk_used, c - 1)
                act.activation(wh[:, s, 0:width], w[:, 0:width], ACT.Copy).then_inc(wh_ready, 1)

            def take(item, slot, use, n, width, func, dst):
                act.wait_ge(m_done, item + 1)
                wait(act, stored[slot], 16 * use)
                act.activation(stage[0:n, slot, 0:width], m_ps[slot][0:n, 0:width], func).then_inc(staged, 1)
                act.wait_ge(staged, item + 1)
                act.dma_start(dst, stage[0:n, slot, 0:width]).then_inc(stored[slot], 16)

            def tokens(c, func):
                for t in range(NT):
                    take(c * NT + t, t % SLOTS, c * (NT // SLOTS) + t // SLOTS, n_of(t), CHUNK, func,
                         z_tok[t * P:t * P + n_of(t), bass.ds(c * CHUNK, CHUNK)])

            high(0, 0)
            high(1, 1)
            for c in range(2):
                tokens(c, ACT.Copy)
                high(c + 2, c % 2)
            for c in range(2, 4):
                tokens(c, ACT.Silu)
                high(c + 2, c % 2)
            with act.Fori(2, TOK_CHUNKS // 2) as i:
                for s in range(2):
                    tokens(2 * i + s, ACT.Sigmoid)
                    high(2 * i + s + 2, s)
            base, uses = TOK_CHUNKS * NT, TOK_CHUNKS * NT // SLOTS

            def features(c):
                for b in range(CHUNK // P):
                    for g, (g0, gn) in enumerate(GROUPS):
                        take(base + c * NF + b * 3 + g, g, uses + c * 4 + b, P, gn, ACT.Copy,
                             z_feat[bass.ds(c * 4 + b, 1), :, g0:g0 + gn].rearrange("o p n -> p (o n)"))

            for c in range(FEAT_CHUNKS):
                features(c)
                if c + 2 < FEAT_CHUNKS:
                    high(TOK_CHUNKS + c + 2, c % 2)
                elif c + 2 == FEAT_CHUNKS:
                    high(TOK_CHUNKS + FEAT_CHUNKS, 0, KT * SMALL)
            base, uses = base + FEAT_CHUNKS * NF, uses + FEAT_CHUNKS * NF // SLOTS
            for t in range(NT):
                take(base + t, t % SLOTS, uses + t // SLOTS, n_of(t), 2 * KV, ACT.Copy, z_kv[t * P:t * P + n_of(t), :])
            base, uses = base + NT, uses + NT // SLOTS
            act.wait_ge(xn_ready, NT)
            for g, (g0, gn) in enumerate(GROUPS):
                take(base + g, g, uses, P, gn, ACT.Copy, z_kT[:, g0:g0 + gn])
            for g, (g0, gn) in enumerate(GROUPS):
                act.wait_ge(m_done, base + 3 + g + 1)
                act.activation(low[:, g0:g0 + gn], m_ps[g][0:RANK, 0:gn], ACT.Copy).then_inc(staged, 1)
            for j in range(GLA_HEADS):
                act.wait_ge(z_taken, 3 * (j + 1))
                wait(act, b_ready, j)
                act.activation(la[:, 0, :], z[:, :], ACT.Abs).then_inc(abs_done, 1)
                act.wait_ge(abs_done, 3 * j + 1)
                act.activation(la[:, 0, :], la[:, 0, :], ACT.Exp, scale=-1.0).then_inc(abs_done, 1)
                act.wait_ge(abs_done, 3 * j + 2)
                act.activation(la[:, 0, :], la[:, 0, :], ACT.Ln, bias=1.0).then_inc(abs_done, 1)
            for slot in range(SLOTS):
                act.wait_ge(stored[slot], 16 * (uses + 1))

        @block.vector
        def _(dve):
            chain = Chain(dve, vstep)
            dve.wait_ge(consts, 48)

            def low_half(t):
                n = n_of(t)
                for i in range(2):
                    dve.wait_ge(xh_ready, 2 * t + i + 1)
                    cols = slice(t * P, t * P + n)
                    dve.tensor_tensor(xl[:, 4 * i:4 * i + 4, cols], t_ps[i][:, :, 0:n],
                                      xh[:, 4 * i:4 * i + 4, cols].bitcast(F32), ALU.subtract).then_inc(xl_ready, 1)

            for t in range(NT):
                n = n_of(t)
                dve.wait_ge(sq_done, t + 1)
                dve.tensor_scalar(stat[0:n, t, 1:2], stat[0:n, t, 0:1], 1.0 / D, EPS, ALU.mult,
                                  ALU.add).then_inc(rt_in, 1)
                dve.wait_ge(rt_done, t + 1)
                chain.link(dve.reciprocal(stat[0:n, t, 3:4], stat[0:n, t, 2:3]))
                dve.scalar_tensor_tensor(out=xn[0:n, t % 2, :], in0=x[0:n, t % 3, :], scalar=stat[0:n, t, 3:4],
                                         in1=g_mix[0:n, :], op0=ALU.mult, op1=ALU.mult).then_inc(xn_ready, 1)
                if t:
                    low_half(t - 1)
            low_half(NT - 1)

            def split(c, s, width=KT * CHUNK):
                dve.wait_ge(wh_ready, c + 1)
                dve.tensor_tensor(wl[:, s, 0:width], w[:, 0:width], wh[:, s, 0:width].bitcast(F32), ALU.subtract
                                  ).then_inc(wl_ready, 1)

            with dve.Fori(0, (TOK_CHUNKS + FEAT_CHUNKS) // 2) as i:
                for s in range(2):
                    split(2 * i + s, s)
            split(TOK_CHUNKS + FEAT_CHUNKS, 0, KT * SMALL)
            for j in range(GLA_HEADS):
                wait(dve, abs_done, 3 * j)
                for g, (g0, gn) in enumerate(GROUPS):
                    dve.wait_ge(z_done, 3 * j + g + 1)
                    if g == 0 and j:
                        dve.wait_ge(b_ready, j)
                    dve.tensor_scalar(z[:, g0:g0 + gn], z_ps[g][:, 0:gn], b_decay[:, j:j + 1], None,
                                      ALU.add).then_inc(z_taken, 1)
                dve.wait_ge(abs_done, 3 * (j + 1))
                chain.link(dve.scalar_tensor_tensor(out=z[:, :], in0=z[:, :], scalar=0.0, in1=la[:, 0, :],
                                                    op0=ALU.min, op1=ALU.subtract))
                wait(dve, b_stored, 16 * j)
                chain.link(dve.tensor_tensor_scan(la[:, 1, :], keep[:, :], z[:, :], 0.0, ALU.mult, ALU.add))
                dve.tensor_scalar(la[:, 1, :], la[:, 1, :], 1.0 / 16.0, None, ALU.mult).then_inc(b_ready, 1)

        @block.tensor
        def _(pe):
            pe.wait_ge(made, 5)
            pe.wait_ge(consts, 48)
            for t in range(NT):
                n = n_of(t)
                pe.wait_ge(xn_ready, t + 1)
                for i in range(2):
                    wait(pe, xl_ready, 2 * (t - 1) + i + 1)
                    for j in range(4):
                        k = 4 * i + j
                        last = pe.transpose(t_ps[i][:, j, 0:n], xn[0:n, t % 2, k * P:(k + 1) * P], ident[0:n, 0:n])
                    last.then_inc(xnT_ps, 1)
            pe.wait_ge(xl_ready, 2 * NT)

            def product(item, slot, width, lhs, rhs):
                wait(pe, staged, item - SLOTS + 1)
                out = m_ps[slot][:, 0:width]
                for k in range(KT):
                    (lh, ll), (rh, rl) = lhs(k), rhs(k)
                    pe.matmul(out, lh, rh, start=(k == 0), stop=False)
                    pe.matmul(out, lh, rl, start=False, stop=False)
                    last = pe.matmul(out, ll, rh, start=False, stop=(k == KT - 1))
                last.then_inc(m_done, 1)

            def xn_part(start, width):
                return lambda k: [half[:, k, start:start + width] for half in (xh, xl)]

            def w_part(s, start, width, columns=CHUNK):
                return lambda k: [half[:, s, k * columns + start:k * columns + start + width] for half in (wh, wl)]

            def tokens(c, s):
                pe.wait_ge(wl_ready, c + 1)
                for t in range(NT):
                    product(c * NT + t, t % SLOTS, CHUNK, xn_part(t * P, P), w_part(s, 0, CHUNK))
                pe.wait_ge(m_done, (c + 1) * NT)
                pe.sem_inc(chunk_used, 1)

            for s in range(2):
                tokens(s, s)
            with pe.Fori(1, TOK_CHUNKS // 2) as i:
                for s in range(2):
                    tokens(2 * i + s, s)
            base = TOK_CHUNKS * NT
            with pe.Fori(0, FEAT_CHUNKS // 2) as i:
                for s in range(2):
                    c = 2 * i + s
                    pe.wait_ge(wl_ready, TOK_CHUNKS + c + 1)
                    for b in range(CHUNK // P):
                        for g, (g0, gn) in enumerate(GROUPS):
                            product(base + c * NF + b * 3 + g, g, gn, w_part(s, b * P, P), xn_part(g0, gn))
                    pe.wait_ge(m_done, base + (c + 1) * NF)
                    pe.sem_inc(chunk_used, 1)
            base += FEAT_CHUNKS * NF
            pe.wait_ge(wl_ready, TOK_CHUNKS + FEAT_CHUNKS + 1)
            for t in range(NT):
                product(base + t, t % SLOTS, 2 * KV, xn_part(t * P, P), w_part(0, RANK, 2 * KV, SMALL))
            base += NT
            for g, (g0, gn) in enumerate(GROUPS):
                product(base + g, g, gn, w_part(0, RANK, KV, SMALL), xn_part(g0, gn))
            for g, (g0, gn) in enumerate(GROUPS):
                product(base + 3 + g, g, gn, w_part(0, 0, P, SMALL), xn_part(g0, gn))
            pe.wait_ge(staged, base + 6)
            for j in range(GLA_HEADS):
                for g, (g0, gn) in enumerate(GROUPS):
                    wait(pe, z_taken, 3 * (j - 1) + g + 1)
                    pe.matmul(z_ps[g][:, 0:gn], w_decay[:, j * DK:(j + 1) * DK], low[:, g0:g0 + gn],
                              start=True, stop=True).then_inc(z_done, 1)


class Tail:

    def __init__(self, sb, sem, name):
        self.v_gate = sb(name + "gate", [P, D])
        self.ga = sb(name + "ga", [P, D])
        self.gb = sb(name + "gb", [P, D])
        self.x = sb(name + "x", [P, D])
        self.oa = sb(name + "oa", [P, D])
        self.oaT = sb(name + "oaT", [P, KT, P])
        self.obT = sb(name + "obT", [P, KT, P])
        self.mT = sb(name + "mT", [P, KT, P])
        self.h = sb(name + "h", [P, D])
        self.stat = sb(name + "stat", [P, 4, GLA_HEADS])
        self.vgate_in = sem(name + "vgate_in")
        self.gates_in = sem(name + "gates_in")
        self.gate_ready = sem(name + "gate_ready")
        self.o_done = sem(name + "o_done")
        self.sq_done = sem(name + "sq_done")
        self.rt_in = sem(name + "rt_in")
        self.rt_done = sem(name + "rt_done")
        self.oa_ready = sem(name + "oa_ready")
        self.ob_done = sem(name + "ob_done")
        self.obT_ready = sem(name + "obT_ready")
        self.r_done = sem(name + "r_done")
        self.r_taken = sem(name + "r_taken")
        self.m_ready = sem(name + "m_ready")
        self.h_stored = sem(name + "h_stored")


TAIL = 10


def mix_stage(nc, sem, x_dram, wa_dram, wb_dram, wo_dram, gla_norm_dram, sinks_dram, sink_rows_dram, mask_dram,
              causal_dram, samp_mask_dram, samp_causal_dram, seg_cols_dram, seg_rows_dram, cache_kT_dram,
              cache_v_dram, cache_k_rows, cache_v_rows, state_dram, z_tok, z_feat, z_kv, z_kT, z_b, h_dram,
              pk_dram, pv_dram, ps_dram, sk_dram, sv_dram, ss_dram):
    QSCALE = DK ** -0.5
    with ExitStack() as outer:
        def sbo(name, shape, dt=F32):
            return outer.enter_context(nc.sbuf_tensor(name, shape, dt))

        wa = sbo("wa", [P, KT, D])
        wb = sbo("wb", [P, KT, D])
        wo = sbo("wo", [P, KT, D])
        gn = sbo("gn", [P, DV])
        ident = sbo("m_ident", [P, P])
        X = outer.enter_context(nc.psum_tensor("X", [P, D], F32))
        O = outer.enter_context(nc.psum_tensor("O", [P, D], F32))
        U = outer.enter_context(nc.psum_tensor("U", [P, D], F32))
        R = outer.enter_context(nc.psum_tensor("R", [P, 2, BANK], F32))


        def tail_norm_act(act, T, t, n):
            for h in range(GLA_HEADS):
                if h == 0:
                    act.wait_ge(T.o_done, GLA_HEADS * (t + 1))
                    wait(act, T.r_done, TAIL * (t - 1) + 2)
                act.activation(T.oa[0:n, h * DV:(h + 1) * DV], O[0:n, h * DV:(h + 1) * DV], ACT.Square,
                               accum_out=T.stat[0:n, 0, h:h + 1]).then_inc(T.sq_done, 1)
            act.wait_ge(T.rt_in, t + 1)
            act.activation(T.stat[0:n, 2, :], T.stat[0:n, 1, :], ACT.Sqrt).then_inc(T.rt_done, 1)

        def tail_oa_dve(dve, chain, T, t, n):
            dve.wait_ge(T.sq_done, GLA_HEADS * (t + 1))
            dve.tensor_scalar(T.stat[0:n, 1, :], T.stat[0:n, 0, :], 1.0 / DV, EPS, ALU.mult, ALU.add).then_inc(T.rt_in, 1)
            dve.wait_ge(T.rt_done, t + 1)
            chain.link(dve.reciprocal(T.stat[0:n, 3, :], T.stat[0:n, 2, :]))
            dve.wait_ge(T.gate_ready, t + 1)
            for h in range(GLA_HEADS):
                cols = slice(h * DV, (h + 1) * DV)
                last = dve.scalar_tensor_tensor(out=T.oa[0:n, cols], in0=O[0:n, cols], scalar=T.stat[0:n, 3, h:h + 1],
                                                in1=T.v_gate[0:n, cols], op0=ALU.mult, op1=ALU.mult)
                if h < GLA_HEADS - 1:
                    chain.step(last)
            last.then_inc(T.oa_ready, 1)

        def tail_dve(dve, chain, T, t, n, step):
            kind, c = divmod(step, 2)
            cols = slice(c * BANK, (c + 1) * BANK)
            dve.wait_ge(T.r_done, TAIL * t + step + 1)
            turned = R[:, c, :].rearrange("p (k n) -> p k n", k=4)[:, :, 0:n]
            if kind == 0:
                dve.tensor_copy(T.oaT[:, 4 * c:4 * c + 4, 0:n], turned).then_inc(T.r_taken, 1)
            elif kind == 1:
                if c == 0:
                    dve.wait_ge(T.gates_in, 48 * (t + 1))
                dve.tensor_tensor(T.ga[0:n, cols], R[0:n, c, :], T.ga[0:n, cols], ALU.mult).then_inc(T.r_taken, 1)
            elif kind == 2:
                dve.tensor_tensor(T.gb[0:n, cols], R[0:n, c, :], T.gb[0:n, cols], ALU.mult).then_inc(T.r_taken, 1)
                dve.wait_ge(T.r_taken, TAIL * t + step + 1)
                dve.tensor_tensor(T.ga[0:n, cols], T.ga[0:n, cols], T.gb[0:n, cols], ALU.add).then_inc(T.m_ready, 1)
            elif kind == 3:
                dve.tensor_copy(T.mT[:, 4 * c:4 * c + 4, 0:n], turned).then_inc(T.r_taken, 1)
            else:
                if c == 0:
                    wait(dve, T.h_stored, 16 * t)
                dve.tensor_tensor(T.h[0:n, cols], R[0:n, c, :], T.x[0:n, cols], ALU.add).then_inc(T.r_taken, 1)

        def tail_act(act, T, t, n):
            act.wait_ge(T.ob_done, t + 1)
            wait(act, T.r_done, TAIL * (t - 1) + 6)
            act.activation(T.obT[:, :, 0:n], U[:, 0:KT * n].rearrange("p (k n) -> p k n", k=KT),
                           ACT.Copy).then_inc(T.obT_ready, 1)

        def tail_pe(pe, T, t, n, step):
            kind, c = divmod(step, 2)
            wait(pe, T.r_taken, TAIL * t + step - 1)
            if step == 0:
                pe.wait_ge(T.oa_ready, t + 1)
            elif kind == 1 or kind == 4:
                pe.wait_ge(T.r_taken, TAIL * t + 2 * kind)
            elif step == 4:
                pe.wait_ge(T.obT_ready, t + 1)
            elif kind == 3:
                pe.wait_ge(T.m_ready, 2 * t + c + 1)
            if kind in (0, 3):
                src = T.oa if kind == 0 else T.ga
                for j in range(4):
                    k = 4 * c + j
                    last = pe.transpose(R[:, c, j * P:j * P + n], src[0:n, k * P:(k + 1) * P], ident[0:n, 0:n])
            else:
                lhsT, w = {1: (T.oaT, wa), 2: (T.obT, wb), 4: (T.mT, wo)}[kind]
                for k in range(KT):
                    last = pe.matmul(R[0:n, c, :], lhsT[:, k, 0:n], w[:, k, c * BANK:(c + 1) * BANK],
                                     start=(k == 0), stop=(k == KT - 1))
            last.then_inc(T.r_done, 1)

        def load_vgate(sp, T, rows, n):
            sp.dma_start(T.v_gate[0:n, :], z_tok[rows, D:2 * D]).then_inc(T.vgate_in, 16)

        def load_gates(sp, T, rows, n):
            for i, dst in ((2, T.ga), (3, T.gb)):
                sp.dma_start(dst[0:n, :], z_tok[rows, i * D:(i + 1) * D]).then_inc(T.gates_in, 16)
            sp.dma_start(T.x[0:n, :], x_dram[rows, :]).then_inc(T.gates_in, 16)

        def gate_norm(pool, T, t, n):
            pool.wait_ge(T.vgate_in, 16 * (t + 1))
            pool.tensor_tensor(T.v_gate[0:n, :].rearrange("p (h e) -> p h e", h=GLA_HEADS),
                               T.v_gate[0:n, :].rearrange("p (h e) -> p h e", h=GLA_HEADS),
                               gn[0:n, :].unsqueeze(1).to_broadcast([n, GLA_HEADS, DV]), ALU.mult
                               ).then_inc(T.gate_ready, 1)


        with ExitStack() as ctx:
            def sb(name, shape, dt=F32):
                return ctx.enter_context(nc.sbuf_tensor(name, shape, dt))

            T = Tail(sb, sem, "p_")
            q = sb("q", [P, GLA_HEADS, P])
            k = sb("k", [P, GLA_HEADS, P])
            b = sb("b", [P, GLA_HEADS, P])
            v = sb("v", [P, D])
            sq = sb("sq", [P, KT, P])
            kk = sb("kk", [P, KV_HEADS, 2, P])
            vv = sb("vv", [P, 2, KV])
            mask = sb("mask", [P, 2, 2 * P])
            causal = sb("causal", [P, P])
            sinks = sb("sinks", [P, SWA_HEADS])
            rel = sb("rel", [P, 2, SUBS, P])
            qt = sb("qt", [P, 2, P])
            qb = sb("qb", [P, 2, P])
            eb = sb("eb", [P, 2, P])
            kp = sb("kp", [P, 2, P])
            kpT = sb("kpT", [P, 2, P])
            scm = sb("scm", [P, 2, P])
            S = sb("S", [P, GLA_HEADS, DV])
            s = sb("s", [P, SWA_HEADS, 2 * P])
            m = sb("m", [P, 4, SWA_HEADS])
            e_sum = sb("e_sum", [P, SWA_HEADS])
            pT = sb("pT", [P, 2, 4, P])

            consts = sem("m_consts")
            weights = sem("m_weights")
            zeroed = sem("zeroed")
            gla_in = sem("gla_in")
            swa_in = sem("swa_in")
            vv_in = sem("vv_in")
            s_done = sem("m_s_done")
            s_taken = sem("m_s_taken")
            neg_ready = sem("neg_ready")
            e_done = sem("m_e_done")
            p_ready = sem("p_ready")
            pT_ps = sem("pT_ps")
            pT_ready = sem("pT_ready")
            rel_ready = sem("rel_ready")
            ex_done = sem("ex_done")
            kq_ready = sem("kq_ready")
            sc_done = sem("sc_done")
            kpT_ready = sem("kpT_ready")
            scm_ready = sem("scm_ready")
            su_done = sem("su_done")
            S_ready = sem("S_ready")
            out_copied = sem("out_copied")
            vstep = sem("m_vstep")
            tick = sem("m_tick")
            astep = sem("m_astep")
            pstep = sem("m_pstep")
            block = ctx.enter_context(nc.Block())

            def score_pair(i, j):
                return (X, O)[i % 2][:, j * BANK:j * BANK + 2 * P]

            def update(h):
                at = (h % 2) * BANK + (h // 2) * DV
                return U[:, at:at + DV]

            @block.sync
            def _(sp):
                def load_gla(t):
                    wait_alone(sp, su_done, GLA_HEADS * t, tick)
                    cols = bass.ds(t * P, P)
                    for dst, src in ((b, z_b[:, :, cols]), (k, z_feat[4:8, :, cols]), (q, z_feat[0:4, :, cols])):
                        sp.dma_start(dst[:, :, :], src.rearrange("h p n -> p h n")).then_inc(gla_in, 16)
                    sp.dma_start(v[:, :], z_tok[cols, 0:D]).then_inc(gla_in, 16)

                def window(t):
                    first = isinstance(t, int) and t == 0
                    return (1, 0, P) if first else (0, t * P - P, 2 * P)

                def load_swa(t):
                    rows, (old, start, width) = bass.ds(t * P, P), window(t)
                    wait_alone(sp, s_done, 8 * t, tick)
                    sp.dma_start(sq[:, :, :], z_feat[8:16, :, rows].rearrange("h p n -> p h n")
                                 ).then_inc(swa_in, 16)
                    for half in range(2):
                        sp.dma_start(kk[half * HD:(half + 1) * HD, :, :, :].rearrange("d g a n -> d g (a n)")[:, :, old * P:],
                                     z_kT[:, bass.ds(start, width)].rearrange("(g d) n -> d g n", g=KV_HEADS)
                                     ).then_inc(swa_in, 16)

                def load_values(t):
                    old, start, width = window(t)
                    wait(sp, T.ob_done, t)
                    sp.dma_start(vv[:, old:, :], z_kv[bass.ds(start, width), KV:2 * KV].rearrange("(a p) c -> p a c", p=P)
                                 ).then_inc(vv_in, 16)

                def finish(t):
                    rows = bass.ds(t * P, P)
                    wait_alone(sp, T.r_taken, TAIL * (t + 1), tick)
                    sp.dma_start(h_dram[rows, :], T.h[:, :]).then_inc(T.h_stored, 16)

                sp.dma_start(mask[:, :, :], mask_dram).then_inc(consts, 16)
                sp.dma_start(causal[:, :], causal_dram).then_inc(consts, 16)
                sp.dma_start(sinks[:, :], sinks_dram.to_broadcast([P, SWA_HEADS])).then_inc(consts, 16)
                sp.dma_start(gn[:, :], gla_norm_dram.to_broadcast([P, DV])).then_inc(consts, 16)
                load_gla(0)
                load_swa(0)
                load_values(0)
                load_vgate(sp, T, bass.ds(0, P), P)
                load_gates(sp, T, bass.ds(0, P), P)
                for dst, src in ((wa, wa_dram), (wb, wb_dram), (wo, wo_dram)):
                    sp.dma_start(dst[:, :, :], src).then_inc(weights, 16)
                for dst, src in ((pk_dram, z_kv[SEQ - WINDOW:SEQ, 0:KV]), (pv_dram, z_kv[SEQ - WINDOW:SEQ, KV:2 * KV])):
                    sp.dma_start(dst, src).then_inc(out_copied, 16)
                for dst, src, new in ((sk_dram, cache_k_rows, 0), (sv_dram, cache_v_rows, KV)):
                    sp.dma_start(dst[:, 0:WINDOW - STEPS, :], src[:, STEPS:WINDOW, :]).then_inc(out_copied, 16)
                    sp.dma_start(dst[:, WINDOW - STEPS:WINDOW, :],
                                 z_kv[SEQ:TOK, new:new + KV].rearrange("(b s) c -> b s c", s=STEPS)).then_inc(out_copied, 16)

                def tile(t):
                    load_swa_next = not (isinstance(t, int) and t == TILES - 1)
                    if load_swa_next:
                        load_swa(t + 1)
                    if not (isinstance(t, int) and t == 0):
                        finish(t - 1)
                        load_gates(sp, T, bass.ds(t * P, P), P)
                    if load_swa_next:
                        load_gla(t + 1)
                        load_values(t + 1)
                        rows = bass.ds((t + 1) * P, P)
                        sp.wait_ge(T.oa_ready, t + 1)
                        load_vgate(sp, T, rows, P)

                tile(0)
                with sp.Fori(1, TILES - 1) as t:
                    tile(t)
                tile(TILES - 1)
                sp.wait_ge(S_ready, GLA_HEADS * TILES)
                sp.dma_start(ps_dram.rearrange("h d e -> d h e"), S[:, :, :]).then_inc(out_copied, 16)
                finish(TILES - 1)
                sp.wait_ge(out_copied, 16 * 7)
                sp.wait_ge(T.h_stored, 16 * TILES)

            @block.gpsimd
            def _(pool):
                pool.memset(ident[:, :], 0.0).then_inc(pstep, 1)
                pool.wait_ge(pstep, 1)
                pool.affine_select(out=ident[:, :], in_=ident[:, :], compare_op=ALU.not_equal, fill=1.0,
                                   base=0, pattern=[[-1, P]], channel_multiplier=1).then_inc(zeroed, 1)
                pool.memset(S[:, :, :], 0.0).then_inc(zeroed, 1)
                pool.memset(kk[:, :, 0, :], 0.0).then_inc(zeroed, 1)
                pool.memset(vv[:, 0, :], 0.0).then_inc(zeroed, 1)
                pool.wait_ge(consts, 16 * 4)
                gate_norm(pool, T, 0, P)
                with pool.Fori(1, TILES) as t:
                    gate_norm(pool, T, t, P)

            @block.scalar
            def _(act):
                chain = Chain(act, astep)
                act.wait_ge(zeroed, 4)

                def gla_exp(t, h):
                    i = GLA_HEADS * t + h
                    act.wait_ge(rel_ready, i + 1)
                    wait(act, T.o_done, i - 1)
                    chain.step(act.activation(rel[:, h % 2, :, :], rel[:, h % 2, :, :], ACT.Exp, scale=-1.0))
                    chain.step(act.activation(qt[:, h % 2, :], qt[:, h % 2, :], ACT.Exp))
                    chain.step(act.activation(eb[:, h % 2, :], b[:, h, :], ACT.Exp))
                    act.activation(kp[:, h % 2, :], b[:, h, :], ACT.Exp, bias=b[:, h, P - 1:P], scale=-1.0).then_inc(ex_done, 1)

                def tile(t):
                    gla_exp(t, 0)
                    gla_exp(t, 1)
                    act.wait_ge(neg_ready, t + 1)
                    for h in range(SWA_HEADS):
                        chain.step(act.activation(s[:, h, :], s[:, h, :], ACT.Exp, bias=m[:, 1, h:h + 1],
                                                  accum_out=e_sum[:, h:h + 1]))
                    act.activation(m[:, 2, :], m[:, 2, :], ACT.Exp).then_inc(e_done, 1)
                    for h in range(GLA_HEADS):
                        act.wait_ge(sc_done, GLA_HEADS * t + h + 1)
                        wait(act, su_done, GLA_HEADS * t + h - 1)
                        act.activation(kpT[:, h % 2, :], X[:, BANK + h * P:BANK + (h + 1) * P],
                                       ACT.Copy).then_inc(kpT_ready, 1)
                        if h < 2:
                            gla_exp(t, h + 2)
                    tail_norm_act(act, T, t, P)
                    for i in range(SWA_HEADS // 2):
                        act.wait_ge(pT_ps, 8 * t + i + 1)
                        act.activation(pT[:, i % 2, :, :], X[:, (i % 2) * BANK:(i % 2 + 1) * BANK].rearrange("p (a n) -> p a n", a=4),
                                       ACT.Copy).then_inc(pT_ready, 1)
                    tail_act(act, T, t, P)
                    chain.restart()

                tile(0)
                with act.Fori(1, TILES) as t:
                    tile(t)

            @block.vector
            def _(dve):
                chain = Chain(dve, vstep)
                dve.wait_ge(consts, 16 * 4)
                dve.wait_ge(zeroed, 4)

                def exponents(t, h):
                    i = GLA_HEADS * t + h
                    if h == 0:
                        dve.wait_ge(gla_in, 64 * (t + 1))
                    wait(dve, sc_done, i - 1)
                    for j in range(SUBS):
                        ref = b[:, h, j * SUB + SUB // 2:j * SUB + SUB // 2 + 1]
                        chain.step(dve.tensor_scalar(rel[:, h % 2, j, :], b[:, h, :], ref, -CLAMP, ALU.subtract, ALU.max))
                    blocks = b[:, h, :].rearrange("p (j i) -> p j i", j=SUBS)
                    view = qt[:, h % 2, :].rearrange("p (j i) -> p j i", j=SUBS)
                    chain.link(dve.tensor_tensor(view, blocks, blocks[:, :, SUB // 2:SUB // 2 + 1].to_broadcast([P, SUBS, SUB]),
                                                 ALU.subtract))
                    dve.tensor_scalar(qt[:, h % 2, :], qt[:, h % 2, :], CLAMP, None, ALU.min).then_inc(rel_ready, 1)

                def rescale(t, h):
                    i = GLA_HEADS * t + h
                    dve.wait_ge(ex_done, i + 1)
                    chain.step(dve.tensor_tensor(rel[:, h % 2, :, :], rel[:, h % 2, :, :],
                                                 k[:, h, :].unsqueeze(1).to_broadcast([P, SUBS, P]), ALU.mult))
                    wait(dve, T.o_done, i - 1)
                    chain.step(dve.scalar_tensor_tensor(out=qt[:, h % 2, :], in0=q[:, h, :], scalar=QSCALE,
                                                        in1=qt[:, h % 2, :], op0=ALU.mult, op1=ALU.mult))
                    chain.step(dve.scalar_tensor_tensor(out=qb[:, h % 2, :], in0=q[:, h, :], scalar=QSCALE,
                                                        in1=eb[:, h % 2, :], op0=ALU.mult, op1=ALU.mult))
                    dve.tensor_tensor(kp[:, h % 2, :], k[:, h, :], kp[:, h % 2, :], ALU.mult).then_inc(kq_ready, 1)

                def masked(t, h):
                    i = GLA_HEADS * t + h
                    dve.wait_ge(sc_done, i + 1)
                    dve.tensor_tensor(scm[:, h % 2, :], X[:, h * P:(h + 1) * P], causal[:, :], ALU.mult).then_inc(scm_ready, 1)

                def advance(t, h):
                    i = GLA_HEADS * t + h
                    dve.wait_ge(su_done, i + 1)
                    dve.scalar_tensor_tensor(out=S[:, h, :], in0=S[:, h, :], scalar=eb[:, h % 2, P - 1:P],
                                             in1=update(h), op0=ALU.mult, op1=ALU.add).then_inc(S_ready, 1)

                def tile(t):
                    first = isinstance(t, int) and t == 0

                    def tail(*steps):
                        for step in steps:
                            if not first:
                                tail_dve(dve, chain, T, t - 1, P, step)

                    exponents(t, 0)
                    exponents(t, 1)
                    for i in range(SWA_HEADS // 2):
                        wait_alone(dve, s_done, 8 * t + i + 1, tick)
                        if i == 0:
                            chain.settle()
                        for j in range(2):
                            h = 2 * i + j
                            last = dve.tensor_tensor_reduce(s[:, h, :], score_pair(i, j), mask[:, 0 if first else 1, :],
                                                            HD ** -0.5, sinks[:, h:h + 1], ALU.add, ALU.max,
                                                            m[:, 0, h:h + 1])
                            if j == 0:
                                chain.step(last)
                        last.then_inc(s_taken, 1)
                        tail(*{1: (0, 1), 3: (2,), 5: (3,)}.get(i, ()))
                    dve.wait_ge(s_taken, 8 * (t + 1))
                    chain.step(dve.tensor_scalar(m[:, 1, :], m[:, 0, :], -1.0, None, ALU.mult))
                    dve.tensor_tensor(m[:, 2, :], sinks[:, :], m[:, 0, :], ALU.subtract).then_inc(neg_ready, 1)
                    rescale(t, 0)
                    rescale(t, 1)
                    tail(4)
                    masked(t, 0)
                    tail(5)
                    advance(t, 0)
                    exponents(t, 2)
                    masked(t, 1)
                    tail(6, 7)
                    advance(t, 1)
                    exponents(t, 3)
                    rescale(t, 2)
                    dve.wait_ge(e_done, t + 1)
                    chain.link(dve.tensor_tensor(m[:, 3, :], e_sum[:, :], m[:, 2, :], ALU.add))
                    chain.link(dve.reciprocal(m[:, 3, :], m[:, 3, :]))
                    dve.tensor_tensor(s[:, :, :], s[:, :, :], m[:, 3, :].unsqueeze(2).to_broadcast([P, SWA_HEADS, 2 * P]),
                                      ALU.mult).then_inc(p_ready, 1)
                    masked(t, 2)
                    tail(8)
                    advance(t, 2)
                    rescale(t, 3)
                    masked(t, 3)
                    tail(9)
                    advance(t, 3)
                    tail_oa_dve(dve, chain, T, t, P)
                    chain.restart()

                tile(0)
                tile(1)
                with dve.Fori(2, TILES) as t:
                    tile(t)
                for step in range(TAIL):
                    tail_dve(dve, chain, T, TILES - 1, P, step)

            @block.tensor
            def _(pe):
                pe.wait_ge(zeroed, 4)

                def gla_scores(t, h):
                    i = GLA_HEADS * t + h
                    pe.wait_ge(kq_ready, i + 1)
                    for j in range(SUBS):
                        pe.matmul(X[:, h * P + j * SUB:h * P + (j + 1) * SUB], rel[:, h % 2, j, :],
                                  qt[:, h % 2, j * SUB:(j + 1) * SUB], start=True, stop=True)
                    pe.transpose(X[:, BANK + h * P:BANK + (h + 1) * P], kp[:, h % 2, :], ident[:, :]).then_inc(sc_done, 1)

                def gla_out(t, h):
                    i = GLA_HEADS * t + h
                    vh = v[:, h * DV:(h + 1) * DV]
                    pe.wait_ge(scm_ready, i + 1)
                    wait(pe, S_ready, i - GLA_HEADS + 1)
                    pe.matmul(O[:, h * DV:(h + 1) * DV], scm[:, h % 2, :], vh, start=True, stop=False)
                    pe.matmul(O[:, h * DV:(h + 1) * DV], qb[:, h % 2, :], S[:, h, :], start=False, stop=True
                              ).then_inc(T.o_done, 1)
                    pe.wait_ge(kpT_ready, i + 1)
                    pe.wait_ge(T.o_done, i + 1)
                    if h >= 2:
                        pe.wait_ge(S_ready, i - 1)
                    pe.matmul(update(h), kpT[:, h % 2, :], vh, start=True, stop=True).then_inc(su_done, 1)

                def tile(t):
                    first = isinstance(t, int) and t == 0

                    def tail(*steps):
                        for step in steps:
                            if not first:
                                if step == 2 and isinstance(t, int):
                                    pe.wait_ge(weights, 48)
                                tail_pe(pe, T, t - 1, P, step)

                    pe.wait_ge(swa_in, 48 * (t + 1))
                    wait(pe, pT_ready, 8 * t)
                    wait(pe, T.oa_ready, t)
                    for i in range(SWA_HEADS // 2):
                        wait(pe, s_taken, 8 * t + i - 1)
                        for j in range(2):
                            half = j * HD
                            last = pe.matmul(score_pair(i, j), sq[half:half + HD, i, :],
                                             kk[half:half + HD, 2 * i // GROUP, :, :].rearrange("d a n -> d (a n)"),
                                             start=True, stop=True)
                        last.then_inc(s_done, 1)
                        tail(*{1: (0, 1), 3: (2,), 5: (3,)}.get(i, ()))
                    tail(4)
                    pe.wait_ge(gla_in, 64 * (t + 1))
                    pe.wait_ge(s_taken, 8 * (t + 1))
                    wait(pe, T.obT_ready, t)
                    for h, steps in enumerate(((5,), (6, 7), (8,), (9,))):
                        gla_scores(t, h)
                        tail(*steps)
                        gla_out(t, h)
                    pe.wait_ge(p_ready, t + 1)
                    pe.wait_ge(vv_in, 16 * (t + 1))
                    pe.wait_ge(S_ready, GLA_HEADS * (t + 1))
                    for i in range(SWA_HEADS // 2 + 1):
                        if i < SWA_HEADS // 2:
                            wait(pe, pT_ready, 8 * t + i - 1)
                            for j in range(4):
                                last = pe.transpose(X[:, (i % 2) * BANK + j * P:(i % 2) * BANK + (j + 1) * P],
                                                    s[:, 2 * i + j // 2, (j % 2) * P:(j % 2 + 1) * P], ident[:, :])
                            last.then_inc(pT_ps, 1)
                        if i:
                            i -= 1
                            pe.wait_ge(pT_ready, 8 * t + i + 1)
                            g = 2 * i // GROUP
                            for j in range(2):
                                for a in range(2):
                                    last = pe.matmul(U[j * HD:(j + 1) * HD, i * P:(i + 1) * P], vv[:, a, g * HD:(g + 1) * HD],
                                                     pT[:, i % 2, 2 * j + a, :], start=(a == 0), stop=(a == 1))
                    last.then_inc(T.ob_done, 1)

                tile(0)
                tile(1)
                with pe.Fori(2, TILES) as t:
                    tile(t)
                for step in range(TAIL):
                    tail_pe(pe, T, TILES - 1, P, step)


        with ExitStack() as ctx:
            def sb(name, shape, dt=F32):
                return ctx.enter_context(nc.sbuf_tensor(name, shape, dt))

            N = NSAMP
            KEYS = WINDOW + STEPS
            T = Tail(sb, sem, "n_")
            q = sb("n_q", [P, GLA_HEADS, N])
            k = sb("n_k", [P, GLA_HEADS, N])
            b = sb("n_b", [P, GLA_HEADS, N])
            v = sb("n_v", [P, D])
            sq = sb("n_sq", [HD, SWA_HEADS, N])
            sq_seq = sb("n_sq_seq", [HD, SEQS, SWA_HEADS, STEPS])
            kk = sb("n_kk", [HD, SEQS, KV_HEADS, KEYS])
            vv = sb("n_vv", [P, SEQS, KV])
            v_new = sb("n_vnew", [STEPS, SEQS, KV])
            mask = sb("n_mask", [P, KEYS])
            causal = sb("n_causal", [N, N])
            seg_cols = sb("n_seg_cols", [P, SEQS, N])
            seg_rows = sb("n_seg_rows", [N, SEQS])
            sink = sb("n_sink", [P, 1])
            st = sb("n_st", [P, SEQS, DV])
            kt = sb("n_kt", [P, N])
            qt = sb("n_qt", [P, N])
            kp = sb("n_kp", [P, N])
            last_e = sb("n_last_e", [P, SEQS])
            qm = sb("n_qm", [P, SEQS, N])
            kpm = sb("n_kpm", [N, SEQS, P])
            scm = sb("n_scm", [N, N])
            s = sb("n_s", [P, SEQS, KEYS])
            m = sb("n_m", [P, 4, SEQS])
            e_sum = sb("n_e_sum", [P, SEQS])
            pT = sb("n_pT", [P, SEQS, P])
            pT_new = sb("n_pT_new", [STEPS, SEQS, P])

            ins = sem("n_ins")
            sq_ready = sem("n_sq_ready")
            st_in = sem("n_st_in")
            st_out = sem("n_st_out")
            ex_in = sem("n_ex_in")
            ex_done = sem("n_ex_done")
            kq_ready = sem("n_kq_ready")
            sc_done = sem("n_sc_done")
            m_ready = sem("n_scm_ready")
            su_done = sem("n_su_done")
            st_ready = sem("n_st_ready")
            s_done = sem("n_s_done")
            neg_ready = sem("n_neg_ready")
            e_done = sem("n_e_done")
            p_ready = sem("n_p_ready")
            pT_ps = sem("n_pT_ps")
            pT_ready = sem("n_pT_ready")
            vstep = sem("n_vstep")
            astep = sem("n_astep")
            block = ctx.enter_context(nc.Block())
            PER_BANK = BANK // KEYS

            def score_place(seq):
                bank, at = seq // PER_BANK, (seq % PER_BANK) * KEYS
                tensor, base = ((X, 0), (X, BANK), (U, 0))[bank]
                return tensor, base + at

            @block.sync
            def _(sp):
                cols = slice(SEQ, TOK)
                for dst, src in ((b, z_b[:, :, cols]), (k, z_feat[4:8, :, cols]), (q, z_feat[0:4, :, cols])):
                    sp.dma_start(dst[:, :, :], src.rearrange("h p n -> p h n")).then_inc(ins, 16)
                sp.dma_start(v[0:N, :], z_tok[cols, 0:D]).then_inc(ins, 16)
                for half in range(2):
                    sp.dma_start(sq[:, half:SWA_HEADS:2, :],
                                 z_feat[8:16, half * HD:(half + 1) * HD, cols].rearrange("c d n -> d c n")).then_inc(ins, 16)
                for g in range(KV_HEADS):
                    sp.dma_start(kk[:, :, g, 0:WINDOW], cache_kT_dram[:, :, g, :]).then_inc(ins, 16)
                    sp.dma_start(kk[:, :, g, WINDOW:KEYS],
                                 z_kT[g * HD:(g + 1) * HD, cols].rearrange("d (b s) -> d b s", s=STEPS)).then_inc(ins, 16)
                sp.dma_start(vv[:, :, :], cache_v_dram).then_inc(ins, 16)
                sp.dma_start(v_new[:, :, :], z_kv[cols, KV:2 * KV].rearrange("(b s) c -> s b c", s=STEPS)).then_inc(ins, 16)
                for dst, src in ((mask[:, :], samp_mask_dram), (causal[:, :], samp_causal_dram),
                                 (seg_cols[:, :, :], seg_cols_dram), (seg_rows[:, :], seg_rows_dram),
                                 (sink[:, :], sink_rows_dram)):
                    sp.dma_start(dst, src).then_inc(ins, 16)
                load_vgate(sp, T, cols, N)
                load_gates(sp, T, cols, N)
                for h in range(GLA_HEADS):
                    wait(sp, st_out, 16 * h)
                    sp.dma_start(st[:, :, :], state_dram[:, h, :, :].rearrange("b d e -> d b e")).then_inc(st_in, 16)
                    sp.wait_ge(st_ready, SEQS * (h + 1))
                    sp.dma_start(ss_dram[:, h, :, :].rearrange("b d e -> d b e"), st[:, :, :]).then_inc(st_out, 16)
                sp.wait_ge(T.r_taken, TAIL)
                for start in (SEQ, TOK):
                    sp.dma_start(h_dram[start:start + N, :], T.h[0:N, :]).then_inc(T.h_stored, 16)
                sp.wait_ge(T.h_stored, 32)
                sp.wait_ge(st_out, 16 * GLA_HEADS)

            @block.gpsimd
            def _(pool):
                pool.wait_ge(ins, 16 * 17)
                pool.tensor_copy(sq_seq[:, :, :, :], sq[:, :, :].rearrange("d h (b s) -> d b h s", s=STEPS)).then_inc(sq_ready, 1)
                gate_norm(pool, T, 0, N)

            @block.scalar
            def _(act):
                chain = Chain(act, astep)
                for h in range(GLA_HEADS):
                    act.wait_ge(ex_in, h + 1)
                    wait(act, T.o_done, h)
                    chain.step(act.activation(kt[:, :], kt[:, :], ACT.Exp, scale=-1.0))
                    chain.step(act.activation(qt[:, :], b[:, h, :], ACT.Exp))
                    chain.step(act.activation(kp[:, :], kp[:, :], ACT.Exp))
                    act.activation(last_e[:, :], b[:, h, STEPS - 1:N:STEPS], ACT.Exp).then_inc(ex_done, 1)
                act.wait_ge(neg_ready, 1)
                for seq in range(SEQS):
                    chain.step(act.activation(s[:, seq, :], s[:, seq, :], ACT.Exp, bias=m[:, 1, seq:seq + 1],
                                              accum_out=e_sum[:, seq:seq + 1]))
                act.activation(m[:, 2, :], m[:, 2, :], ACT.Exp).then_inc(e_done, 1)
                tail_norm_act(act, T, 0, N)
                for seq in range(SEQS):
                    r = seq % 2
                    act.wait_ge(pT_ps, seq + 1)
                    chain.step(act.activation(pT[:, seq, :], R[:, r, 0:P], ACT.Copy))
                    act.activation(pT_new[:, seq, :], R[0:STEPS, r, P:2 * P], ACT.Copy).then_inc(pT_ready, 1)
                tail_act(act, T, 0, N)

            @block.vector
            def _(dve):
                chain = Chain(dve, vstep)
                dve.wait_ge(ins, 16 * 17)
                for h in range(GLA_HEADS):
                    blocks = b[:, h, :].rearrange("p (s i) -> p s i", s=SEQS)
                    wait(dve, sc_done, h)
                    chain.step(dve.tensor_scalar(kt[:, :], b[:, h, :], -CLAMP, None, ALU.max))
                    dve.tensor_tensor(kp[:, :].rearrange("p (s i) -> p s i", s=SEQS),
                                      blocks[:, :, STEPS - 1:STEPS].to_broadcast([P, SEQS, STEPS]), blocks,
                                      ALU.subtract).then_inc(ex_in, 1)
                    dve.wait_ge(ex_done, h + 1)
                    chain.step(dve.tensor_tensor(kt[:, :], kt[:, :], k[:, h, :], ALU.mult))
                    chain.step(dve.tensor_tensor(kp[:, :], kp[:, :], k[:, h, :], ALU.mult))
                    chain.link(dve.scalar_tensor_tensor(out=qt[:, :], in0=q[:, h, :], scalar=QSCALE, in1=qt[:, :],
                                                        op0=ALU.mult, op1=ALU.mult))
                    dve.tensor_tensor(qm[:, :, :], qt[:, :].unsqueeze(1).to_broadcast([P, SEQS, N]), seg_cols[:, :, :],
                                      ALU.mult).then_inc(kq_ready, 1)
                    dve.wait_ge(sc_done, h + 1)
                    wait(dve, su_done, SEQS * h)
                    chain.step(dve.tensor_tensor(scm[:, :], R[0:N, 0, 0:N], causal[:, :], ALU.mult))
                    dve.tensor_tensor(kpm[:, :, :], R[0:N, 1, 0:P].unsqueeze(1).to_broadcast([N, SEQS, P]),
                                      seg_rows[:, :].unsqueeze(2).to_broadcast([N, SEQS, P]), ALU.mult).then_inc(m_ready, 1)
                    dve.wait_ge(T.o_done, h + 1)
                    for seq in range(SEQS):
                        dve.wait_ge(su_done, SEQS * h + seq + 1)
                        at = (seq % 2) * BANK
                        dve.scalar_tensor_tensor(out=st[:, seq, :], in0=st[:, seq, :], scalar=last_e[:, seq:seq + 1],
                                                 in1=U[:, at:at + DV], op0=ALU.mult, op1=ALU.add).then_inc(st_ready, 1)
                dve.wait_ge(s_done, 1)
                for seq in range(SEQS):
                    tensor, at = score_place(seq)
                    chain.step(dve.tensor_tensor_reduce(s[:, seq, :], tensor[:, at:at + KEYS], mask[:, :], HD ** -0.5, sink[:, :],
                                                        ALU.add, ALU.max, m[:, 0, seq:seq + 1]))
                chain.settle()
                chain.step(dve.tensor_scalar(m[:, 1, :], m[:, 0, :], -1.0, None, ALU.mult))
                dve.tensor_tensor(m[:, 2, :], sink[:, :].to_broadcast([P, SEQS]), m[:, 0, :], ALU.subtract).then_inc(neg_ready, 1)
                dve.wait_ge(e_done, 1)
                chain.link(dve.tensor_tensor(m[:, 3, :], e_sum[:, :], m[:, 2, :], ALU.add))
                chain.link(dve.reciprocal(m[:, 3, :], m[:, 3, :]))
                dve.tensor_tensor(s[:, :, :], s[:, :, :], m[:, 3, :].unsqueeze(2).to_broadcast([P, SEQS, KEYS]),
                                  ALU.mult).then_inc(p_ready, 1)
                tail_oa_dve(dve, chain, T, 0, N)
                for step in range(TAIL):
                    tail_dve(dve, chain, T, 0, N, step)

            @block.tensor
            def _(pe):
                for h in range(GLA_HEADS):
                    vh = v[0:N, h * DV:(h + 1) * DV]
                    pe.wait_ge(kq_ready, h + 1)
                    wait(pe, m_ready, h)
                    pe.matmul(R[0:N, 0, 0:N], kt[:, :], qt[:, :], start=True, stop=True)
                    pe.transpose(R[0:N, 1, 0:P], kp[:, :], ident[:, :]).then_inc(sc_done, 1)
                    pe.wait_ge(m_ready, h + 1)
                    pe.wait_ge(st_in, 16 * (h + 1))
                    pe.matmul(O[0:N, h * DV:(h + 1) * DV], scm[:, :], vh, start=True, stop=False)
                    for seq in range(SEQS):
                        last = pe.matmul(O[0:N, h * DV:(h + 1) * DV], qm[:, seq, :], st[:, seq, :],
                                         start=False, stop=(seq == SEQS - 1))
                    last.then_inc(T.o_done, 1)
                    for seq in range(SEQS):
                        at = (seq % 2) * BANK
                        wait(pe, st_ready, SEQS * h + seq - 1)
                        pe.matmul(U[:, at:at + DV], kpm[:, seq, :], vh, start=True, stop=True).then_inc(su_done, 1)
                pe.wait_ge(st_ready, SEQS * GLA_HEADS)
                pe.wait_ge(sq_ready, 1)
                for seq in range(SEQS):
                    tensor, at = score_place(seq)
                    for g in range(KV_HEADS):
                        last = pe.matmul(tensor[g * HD:(g + 1) * HD, at:at + KEYS],
                                         sq_seq[:, seq, g * GROUP:(g + 1) * GROUP, :].rearrange("d h s -> d (h s)"),
                                         kk[:, seq, g, :], start=True, stop=True)
                last.then_inc(s_done, 1)
                pe.wait_ge(p_ready, 1)
                for seq in range(SEQS):
                    r = seq % 2
                    wait(pe, pT_ready, seq - 1)
                    pe.transpose(R[:, r, 0:P], s[:, seq, 0:WINDOW], ident[:, :])
                    pe.transpose(R[0:STEPS, r, P:2 * P], s[:, seq, WINDOW:KEYS], ident[:, :]).then_inc(pT_ps, 1)
                    pe.wait_ge(pT_ready, seq + 1)
                    for g in range(KV_HEADS):
                        for j in range(2):
                            rows = lambda t: t[:, seq, g * HD:(g + 1) * HD].rearrange("k (h s) -> k h s", s=STEPS)[:, j:GROUP:2, :]
                            out = U[j * HD:(j + 1) * HD, 0:KT * N].rearrange("d (c n) -> d c n", c=KT)[
                                :, g * (GROUP // 2):(g + 1) * (GROUP // 2), seq * STEPS:(seq + 1) * STEPS]
                            pe.matmul(out, vv[:, seq, g * HD:(g + 1) * HD], rows(pT), start=True, stop=False)
                            last = pe.matmul(out, v_new[:, seq, g * HD:(g + 1) * HD], rows(pT_new), start=False, stop=True)
                last.then_inc(T.ob_done, 1)
                for step in range(TAIL):
                    tail_pe(pe, T, 0, N, step)


def peer_stage(nc, sem, h_dram, wq_dram, keys_dram, u_dram, v_dram, g_ffn_dram, g_final_dram, y_dram):
    RING = 8
    IDX = 4
    WQ_PARTS = 2
    with ExitStack() as ctx:
        def sb(name, shape, dt=F32):
            return ctx.enter_context(nc.sbuf_tensor(name, shape, dt))

        def pb(name, shape):
            return ctx.enter_context(nc.psum_tensor(name, shape, F32))

        wq = sb("e_wq", [P, KT, QD])
        keys = sb("e_keys", [P, 2 * HEADS, NKEYS])
        g_ffn = sb("e_g_ffn", [P, D])
        g_final = sb("e_g_final", [P, D])
        ident = sb("e_ident", [P, P])
        ident_pair = sb("e_ident_pair", [P, NSAMP])
        iota16 = sb("e_iota16", [P, TOPK])
        u_rows = sb("e_u_rows", [P, RING, D])
        v_rows = sb("e_v_rows", [P, RING, D])
        h_next = sb("e_h_next", [P, D])
        xn_next = sb("e_xn_next", [P, D])
        xn = sb("e_xn", [P, D])
        xnT = sb("e_xnT", [P, KT, P])
        h_out = sb("e_h_out", [P, D])
        acc = sb("e_acc", [P, D])
        y = sb("e_y", [P, D])
        q_sb = sb("e_q_sb", [P, 2, P])
        s_sb = sb("e_s_sb", [P, 2, NKEYS])
        s_rest = sb("e_s_rest", [P, 2, NKEYS])
        top_val = sb("e_top_val", [P, 2, TOPK])
        top_idx = sb("e_top_idx", [P, 2, TOPK], U32)
        top_idxf = sb("e_top_idxf", [P, 2, TOPK])
        cand = sb("e_cand", [P, TOPK, TOPK])
        cand_rest = sb("e_cand_rest", [P, TOPK, TOPK])
        best = sb("e_best", [P, IDX, TOPK])
        pos = sb("e_pos", [P, TOPK], U32)
        pos_ab = sb("e_pos_ab", [P, 2, TOPK], U32)
        pos_abf = sb("e_pos_abf", [P, 2, TOPK])
        hot = sb("e_hot", [P, 2, TOPK, TOPK])
        picked = sb("e_picked", [P, 2, TOPK])
        expert = sb("e_expert", [P, IDX, TOPK], U32)
        expert_pair = sb("e_expert_pair", [P, IDX, TOPK // 2], U32)
        neg_best = sb("e_neg_best", [P, IDX])
        e_top = sb("e_e_top", [P, IDX, TOPK])
        e_sum = sb("e_e_sum", [P, IDX])
        e_rec = sb("e_e_rec", [P, IDX])
        dots = sb("e_dots", [P, 2, TOPK])
        gelus = sb("e_gelus", [P, 2, TOPK])
        weight = sb("e_weight", [P, 2, TOPK])
        diag = sb("e_diag", [P, TOPK, P])
        stat = sb("e_stat", [P, 8])
        q_ps = pb("e_q_ps", [P, 2, P])
        s_ps = pb("e_s_ps", [P, 2, NKEYS])
        t_ps = [pb(f"e_t_ps{i}", [P, 4, P]) for i in range(2)]
        o_ps = pb("e_o_ps", [P, D])

        norm_in = sem("e_norm_in")
        keys_in = sem("e_keys_in")
        wq_in = [sem(f"e_wq_in{i}") for i in range(WQ_PARTS)]
        consts = sem("e_consts")
        made = sem("e_made")
        h_loaded = sem("e_h_loaded")
        h_again = sem("e_h_again")
        sq_done = sem("e_sq_done")
        rt_in = sem("e_rt_in")
        rt_done = sem("e_rt_done")
        xn_ready = sem("e_xn_ready")
        xnT_ps = sem("e_xnT_ps")
        xnT_ready = sem("e_xnT_ready")
        q_done = sem("e_q_done")
        q_ready = sem("e_q_ready")
        s_done = sem("e_s_done")
        s_taken = sem("e_s_taken")
        picked_ready = sem("e_picked_ready")
        paired = sem("e_paired")
        e_done = sem("e_e_done")
        u_got = [sem(f"e_u_got{i}") for i in range(RING)]
        v_got = [sem(f"e_v_got{i}") for i in range(RING)]
        u_used = sem("e_u_used")
        v_used = sem("e_v_used")
        gelu_done = sem("e_gelu_done")
        w_ready = sem("e_w_ready")
        diag_ready = sem("e_diag_ready")
        acc_ready = sem("e_acc_ready")
        out_sq = sem("e_out_sq")
        out_rt = sem("e_out_rt")
        y_ready = sem("e_y_ready")
        y_stored = sem("e_y_stored")
        vstep = sem("e_vstep")
        tick = sem("e_tick")
        pstep = sem("e_pstep")
        block = ctx.enter_context(nc.Block())
        LAST = TILES

        def rows(t):
            return NSAMP if isinstance(t, int) and t == LAST else P

        def slots(t, h=0):
            return TOPK // 2 if isinstance(t, int) and t == LAST and h >= 0 else TOPK

        def slots_before(unit):
            if isinstance(unit, int) and unit > LAST * HEADS:
                return LAST * HEADS * TOPK + (unit - LAST * HEADS) * (TOPK // 2)
            return unit * TOPK

        def rounds(unit, k):
            if isinstance(unit, int):
                return slots_before(unit) // RING + k // RING + 1
            return unit * (TOPK // RING) + k // RING + 1

        @block.sync
        def _(sp):

            def load_next(t):
                wait(sp, xn_ready, t)
                wait(sp, sq_done, t)
                sp.dma_start(h_next[:, :], h_dram[bass.ds(t * P, P), :]).then_inc(h_loaded, 16)

            def load_again(t):
                wait(sp, out_sq, t)
                sp.dma_start(h_out[0:rows(t), :], h_dram[bass.ds(t * P, rows(t)), :]).then_inc(h_again, 16)

            def store(t):
                sp.wait_ge(y_ready, t + 1)
                sp.dma_start(y_dram[bass.ds(t * P, rows(t)), :], y[0:rows(t), :]).then_inc(y_stored, 16)

            load_next(0)
            sp.dma_start(g_ffn[:, :], g_ffn_dram.to_broadcast([P, D])).then_inc(norm_in, 16)
            part = QD // WQ_PARTS
            for i in range(WQ_PARTS):
                sp.dma_start(wq[:, :, i * part:(i + 1) * part], wq_dram[:, :, i * part:(i + 1) * part]).then_inc(wq_in[i], 16)
                if i == 0:
                    sp.dma_start(keys[:, :, :], keys_dram).then_inc(keys_in, 16)
            sp.dma_start(g_final[:, :], g_final_dram.to_broadcast([P, D])).then_inc(consts, 16)

            def tile(t):
                if not (isinstance(t, int) and t == LAST):
                    load_next(t + 1)
                if not (isinstance(t, int) and t == 0):
                    store(t - 1)
                load_again(t)

            tile(0)
            with sp.Fori(1, LAST) as t:
                tile(t)
            tile(LAST)
            store(LAST)
            sp.wait_ge(y_stored, 16 * (LAST + 1))

        @block.gpsimd
        def _(pool):
            pool.memset(ident[:, :], 0.0).then_inc(pstep, 1)
            pool.wait_ge(pstep, 1)
            pool.affine_select(out=ident[:, :], in_=ident[:, :], compare_op=ALU.not_equal, fill=1.0,
                               base=0, pattern=[[-1, P]], channel_multiplier=1).then_inc(made, 1)
            pool.memset(ident_pair[:, :], 0.0).then_inc(pstep, 1)
            for i in range(2):
                pool.wait_ge(pstep, 2 + i)
                pool.affine_select(out=ident_pair[:, :], in_=ident_pair[:, :], compare_op=ALU.not_equal, fill=1.0,
                                   base=-i * NSAMP, pattern=[[-1, NSAMP]], channel_multiplier=1
                                   ).then_inc(made if i else pstep, 1)
            pool.iota(iota16[:, :], [[1, TOPK]], base=0, channel_multiplier=0,
                      allow_small_or_imprecise_dtypes=True).then_inc(made, 1)

            def gather(table, ring, got, used, t, h, k):
                wait_alone(pool, used, slots_before(t * HEADS + h) + k - RING + 1, tick)
                index = expert if slots(t, h) == TOPK else expert_pair
                pool.indirect_dma_start(ring[:, k % RING, :], None, table,
                                        bass.IndirectOffsetOnAxis(ap=index[:, h % IDX, k:k + 1], axis=0)
                                        ).then_inc(got[k % RING], 16)

            def u_gather(t, h, k):
                gather(u_dram, u_rows, u_got, u_used, t, h, k)

            def v_gather(t, h, k):
                gather(v_dram, v_rows, v_got, v_used, t, h, k)

            def tile(t):
                for h in range(HEADS):
                    early = 0
                    if slots(t) == TOPK:
                        wait_alone(pool, picked_ready, t * HEADS + h + 1, tick)
                    else:
                        if h == 0:
                            early = TOPK // 2
                            for k in range(early):
                                v_gather(t, -1, k)
                        pool.wait_ge(paired, h + 1)
                    for k in range(TOPK):
                        if k < slots(t):
                            u_gather(t, h, k)
                        if early + k < slots(t, h - 1) and not (isinstance(t, int) and t == 0 and h == 0):
                            v_gather(t, h - 1, early + k)

            tile(0)
            with pool.Fori(1, LAST) as t:
                tile(t)
            tile(LAST)
            for k in range(slots(LAST)):
                v_gather(LAST, HEADS - 1, k)

        @block.scalar
        def _(act):
            def norm(t):
                act.wait_ge(h_loaded, 16 * (t + 1))
                wait(act, xnT_ps, 2 * t)
                wait(act, xn_ready, t)
                act.activation(xn_next[:, :], h_next[:, :], ACT.Square, accum_out=stat[:, 0:1]).then_inc(sq_done, 1)
                act.wait_ge(rt_in, t + 1)
                act.activation(stat[:, 2:3], stat[:, 1:2], ACT.Sqrt).then_inc(rt_done, 1)
                for i in range(2):
                    act.wait_ge(xnT_ps, 2 * t + i + 1)
                    act.activation(xnT[:, 4 * i:4 * i + 4, :], t_ps[i][:, :, :], ACT.Copy).then_inc(xnT_ready, 1)

            def queries(unit):
                act.wait_ge(q_done, unit + 1)
                wait(act, s_done, unit)
                act.activation(q_sb[:, :, :], q_ps[:, :, :], ACT.Copy).then_inc(q_ready, 1)

            def exponentials(unit, h):
                b = h % IDX
                act.wait_ge(picked_ready, unit + 1)
                act.activation(e_top[:, b, :], best[:, b, :], ACT.Exp, bias=neg_best[:, b:b + 1],
                               accum_out=e_sum[:, b:b + 1]).then_inc(e_done, 1)

            def gelu(t, h):
                unit, n = t * HEADS + h, slots(t, h)
                act.wait_ge(u_used, slots_before(unit + 1))
                wait(act, w_ready, unit - 1)
                act.activation(gelus[:, h % 2, 0:n], dots[:, h % 2, 0:n], ACT.Gelu).then_inc(gelu_done, 1)

            def diagonals(t, h):
                unit = t * HEADS + h
                act.wait_ge(w_ready, unit + 1)
                eye = ident if slots(t, h) == TOPK else ident_pair
                for k in range(slots(t, h)):
                    wait(act, v_used, slots_before(unit - 1) + k + 1)
                    act.activation(diag[:, k, 0:eye.shape[1]], eye[:, :], ACT.Copy,
                                   scale=weight[:, h % 2, k:k + 1]).then_inc(diag_ready, 1)

            def evacuate(t):
                act.wait_ge(v_used, slots_before((t + 1) * HEADS))
                wait(act, out_sq, t)
                act.activation(acc[0:rows(t), :], o_ps[0:rows(t), :], ACT.Copy).then_inc(acc_ready, 1)

            def out_root(t):
                act.wait_ge(out_sq, t + 1)
                act.activation(stat[0:rows(t), 6:7], stat[0:rows(t), 5:6], ACT.Sqrt).then_inc(out_rt, 1)

            act.wait_ge(made, 3)
            norm(0)
            queries(0)
            queries(1)
            exponentials(0, 0)
            exponentials(1, 1)

            def tile(t):
                first = isinstance(t, int) and t == 0
                last = isinstance(t, int) and t == LAST
                for h in range(HEADS):
                    unit = t * HEADS + h
                    if h == HEADS - 2 and not last:
                        norm(t + 1)
                    if h < HEADS - 2 or not last:
                        queries(unit + 2)
                    if not (first and h == 0):
                        diagonals(t, h - 1)
                    gelu(t, h)
                    if h < HEADS - 2 or not last:
                        exponentials(unit + 2, (h + 2) % HEADS)
                    if h == 0 and not first:
                        evacuate(t - 1)
                    if h == 1 and not first:
                        out_root(t - 1)

            tile(0)
            with act.Fori(1, LAST) as t:
                tile(t)
            tile(LAST)
            diagonals(LAST, HEADS - 1)
            evacuate(LAST)
            out_root(LAST)

        @block.vector
        def _(dve):
            chain = Chain(dve, vstep)

            def norm(t):
                dve.wait_ge(sq_done, t + 1)
                dve.tensor_scalar(stat[:, 1:2], stat[:, 0:1], 1.0 / D, EPS, ALU.mult, ALU.add).then_inc(rt_in, 1)
                dve.wait_ge(rt_done, t + 1)
                chain.link(dve.reciprocal(stat[:, 3:4], stat[:, 2:3]))
                dve.scalar_tensor_tensor(out=xn_next[:, :], in0=h_next[:, :], scalar=stat[:, 3:4],
                                         in1=g_ffn[:, :], op0=ALU.mult, op1=ALU.mult).then_inc(xn_ready, 1)

            def take(t):
                dve.wait_ge(xn_ready, t + 1)
                wait(dve, u_used, t * HEADS * TOPK)
                chain.link(dve.tensor_copy(xn[:, :], xn_next[:, :]))

            def top16(values, indices, source, rest):
                chain.link(dve.max(values[:, 0:8], source))
                chain.step(dve.max_index(indices[:, 0:8], values[:, 0:8], source))
                chain.link(dve.match_replace(rest, values[:, 0:8], source, LOWEST))
                chain.link(dve.max(values[:, 8:16], rest))
                chain.step(dve.max_index(indices[:, 8:16], values[:, 8:16], rest))

            def select(unit, h):
                b = h % IDX
                dve.wait_ge(s_done, unit + 1)
                dve.tensor_copy(s_sb[:, :, :], s_ps[:, :, :]).then_inc(s_taken, 1)
                dve.wait_ge(s_taken, unit + 1)
                wait(dve, v_used, slots_before(unit - IDX + 1))
                chain.step(dve.tensor_copy(stat[:, 7:8], stat[:, 3:4]))
                for half in range(2):
                    top16(top_val[:, half, :], top_idx[:, half, :], s_sb[:, half, :], s_rest[:, half, :])
                chain.settle()
                chain.step(dve.tensor_copy(top_idxf[:, :, :], top_idx[:, :, :]))
                chain.link(dve.tensor_tensor(cand[:, :, :],
                                             top_val[:, 0, :].unsqueeze(2).to_broadcast([P, TOPK, TOPK]),
                                             top_val[:, 1, :].unsqueeze(1).to_broadcast([P, TOPK, TOPK]), ALU.add))
                flat = cand[:, :, :].rearrange("p a b -> p (a b)")
                rest = cand_rest[:, :, :].rearrange("p a b -> p (a b)")
                top16(best[:, b, :], pos[:, :], flat, rest)
                chain.settle()
                chain.step(dve.tensor_scalar(pos_ab[:, 0, :], pos[:, :], 4, None, ALU.logical_shift_right))
                chain.step(dve.tensor_scalar(pos_ab[:, 1, :], pos[:, :], TOPK - 1, None, ALU.bitwise_and))
                chain.link(dve.tensor_scalar(neg_best[:, b:b + 1], best[:, b, 0:1], -1.0, None, ALU.mult))
                chain.link(dve.tensor_copy(pos_abf[:, :, :], pos_ab[:, :, :]))
                chain.link(dve.tensor_tensor(
                    hot[:, :, :, :].rearrange("p s a b -> p (s a) b"),
                    pos_abf[:, :, :].rearrange("p s a -> p (s a)").unsqueeze(2).to_broadcast([P, 2 * TOPK, TOPK]),
                    iota16[:, :].unsqueeze(1).to_broadcast([P, 2 * TOPK, TOPK]), ALU.is_equal))
                chain.link(dve.tensor_tensor(hot[:, :, :, :], hot[:, :, :, :],
                                             top_idxf[:, :, :].unsqueeze(2).to_broadcast([P, 2, TOPK, TOPK]), ALU.mult))
                chain.link(dve.tensor_reduce(picked[:, :, :], hot[:, :, :, :], AX_X, ALU.add))
                dve.scalar_tensor_tensor(out=expert[:, b, :], in0=picked[:, 0, :], scalar=float(NKEYS),
                                         in1=picked[:, 1, :], op0=ALU.mult, op1=ALU.add).then_inc(picked_ready, 1)

            def pair(h):
                b = h % IDX
                dve.wait_ge(picked_ready, LAST * HEADS + h + 1)
                chain.step(dve.tensor_copy(expert_pair[0:NSAMP, b, :], expert[0:NSAMP, b, 0:TOPK:2]))
                dve.tensor_copy(expert_pair[NSAMP:P, b, :], expert[NSAMP:P, b, 1:TOPK:2]).then_inc(paired, 1)

            def u_dots(t, h):
                unit = t * HEADS + h
                wait(dve, gelu_done, unit - 1)
                for k in range(slots(t, h)):
                    dve.wait_ge(u_got[k % RING], 16 * rounds(unit, k))
                    dve.tensor_tensor_reduce(u_rows[:, k % RING, :], u_rows[:, k % RING, :], xn[:, :], 1.0, 0.0,
                                             ALU.mult, ALU.add, dots[:, h % 2, k:k + 1]).then_inc(u_used, 1)

            def weights(t, h):
                unit, b = t * HEADS + h, h % IDX
                dve.wait_ge(e_done, unit + 1)
                chain.link(dve.reciprocal(e_rec[:, b:b + 1], e_sum[:, b:b + 1]))
                dve.wait_ge(gelu_done, unit + 1)
                wait(dve, diag_ready, slots_before(unit - 1))

                def product(p0, p1, first, stride, n):
                    return dve.scalar_tensor_tensor(out=weight[p0:p1, h % 2, 0:n], in0=gelus[p0:p1, h % 2, 0:n],
                                                    scalar=e_rec[p0:p1, b:b + 1], in1=e_top[p0:p1, b, first:TOPK:stride],
                                                    op0=ALU.mult, op1=ALU.mult)

                if slots(t, h) == TOPK:
                    product(0, P, 0, 1, TOPK).then_inc(w_ready, 1)
                else:
                    chain.step(product(0, NSAMP, 0, 2, TOPK // 2))
                    product(NSAMP, P, 1, 2, TOPK // 2).then_inc(w_ready, 1)

            def out_square(t):
                n = rows(t)
                dve.wait_ge(acc_ready, t + 1)
                dve.wait_ge(h_again, 16 * (t + 1))
                chain.link(dve.tensor_tensor(h_out[0:n, :], h_out[0:n, :], acc[0:n, :], ALU.add))
                wait(dve, y_stored, 16 * t)
                chain.link(dve.tensor_tensor_reduce(y[0:n, :], h_out[0:n, :], h_out[0:n, :], 1.0, 0.0,
                                                    ALU.mult, ALU.add, stat[0:n, 4:5]))
                chain.link(dve.tensor_copy(acc[0:n, :], h_out[0:n, :]))
                dve.tensor_scalar(stat[0:n, 5:6], stat[0:n, 4:5], 1.0 / D, EPS, ALU.mult, ALU.add).then_inc(out_sq, 1)

            def out_norm(t):
                n = rows(t)
                dve.wait_ge(out_rt, t + 1)
                dve.wait_ge(consts, 16)
                chain.link(dve.reciprocal(stat[0:n, 6:7], stat[0:n, 6:7]))
                dve.scalar_tensor_tensor(out=y[0:n, :], in0=acc[0:n, :], scalar=stat[0:n, 6:7],
                                         in1=g_final[0:n, :], op0=ALU.mult, op1=ALU.mult).then_inc(y_ready, 1)

            dve.wait_ge(norm_in, 16)
            dve.wait_ge(made, 3)
            norm(0)
            take(0)
            select(0, 0)
            select(1, 1)
            chain.restart()

            def tile(t):
                first = isinstance(t, int) and t == 0
                last = isinstance(t, int) and t == LAST
                if last:
                    pair(0)
                    pair(1)
                for h in range(HEADS):
                    unit = t * HEADS + h
                    if h == HEADS - 2 and not last:
                        norm(t + 1)
                    u_dots(t, h)
                    if h == HEADS - 1 and not last:
                        take(t + 1)
                    if h < HEADS - 2 or not last:
                        select(unit + 2, (h + 2) % HEADS)
                    if h < HEADS - 2 and last:
                        pair(h + 2)
                    weights(t, h)
                    if h == 1 and not first:
                        out_square(t - 1)
                    if h == 2 and not first:
                        out_norm(t - 1)
                chain.restart()

            tile(0)
            with dve.Fori(1, LAST) as t:
                tile(t)
            tile(LAST)
            out_square(LAST)
            out_norm(LAST)

        @block.tensor
        def _(pe):
            def transposes(t):
                pe.wait_ge(xn_ready, t + 1)
                for i in range(2):
                    wait(pe, xnT_ready, 2 * (t - 1) + i + 1)
                    for j in range(4):
                        k = 4 * i + j
                        last = pe.transpose(t_ps[i][:, j, :], xn_next[:, k * P:(k + 1) * P], ident[:, :])
                    last.then_inc(xnT_ps, 1)

            def queries(unit, h, t):
                if isinstance(unit, int) and unit < HEADS:
                    pe.wait_ge(wq_in[h * WQ_PARTS // HEADS], 16)
                pe.wait_ge(xnT_ready, 2 * (t + 1))
                wait(pe, q_ready, unit)
                for half in range(2):
                    j = 2 * h + half
                    for k in range(KT):
                        last = pe.matmul(q_ps[:, half, :], wq[:, k, j * P:(j + 1) * P], xnT[:, k, :],
                                         start=(k == 0), stop=(k == KT - 1))
                last.then_inc(q_done, 1)

            def scores(unit, h):
                pe.wait_ge(q_ready, unit + 1)
                if isinstance(unit, int) and unit == 0:
                    pe.wait_ge(keys_in, 16)
                wait(pe, s_taken, unit)
                for half in range(2):
                    last = pe.matmul(s_ps[:, half, :], q_sb[:, half, :], keys[:, 2 * h + half, :],
                                     start=True, stop=True)
                last.then_inc(s_done, 1)

            def v_sum(t, h, part):
                unit, count = t * HEADS + h, slots(t, h)
                n = P if count == TOPK else NSAMP
                for k in range(part * count // 2, (part + 1) * count // 2):
                    pe.wait_ge(diag_ready, slots_before(unit) + k + 1)
                    pe.wait_ge(v_got[k % RING], 16 * rounds(unit, k))
                    for c in range(D // BANK):
                        last = pe.matmul(o_ps[0:n, c * BANK:(c + 1) * BANK], diag[:, k, 0:n],
                                         v_rows[:, k % RING, c * BANK:(c + 1) * BANK],
                                         start=(h == 0 and k == 0), stop=(h % HEADS == HEADS - 1 and k == count - 1))
                    last.then_inc(v_used, 1)

            pe.wait_ge(made, 3)
            transposes(0)
            for h in range(2):
                queries(h, h, 0)
                scores(h, h)

            def tile(t):
                first = isinstance(t, int) and t == 0
                last = isinstance(t, int) and t == LAST
                for h in range(HEADS):
                    unit = t * HEADS + h
                    if h == HEADS - 2 and not last:
                        transposes(t + 1)
                    ahead = h < HEADS - 2 or not last
                    if ahead:
                        queries(unit + 2, (h + 2) % HEADS, t + (h + 2) // HEADS)
                    if not first or h:
                        if h == 1:
                            wait(pe, acc_ready, t)
                        v_sum(t, h - 1, 0)
                    if ahead:
                        scores(unit + 2, (h + 2) % HEADS)
                    if not first or h:
                        v_sum(t, h - 1, 1)

            tile(0)
            with pe.Fori(1, LAST) as t:
                tile(t)
            tile(LAST)
            for part in range(2):
                v_sum(LAST, HEADS - 1, part)


def build(nc, i, o):
    with ExitStack() as ctx:
        stages(nc, lambda name: ctx.enter_context(nc.semaphore(name)), i, o)


def stages(nc, sem, i, o):
    scratch = lambda name, shape: nc.dram_tensor(name, shape, F32, kind="Internal").ap()
    z_tok = scratch("z_tok", (TOK, 4 * D))
    z_feat = scratch("z_feat", (16, P, TOK))
    z_kv = scratch("z_kv", (TOK, 2 * KV))
    z_kT = scratch("z_kT", (KV, TOK))
    z_b = scratch("z_b", (GLA_HEADS, P, TOK))
    h = scratch("h_mid", ((TILES + 1) * P, D))
    project_stage(nc, sem, i("x"), i("g_mix"), i("w_big"), i("w_small"), i("w_decay"), i("b_decay"),
                  z_tok, z_feat, z_kv, z_kT, z_b)
    mix_stage(nc, sem, i("x"), i("wa"), i("wb"), i("wo"), i("gla_norm"), i("sinks"), i("sink_rows"), i("mask"),
              i("causal"), i("samp_mask"), i("samp_causal"), i("seg_cols"), i("seg_rows"), i("cache_kT"),
              i("cache_v"), i("cache_k_rows"), i("cache_v_rows"), i("state"), z_tok, z_feat, z_kv, z_kT, z_b, h,
              o["pk"], o["pv"], o["ps"], o["sk"], o["sv"], o["ss"])
    peer_stage(nc, sem, h, i("wq"), i("keys"), i("u"), i("v"), i("g_ffn"), i("g_final"), o["y"])


OUTPUTS = [("y", (TOK, D)), ("pk", (WINDOW, KV)), ("pv", (WINDOW, KV)), ("ps", (GLA_HEADS, DK, DV)),
           ("sk", (SEQS, WINDOW, KV)), ("sv", (SEQS, WINDOW, KV)), ("ss", (SEQS, GLA_HEADS, DK, DV))]


def kernel(**inputs):
    import numpy as np
    import concourse.bacc as bacc
    from concourse.bass_utils import run_bass_kernel_spmd as run

    a = {name: np.asarray(value) for name, value in inputs.items()}
    w_in = a["w_in"][0]

    def tiled(w):
        return w.reshape(-1, P, w.shape[1]).transpose(1, 0, 2)

    gq, gk, gv, gg, glr, sq, sk, ga, gb = 0, 512, 1024, 2048, 3072, 3088, 4112, 4368, 5392
    starts = [c + d for c in (gv, gg, ga, gb) for d in (0, CHUNK)] + [gq, gk, sq, sq + CHUNK]
    token, key = np.arange(P)[:, None], np.arange(P)[None, :]
    window = np.concatenate([np.where(key > token, 0.0, MASKED), np.where(key <= token, 0.0, MASKED)], 1)
    first = np.concatenate([np.full((P, P), MASKED), window[:, P:]], 1)
    step = np.arange(P)[:, None] % STEPS
    late = np.arange(WINDOW + STEPS)[None, :]
    samp = np.where((late > step) & (late <= WINDOW + step), 0.0, MASKED)
    row, col = np.arange(NSAMP)[:, None], np.arange(NSAMP)[None, :]
    same = row // STEPS == col // STEPS
    seg = np.arange(SEQS)[:, None] == col // STEPS
    f32 = np.float32
    arrays = {
        "x": np.concatenate([a["x_prompt"].reshape(SEQ, D), a["x_sample"].reshape(NSAMP, D)]),
        "g_mix": a["norm_mix"], "g_ffn": a["norm_ffn"], "g_final": a["norm_final"][None],
        "w_big": np.stack([tiled(w_in[:, c:c + CHUNK]).reshape(P, KT * CHUNK) for c in starts]),
        "w_small": tiled(np.concatenate([w_in[:, glr:glr + RANK], w_in[:, sk:sk + 2 * KV]], 1)),
        "w_decay": a["gla_w_decay"][0], "b_decay": a["gla_b_decay"].reshape(GLA_HEADS, DK).T,
        "wa": tiled(a["w_branch_a"][0]), "wb": tiled(a["w_branch_b"][0]), "wo": tiled(a["w_out"][0]),
        "gla_norm": a["gla_norm"], "sinks": a["swa_sinks"],
        "sink_rows": np.repeat(a["swa_sinks"][0], STEPS)[:, None],
        "mask": np.stack([first, window], 1).astype(f32), "causal": (token <= key).astype(f32),
        "samp_mask": samp.astype(f32), "samp_causal": (same & (row <= col)).astype(f32),
        "seg_cols": np.broadcast_to(seg, (P, SEQS, NSAMP)).astype(f32), "seg_rows": seg.T.astype(f32),
        "cache_kT": a["cache_win_k"][0].transpose(3, 0, 2, 1),
        "cache_v": a["cache_win_v"][0].transpose(1, 0, 2, 3).reshape(WINDOW, SEQS, KV),
        "cache_k_rows": a["cache_win_k"][0].reshape(SEQS, WINDOW, KV),
        "cache_v_rows": a["cache_win_v"][0].reshape(SEQS, WINDOW, KV),
        "state": a["state_gla"][0],
        "wq": tiled(a["peer_w_q"][0]),
        "keys": np.stack([a["peer_keys1"][0], a["peer_keys2"][0]], 1).reshape(2 * HEADS, NKEYS, HALF).transpose(2, 0, 1),
        "u": a["peer_u"][0], "v": a["peer_v"][0],
    }
    nc = bacc.Bacc("TRN2", target_bir_lowering=False, num_devices=1)
    given, feeds = {}, {}
    for name, value in arrays.items():
        feeds[f"in_{name}"] = np.ascontiguousarray(value)
        given[name] = nc.dram_tensor(f"in_{name}", value.shape, F32, kind="ExternalInput").ap()
    outs = {name: nc.dram_tensor(f"out_{name}", shape, F32, kind="ExternalOutput").ap() for name, shape in OUTPUTS}
    build(nc, given.__getitem__, outs)
    result = run(nc, [feeds], core_ids=[0]).results[0]
    r = {name: result[f"out_{name}"] for name, _ in OUTPUTS}
    win = (1, 1, WINDOW, KV_HEADS, HD)
    return (r["y"][:SEQ].reshape(1, SEQ, D), r["y"][SEQ:].reshape(SEQS, STEPS, D),
            r["pk"].reshape(win), r["pv"].reshape(win), r["ps"].reshape(1, 1, GLA_HEADS, DK, DV),
            r["sk"].reshape(1, SEQS, WINDOW, KV_HEADS, HD), r["sv"].reshape(1, SEQS, WINDOW, KV_HEADS, HD),
            r["ss"].reshape(1, SEQS, GLA_HEADS, DK, DV))
```

```python
from contextlib import ExitStack

import concourse.bass as bass
from concourse import mybir

F32 = mybir.dt.float32
F32R = mybir.dt.float32r
U32 = mybir.dt.uint32
ALU = mybir.AluOpType
ACT = mybir.ActivationFunctionType
AX_X = mybir.AxisListType.X

P = 128
D = 1024
KT = D // P
SEQ = 1024
SEQS = 8
STEPS = 8
NSAMP = SEQS * STEPS
TOK = SEQ + NSAMP
TILES = SEQ // P
BANK = 512

GLA_HEADS, DK, DV, RANK = 4, 128, 256, 16
SUB = 16
SUBS = P // SUB
CLAMP = 60.0
SWA_HEADS, KV_HEADS, HD, WINDOW = 16, 2, 64, 128
GROUP = SWA_HEADS // KV_HEADS
MASKED = -1e30

HEADS, NKEYS, HALF, TOPK = 8, 128, 128, 16
QD = HEADS * 2 * HALF
LOWEST = -3.0e38
EPS = 1e-6


def wait(eng, sem, value):
    if not isinstance(value, int) or value > 0:
        eng.wait_ge(sem, value)


def wait_alone(eng, sem, value, tick):
    if not isinstance(value, int) or value > 0:
        eng.wait_ge(sem, value)
        eng.sem_inc(tick, 1)


class Chain:

    def __init__(self, eng, sem):
        self.eng, self.sem, self.n = eng, sem, 0

    def step(self, ins):
        ins.then_inc(self.sem, 1)
        self.n += 1

    def link(self, ins):
        self.step(ins)
        self.eng.wait_ge(self.sem, self.n)

    def settle(self):
        self.eng.wait_ge(self.sem, self.n)

    def restart(self):
        if self.n:
            self.settle()
            self.eng.sem_clear(self.sem)
            self.n = 0


CHUNK = 512
GROUPS = [(0, BANK), (BANK, BANK), (2 * BANK, NSAMP)]
KV = KV_HEADS * HD
SMALL = RANK + 2 * KV
PAD = (TILES + 1) * P


def project_stage(nc, sem, x_dram, g_mix_dram, w_big_dram, w_small_dram, w_decay_dram, b_decay_dram,
                  z_tok, z_feat, z_kv, z_kT, z_b):
    SLOTS = 3
    TOK_CHUNKS, FEAT_CHUNKS = 8, 4
    NT = TILES + 1
    NF = CHUNK // P * len(GROUPS)
    NS = NT + 2 * len(GROUPS)
    USES = (NT + len(GROUPS)) // SLOTS
    with ExitStack() as ctx:
        def sb(name, shape, dt=F32):
            return ctx.enter_context(nc.sbuf_tensor(name, shape, dt))

        def pb(name, shape):
            return ctx.enter_context(nc.psum_tensor(name, shape, F32))

        xh = sb("j_xh", [P, KT, PAD], F32R)
        xl = sb("j_xl", [P, KT, PAD], F32R)
        w = sb("j_w", [P, KT * CHUNK])
        wh = sb("j_wh", [P, 2, KT * CHUNK], F32R)
        wl = sb("j_wl", [P, 2, KT * CHUNK], F32R)
        w_decay = sb("j_w_decay", [RANK, GLA_HEADS * DK])
        b_decay = sb("j_b_decay", [P, GLA_HEADS])
        room = sb("j_room", [P, 6 * D])
        x = room[:, 0:3 * D].rearrange("p (s n) -> p s n", s=3)
        xn = room[:, 3 * D:5 * D].rearrange("p (s n) -> p s n", s=2)
        g_mix = room[:, 5 * D:6 * D]
        z = room[:, 0:TOK]
        la = room[:, TOK:3 * TOK].rearrange("p (s n) -> p s n", s=2)
        low = room[0:RANK, 3 * TOK:4 * TOK]
        ident = sb("j_ident", [P, P])
        keep = sb("j_keep", [P, TOK])
        stat = sb("j_stat", [P, NT, 4])
        stage = sb("j_stage", [P, SLOTS, CHUNK])
        t_ps = [pb(f"j_t{i}", [P, 4, P]) for i in range(2)]
        m_ps = [pb(f"j_m{i}", [P, BANK]) for i in range(SLOTS)]
        z_ps = [pb(f"j_z{i}", [P, BANK]) for i in range(3)]

        consts = sem("j_consts")
        made = sem("j_made")
        x_in = [sem(f"j_x{i}") for i in range(3)]
        sq_done = sem("j_sq")
        rt_in = sem("j_rt_in")
        rt_done = sem("j_rt")
        xn_ready = sem("j_xn")
        xnT_ps = sem("j_xnT_ps")
        xh_ready = sem("j_xh_ready")
        xl_ready = sem("j_xl_ready")
        w_in = sem("j_w_in")
        wh_ready = sem("j_wh_ready")
        wl_ready = sem("j_wl_ready")
        chunk_used = sem("j_chunk_used")
        m_done = sem("j_m_done")
        staged = sem("j_staged")
        stored = [sem(f"j_stored{i}") for i in range(SLOTS)]
        z_done = sem("j_z_done")
        z_taken = sem("j_z_taken")
        abs_done = sem("j_abs")
        b_ready = sem("j_b")
        b_stored = sem("j_b_stored")
        vstep = sem("j_vstep")
        pstep = sem("j_pstep")
        tick = sem("tick")
        block = ctx.enter_context(nc.Block())

        def n_of(t):
            return NSAMP if t == TILES else P

        @block.sync
        def _(sp):
            sp.dma_start(g_mix[:, :], g_mix_dram.to_broadcast([P, D])).then_inc(consts, 16)
            sp.dma_start(w_decay[:, :], w_decay_dram).then_inc(consts, 16)
            sp.dma_start(b_decay[:, :], b_decay_dram).then_inc(consts, 16)
            for t in range(NT):
                wait(sp, xn_ready, t - 2)
                sp.dma_start(x[0:n_of(t), t % 3, :], x_dram[t * P:t * P + n_of(t), :]).then_inc(x_in[t % 3], 16)
                if t == 0:
                    sp.dma_start(w[:, 0:KT * SMALL], w_small_dram.rearrange("p k n -> p (k n)")).then_inc(w_in, 16)
            sp.wait_ge(wl_ready, 1)
            sp.dma_start(w[:, :], w_big_dram[0]).then_inc(w_in, 16)
            with sp.Fori(1, TOK_CHUNKS + FEAT_CHUNKS) as c:
                wait_alone(sp, wl_ready, c + 1, tick)
                sp.dma_start(w[:, :], w_big_dram[bass.ds(c, 1), :, :].rearrange("o p n -> p (o n)")).then_inc(w_in, 16)

        @block.gpsimd
        def _(pool):
            pool.memset(ident[:, :], 0.0).then_inc(pstep, 1)
            pool.wait_ge(pstep, 1)
            pool.affine_select(out=ident[:, :], in_=ident[:, :], compare_op=ALU.not_equal, fill=1.0,
                               base=0, pattern=[[-1, P]], channel_multiplier=1).then_inc(made, 1)
            pool.memset(keep[:, :], 1.0).then_inc(pstep, 1)
            pool.wait_ge(pstep, 2)
            pool.memset(keep[:, 0:SEQ:P], 0.0).then_inc(made, 1)
            pool.memset(keep[:, SEQ:TOK:STEPS], 0.0).then_inc(made, 1)
            for half in (xh, xl):
                pool.memset(half[:, :, TOK:PAD].bitcast(F32), 0.0).then_inc(made, 1)
            for j in range(GLA_HEADS):
                pool.wait_ge(b_ready, j + 1)
                pool.dma_start(z_b[j], la[:, 1, :]).then_inc(b_stored, 16)
            pool.wait_ge(b_stored, 16 * GLA_HEADS)

        @block.scalar
        def _(act):
            act.wait_ge(made, 5)

            def transposed(t):
                n = n_of(t)
                for i in range(2):
                    act.wait_ge(xnT_ps, 2 * t + i + 1)
                    act.activation(xh[:, 4 * i:4 * i + 4, t * P:t * P + n], t_ps[i][:, :, 0:n],
                                   ACT.Copy).then_inc(xh_ready, 1)

            def high(c, s, width=KT * CHUNK):
                act.wait_ge(w_in, 16 * (c + 1))
                wait(act, chunk_used, c - 1)
                act.activation(wh[:, s, 0:width], w[:, 0:width], ACT.Copy).then_inc(wh_ready, 1)

            def take(item, slot, use, n, width, func, dst):
                act.wait_ge(m_done, item + 1)
                wait(act, stored[slot], 16 * use)
                act.activation(stage[0:n, slot, 0:width], m_ps[slot][0:n, 0:width], func).then_inc(staged, 1)
                act.wait_ge(staged, item + 1)
                act.dma_start(dst, stage[0:n, slot, 0:width]).then_inc(stored[slot], 16)

            def keys_values(t):
                take(t, t % SLOTS, t // SLOTS, n_of(t), 2 * KV, ACT.Copy, z_kv[t * P:t * P + n_of(t), :])

            for t in range(NT):
                n = n_of(t)
                act.wait_ge(x_in[t % 3], 16 * (t // 3 + 1))
                if t >= 2:
                    act.wait_ge(xnT_ps, 2 * (t - 1))
                act.activation(xn[0:n, t % 2, :], x[0:n, t % 3, :], ACT.Square,
                               accum_out=stat[0:n, t, 0:1]).then_inc(sq_done, 1)
                act.wait_ge(rt_in, t + 1)
                act.activation(stat[0:n, t, 2:3], stat[0:n, t, 1:2], ACT.Sqrt).then_inc(rt_done, 1)
                if t:
                    transposed(t - 1)
                if t == 1:
                    high(0, 0, KT * SMALL)
                if t >= 2:
                    keys_values(t - 2)
            transposed(NT - 1)
            for t in range(NT - 2, NT):
                keys_values(t)

            def tokens(c, func):
                for t in range(NT):
                    take(NS + c * NT + t, t % SLOTS, USES + c * (NT // SLOTS) + t // SLOTS, n_of(t), CHUNK, func,
                         z_tok[t * P:t * P + n_of(t), bass.ds(c * CHUNK, CHUNK)])

            def decay(j):
                act.wait_ge(z_taken, 3 * (j + 1))
                wait(act, b_ready, j)
                act.activation(la[:, 0, :], z[:, :], ACT.Abs).then_inc(abs_done, 1)
                act.wait_ge(abs_done, 3 * j + 1)
                act.activation(la[:, 0, :], la[:, 0, :], ACT.Exp, scale=-1.0).then_inc(abs_done, 1)
                act.wait_ge(abs_done, 3 * j + 2)
                act.activation(la[:, 0, :], la[:, 0, :], ACT.Ln, bias=1.0).then_inc(abs_done, 1)

            high(1, 1)
            act.wait_ge(xn_ready, NT)
            for g, (g0, gn) in enumerate(GROUPS):
                take(NT + g, g, NT // SLOTS, P, gn, ACT.Copy, z_kT[:, g0:g0 + gn])
            for g, (g0, gn) in enumerate(GROUPS):
                act.wait_ge(m_done, NT + 3 + g + 1)
                act.activation(low[:, g0:g0 + gn], m_ps[g][0:RANK, 0:gn], ACT.Copy).then_inc(staged, 1)
            high(2, 0)
            for c in range(GLA_HEADS):
                decay(c)
                tokens(c, ACT.Copy if c < 2 else ACT.Silu)
                high(c + 3, (c + 1) % 2)
            with act.Fori(2, TOK_CHUNKS // 2) as i:
                for s in range(2):
                    tokens(2 * i + s, ACT.Sigmoid)
                    high(2 * i + s + 3, (s + 1) % 2)
            base, uses = NS + TOK_CHUNKS * NT, USES + TOK_CHUNKS * NT // SLOTS
            for c in range(FEAT_CHUNKS):
                for b in range(CHUNK // P):
                    for g, (g0, gn) in enumerate(GROUPS):
                        take(base + c * NF + b * 3 + g, g, uses + c * 4 + b, P, gn, ACT.Copy,
                             z_feat[bass.ds(c * 4 + b, 1), :, g0:g0 + gn].rearrange("o p n -> p (o n)"))
                if c + 2 < FEAT_CHUNKS:
                    high(TOK_CHUNKS + c + 3, (c + 1) % 2)
            uses += FEAT_CHUNKS * NF // SLOTS
            for slot in range(SLOTS):
                act.wait_ge(stored[slot], 16 * uses)

        @block.vector
        def _(dve):
            chain = Chain(dve, vstep)
            dve.wait_ge(consts, 48)

            def split(c, s, width=KT * CHUNK):
                dve.wait_ge(wh_ready, c + 1)
                dve.tensor_tensor(wl[:, s, 0:width], w[:, 0:width], wh[:, s, 0:width].bitcast(F32), ALU.subtract
                                  ).then_inc(wl_ready, 1)

            def low_half(t):
                n = n_of(t)
                for i in range(2):
                    dve.wait_ge(xh_ready, 2 * t + i + 1)
                    cols = slice(t * P, t * P + n)
                    dve.tensor_tensor(xl[:, 4 * i:4 * i + 4, cols], t_ps[i][:, :, 0:n],
                                      xh[:, 4 * i:4 * i + 4, cols].bitcast(F32), ALU.subtract).then_inc(xl_ready, 1)

            for t in range(NT):
                n = n_of(t)
                dve.wait_ge(sq_done, t + 1)
                dve.tensor_scalar(stat[0:n, t, 1:2], stat[0:n, t, 0:1], 1.0 / D, EPS, ALU.mult,
                                  ALU.add).then_inc(rt_in, 1)
                dve.wait_ge(rt_done, t + 1)
                chain.link(dve.reciprocal(stat[0:n, t, 3:4], stat[0:n, t, 2:3]))
                dve.scalar_tensor_tensor(out=xn[0:n, t % 2, :], in0=x[0:n, t % 3, :], scalar=stat[0:n, t, 3:4],
                                         in1=g_mix[0:n, :], op0=ALU.mult, op1=ALU.mult).then_inc(xn_ready, 1)
                if t:
                    low_half(t - 1)
                if t == 1:
                    split(0, 0, KT * SMALL)
            low_half(NT - 1)

            def shift(j):
                for g, (g0, gn) in enumerate(GROUPS):
                    dve.wait_ge(z_done, 3 * j + g + 1)
                    if g == 0 and j:
                        dve.wait_ge(b_ready, j)
                    dve.tensor_scalar(z[:, g0:g0 + gn], z_ps[g][:, 0:gn], b_decay[:, j:j + 1], None,
                                      ALU.add).then_inc(z_taken, 1)

            def decay(j):
                dve.wait_ge(abs_done, 3 * (j + 1))
                chain.link(dve.scalar_tensor_tensor(out=z[:, :], in0=z[:, :], scalar=0.0, in1=la[:, 0, :],
                                                    op0=ALU.min, op1=ALU.subtract))
                wait(dve, b_stored, 16 * j)
                chain.link(dve.tensor_tensor_scan(la[:, 1, :], keep[:, :], z[:, :], 0.0, ALU.mult, ALU.add))
                dve.tensor_scalar(la[:, 1, :], la[:, 1, :], 1.0 / 16.0, None, ALU.mult).then_inc(b_ready, 1)

            split(1, 1)
            for j in range(GLA_HEADS):
                shift(j)
                split(j + 2, j % 2)
                decay(j)
            with dve.Fori(3, (TOK_CHUNKS + FEAT_CHUNKS) // 2) as i:
                for s in range(2):
                    split(2 * i + s, s)
            split(TOK_CHUNKS + FEAT_CHUNKS, 0)

        @block.tensor
        def _(pe):
            pe.wait_ge(made, 5)
            pe.wait_ge(consts, 48)
            def product(item, slot, width, lhs, rhs):
                wait(pe, staged, item - SLOTS + 1)
                out = m_ps[slot][:, 0:width]
                for k in range(KT):
                    (lh, ll), (rh, rl) = lhs(k), rhs(k)
                    pe.matmul(out, lh, rh, start=(k == 0), stop=False)
                    pe.matmul(out, lh, rl, start=False, stop=False)
                    last = pe.matmul(out, ll, rh, start=False, stop=(k == KT - 1))
                last.then_inc(m_done, 1)

            def xn_part(start, width):
                return lambda k: [half[:, k, start:start + width] for half in (xh, xl)]

            def w_part(s, start, width, columns=CHUNK):
                return lambda k: [half[:, s, k * columns + start:k * columns + start + width] for half in (wh, wl)]

            def keys_values(t):
                pe.wait_ge(wl_ready, 1)
                pe.wait_ge(xl_ready, 2 * (t + 1))
                product(t, t % SLOTS, 2 * KV, xn_part(t * P, P), w_part(0, RANK, 2 * KV, SMALL))

            for t in range(NT):
                n = n_of(t)
                pe.wait_ge(xn_ready, t + 1)
                for i in range(2):
                    wait(pe, xl_ready, 2 * (t - 1) + i + 1)
                    for j in range(4):
                        k = 4 * i + j
                        last = pe.transpose(t_ps[i][:, j, 0:n], xn[0:n, t % 2, k * P:(k + 1) * P], ident[0:n, 0:n])
                    last.then_inc(xnT_ps, 1)
                if t:
                    keys_values(t - 1)
            keys_values(NT - 1)

            def tokens(c, s):
                pe.wait_ge(wl_ready, c + 2)
                for t in range(NT):
                    product(NS + c * NT + t, t % SLOTS, CHUNK, xn_part(t * P, P), w_part(s, 0, CHUNK))
                pe.wait_ge(m_done, NS + (c + 1) * NT)
                pe.sem_inc(chunk_used, 1)

            for g, (g0, gn) in enumerate(GROUPS):
                product(NT + g, g, gn, w_part(0, RANK, KV, SMALL), xn_part(g0, gn))
            for g, (g0, gn) in enumerate(GROUPS):
                product(NT + 3 + g, g, gn, w_part(0, 0, P, SMALL), xn_part(g0, gn))
            pe.wait_ge(m_done, NS)
            pe.sem_inc(chunk_used, 1)
            pe.wait_ge(staged, NS)
            for j in range(GLA_HEADS):
                for g, (g0, gn) in enumerate(GROUPS):
                    wait(pe, z_taken, 3 * (j - 1) + g + 1)
                    pe.matmul(z_ps[g][:, 0:gn], w_decay[:, j * DK:(j + 1) * DK], low[:, g0:g0 + gn],
                              start=True, stop=True).then_inc(z_done, 1)
                tokens(j, (j + 1) % 2)
            with pe.Fori(GLA_HEADS // 2, TOK_CHUNKS // 2) as i:
                for s in range(2):
                    tokens(2 * i + s, (s + 1) % 2)
            base = NS + TOK_CHUNKS * NT
            with pe.Fori(0, FEAT_CHUNKS // 2) as i:
                for s in range(2):
                    c = 2 * i + s
                    pe.wait_ge(wl_ready, TOK_CHUNKS + c + 2)
                    for b in range(CHUNK // P):
                        for g, (g0, gn) in enumerate(GROUPS):
                            product(base + c * NF + b * 3 + g, g, gn, w_part((s + 1) % 2, b * P, P), xn_part(g0, gn))
                    pe.wait_ge(m_done, base + (c + 1) * NF)
                    pe.sem_inc(chunk_used, 1)


class Tail:

    def __init__(self, sb, sem, name):
        self.v_gate = sb(name + "gate", [P, D])
        self.ga = sb(name + "ga", [P, D])
        self.gb = sb(name + "gb", [P, D])
        self.oa = sb(name + "oa", [P, D])
        self.oaT = sb(name + "oaT", [P, KT, P])
        self.obT = sb(name + "obT", [P, KT, P])
        self.mT = sb(name + "mT", [P, KT, P])
        self.stat = sb(name + "stat", [P, 4, GLA_HEADS])
        self.vgate_in = sem(name + "vgate_in")
        self.gates_in = sem(name + "gates_in")
        self.gate_ready = sem(name + "gate_ready")
        self.o_done = sem(name + "o_done")
        self.sq_done = sem(name + "sq_done")
        self.rt_in = sem(name + "rt_in")
        self.rt_done = sem(name + "rt_done")
        self.oa_ready = sem(name + "oa_ready")
        self.ob_done = sem(name + "ob_done")
        self.obT_ready = sem(name + "obT_ready")
        self.r_done = sem(name + "r_done")
        self.r_taken = sem(name + "r_taken")
        self.m_ready = sem(name + "m_ready")
        self.m_stored = sem(name + "m_stored")


TAIL = 8


def mix_stage(nc, sem, wa_dram, wb_dram, gla_norm_dram, sinks_dram, sink_rows_dram, mask_dram,
              causal_dram, samp_mask_dram, samp_causal_dram, seg_cols_dram, seg_rows_dram, cache_kT_dram,
              cache_v_dram, cache_k_rows, cache_v_rows, state_dram, z_tok, z_feat, z_kv, z_kT, z_b, m_dram,
              pk_dram, pv_dram, ps_dram, sk_dram, sv_dram, ss_dram):
    QSCALE = DK ** -0.5
    with ExitStack() as outer:
        def sbo(name, shape, dt=F32):
            return outer.enter_context(nc.sbuf_tensor(name, shape, dt))

        wa = sbo("wa", [P, KT, D])
        wb = sbo("wb", [P, KT, D])
        gn = sbo("gn", [P, DV])
        ident = sbo("m_ident", [P, P])
        X = outer.enter_context(nc.psum_tensor("X", [P, D], F32))
        O = outer.enter_context(nc.psum_tensor("O", [P, D], F32))
        U = outer.enter_context(nc.psum_tensor("U", [P, D], F32))
        R = outer.enter_context(nc.psum_tensor("R", [P, 2, BANK], F32))

        vstep = sem("m_vstep")
        astep = sem("m_astep")


        def tail_norm_act(act, T, t, n):
            for h in range(GLA_HEADS):
                if h == 0:
                    act.wait_ge(T.o_done, GLA_HEADS * (t + 1))
                    wait(act, T.r_done, TAIL * (t - 1) + 2)
                act.activation(T.oa[0:n, h * DV:(h + 1) * DV], O[0:n, h * DV:(h + 1) * DV], ACT.Square,
                               accum_out=T.stat[0:n, 0, h:h + 1]).then_inc(T.sq_done, 1)
            act.wait_ge(T.rt_in, t + 1)
            act.activation(T.stat[0:n, 2, :], T.stat[0:n, 1, :], ACT.Sqrt).then_inc(T.rt_done, 1)

        def tail_oa_dve(dve, chain, T, t, n):
            dve.wait_ge(T.sq_done, GLA_HEADS * (t + 1))
            dve.tensor_scalar(T.stat[0:n, 1, :], T.stat[0:n, 0, :], 1.0 / DV, EPS, ALU.mult, ALU.add).then_inc(T.rt_in, 1)
            dve.wait_ge(T.rt_done, t + 1)
            chain.link(dve.reciprocal(T.stat[0:n, 3, :], T.stat[0:n, 2, :]))
            dve.wait_ge(T.gate_ready, t + 1)
            for h in range(GLA_HEADS):
                cols = slice(h * DV, (h + 1) * DV)
                last = dve.scalar_tensor_tensor(out=T.oa[0:n, cols], in0=O[0:n, cols], scalar=T.stat[0:n, 3, h:h + 1],
                                                in1=T.v_gate[0:n, cols], op0=ALU.mult, op1=ALU.mult)
                if h < GLA_HEADS - 1:
                    chain.step(last)
            last.then_inc(T.oa_ready, 1)

        def tail_dve(dve, chain, T, t, n, step):
            kind, c = divmod(step, 2)
            cols = slice(c * BANK, (c + 1) * BANK)
            dve.wait_ge(T.r_done, TAIL * t + step + 1)
            turned = R[:, c, :].rearrange("p (k n) -> p k n", k=4)[:, :, 0:n]
            if kind == 0:
                dve.tensor_copy(T.oaT[:, 4 * c:4 * c + 4, 0:n], turned).then_inc(T.r_taken, 1)
            elif kind == 1:
                if c == 0:
                    dve.wait_ge(T.gates_in, 32 * (t + 1))
                dve.tensor_tensor(T.ga[0:n, cols], R[0:n, c, :], T.ga[0:n, cols], ALU.mult).then_inc(T.r_taken, 1)
            elif kind == 2:
                dve.tensor_tensor(T.gb[0:n, cols], R[0:n, c, :], T.gb[0:n, cols], ALU.mult).then_inc(T.r_taken, 1)
                dve.wait_ge(T.r_taken, TAIL * t + step + 1)
                dve.tensor_tensor(T.ga[0:n, cols], T.ga[0:n, cols], T.gb[0:n, cols], ALU.add).then_inc(T.m_ready, 1)
            else:
                if c == 0:
                    wait(dve, T.m_stored, 16 * t)
                dve.tensor_copy(T.mT[:, 4 * c:4 * c + 4, 0:n], turned).then_inc(T.r_taken, 1)

        def tail_act(act, T, t, n):
            act.wait_ge(T.ob_done, t + 1)
            wait(act, T.r_done, TAIL * (t - 1) + 6)
            act.activation(T.obT[:, :, 0:n], U[:, 0:KT * n].rearrange("p (k n) -> p k n", k=KT),
                           ACT.Copy).then_inc(T.obT_ready, 1)

        def tail_pe(pe, T, t, n, step):
            kind, c = divmod(step, 2)
            wait(pe, T.r_taken, TAIL * t + step - 1)
            if step == 0:
                pe.wait_ge(T.oa_ready, t + 1)
            elif kind == 1:
                pe.wait_ge(T.r_taken, TAIL * t + 2)
            elif step == 4:
                pe.wait_ge(T.obT_ready, t + 1)
            elif kind == 3:
                pe.wait_ge(T.m_ready, 2 * t + c + 1)
            if kind in (0, 3):
                src = T.oa if kind == 0 else T.ga
                for j in range(4):
                    k = 4 * c + j
                    last = pe.transpose(R[:, c, j * P:j * P + n], src[0:n, k * P:(k + 1) * P], ident[0:n, 0:n])
            else:
                lhsT, w = (T.oaT, wa) if kind == 1 else (T.obT, wb)
                for k in range(KT):
                    last = pe.matmul(R[0:n, c, :], lhsT[:, k, 0:n], w[:, k, c * BANK:(c + 1) * BANK],
                                     start=(k == 0), stop=(k == KT - 1))
            last.then_inc(T.r_done, 1)

        def load_vgate(sp, T, rows, n):
            sp.dma_start(T.v_gate[0:n, :], z_tok[rows, D:2 * D]).then_inc(T.vgate_in, 16)

        def load_gates(sp, T, rows, n):
            for i, dst in ((2, T.ga), (3, T.gb)):
                sp.dma_start(dst[0:n, :], z_tok[rows, i * D:(i + 1) * D]).then_inc(T.gates_in, 16)

        def gate_norm(pool, T, t, n):
            pool.wait_ge(T.vgate_in, 16 * (t + 1))
            pool.tensor_tensor(T.v_gate[0:n, :].rearrange("p (h e) -> p h e", h=GLA_HEADS),
                               T.v_gate[0:n, :].rearrange("p (h e) -> p h e", h=GLA_HEADS),
                               gn[0:n, :].unsqueeze(1).to_broadcast([n, GLA_HEADS, DV]), ALU.mult
                               ).then_inc(T.gate_ready, 1)


        with ExitStack() as ctx:
            def sb(name, shape, dt=F32):
                return ctx.enter_context(nc.sbuf_tensor(name, shape, dt))

            T = Tail(sb, sem, "p_")
            q = sb("q", [P, GLA_HEADS, P])
            k = sb("k", [P, GLA_HEADS, P])
            b = sb("b", [P, GLA_HEADS, P])
            v = sb("v", [P, D])
            sq = sb("sq", [P, KT, P])
            kk = sb("kk", [P, KV_HEADS, 2, P])
            vv = sb("vv", [P, 2, KV])
            mask = sb("mask", [P, 2, 2 * P])
            causal = sb("causal", [P, P])
            sinks = sb("sinks", [P, SWA_HEADS])
            rel = sb("rel", [P, 2, SUBS, P])
            qt = sb("qt", [P, 2, P])
            qb = sb("qb", [P, 2, P])
            eb = sb("eb", [P, 2, P])
            kp = sb("kp", [P, 2, P])
            kpT = sb("kpT", [P, 2, P])
            scm = sb("scm", [P, 2, P])
            S = sb("S", [P, GLA_HEADS, DV])
            s = sb("s", [P, SWA_HEADS, 2 * P])
            m = sb("m", [P, 4, SWA_HEADS])
            e_sum = sb("e_sum", [P, SWA_HEADS])
            pT = sb("pT", [P, 2, 4, P])

            consts = sem("m_consts")
            weights = sem("m_weights")
            zeroed = sem("zeroed")
            gla_in = sem("gla_in")
            swa_in = sem("swa_in")
            vv_in = sem("vv_in")
            s_done = sem("m_s_done")
            s_taken = sem("m_s_taken")
            neg_ready = sem("neg_ready")
            e_done = sem("m_e_done")
            p_ready = sem("p_ready")
            pT_ps = sem("pT_ps")
            pT_ready = sem("pT_ready")
            rel_ready = sem("rel_ready")
            ex_done = sem("ex_done")
            kq_ready = sem("kq_ready")
            sc_done = sem("sc_done")
            kpT_ready = sem("kpT_ready")
            scm_ready = sem("scm_ready")
            su_done = sem("su_done")
            S_ready = sem("S_ready")
            out_copied = sem("out_copied")
            tick = sem("tick")
            pstep = sem("m_pstep")
            block = ctx.enter_context(nc.Block())

            def score_pair(i, j):
                return (X, O)[i % 2][:, j * BANK:j * BANK + 2 * P]

            def update(h):
                at = (h % 2) * BANK + (h // 2) * DV
                return U[:, at:at + DV]

            @block.sync
            def _(sp):
                def load_gla(t):
                    wait_alone(sp, su_done, GLA_HEADS * t, tick)
                    cols = bass.ds(t * P, P)
                    for dst, src in ((b, z_b[:, :, cols]), (k, z_feat[4:8, :, cols]), (q, z_feat[0:4, :, cols])):
                        sp.dma_start(dst[:, :, :], src.rearrange("h p n -> p h n")).then_inc(gla_in, 16)
                    sp.dma_start(v[:, :], z_tok[cols, 0:D]).then_inc(gla_in, 16)

                def window(t):
                    first = isinstance(t, int) and t == 0
                    return (1, 0, P) if first else (0, t * P - P, 2 * P)

                def load_swa(t):
                    rows, (old, start, width) = bass.ds(t * P, P), window(t)
                    wait_alone(sp, s_done, 8 * t, tick)
                    sp.dma_start(sq[:, :, :], z_feat[8:16, :, rows].rearrange("h p n -> p h n")
                                 ).then_inc(swa_in, 16)
                    for half in range(2):
                        sp.dma_start(kk[half * HD:(half + 1) * HD, :, :, :].rearrange("d g a n -> d g (a n)")[:, :, old * P:],
                                     z_kT[:, bass.ds(start, width)].rearrange("(g d) n -> d g n", g=KV_HEADS)
                                     ).then_inc(swa_in, 16)

                def load_values(t):
                    old, start, width = window(t)
                    wait(sp, T.ob_done, t)
                    sp.dma_start(vv[:, old:, :], z_kv[bass.ds(start, width), KV:2 * KV].rearrange("(a p) c -> p a c", p=P)
                                 ).then_inc(vv_in, 16)

                def finish(t):
                    wait_alone(sp, T.r_taken, TAIL * (t + 1), tick)
                    sp.dma_start(m_dram[bass.ds(t, 1), :, :].rearrange("o p n -> p (o n)"),
                                 T.mT[:, :, :].rearrange("p k n -> p (k n)")).then_inc(T.m_stored, 16)

                sp.dma_start(mask[:, :, :], mask_dram).then_inc(consts, 16)
                sp.dma_start(causal[:, :], causal_dram).then_inc(consts, 16)
                sp.dma_start(sinks[:, :], sinks_dram.to_broadcast([P, SWA_HEADS])).then_inc(consts, 16)
                sp.dma_start(gn[:, :], gla_norm_dram.to_broadcast([P, DV])).then_inc(consts, 16)
                load_gla(0)
                load_swa(0)
                load_values(0)
                load_vgate(sp, T, bass.ds(0, P), P)
                load_gates(sp, T, bass.ds(0, P), P)
                for dst, src in ((wa, wa_dram), (wb, wb_dram)):
                    sp.dma_start(dst[:, :, :], src).then_inc(weights, 16)
                for dst, src in ((pk_dram, z_kv[SEQ - WINDOW:SEQ, 0:KV]), (pv_dram, z_kv[SEQ - WINDOW:SEQ, KV:2 * KV])):
                    sp.dma_start(dst, src).then_inc(out_copied, 16)
                for dst, src, new in ((sk_dram, cache_k_rows, 0), (sv_dram, cache_v_rows, KV)):
                    sp.dma_start(dst[:, 0:WINDOW - STEPS, :], src[:, STEPS:WINDOW, :]).then_inc(out_copied, 16)
                    sp.dma_start(dst[:, WINDOW - STEPS:WINDOW, :],
                                 z_kv[SEQ:TOK, new:new + KV].rearrange("(b s) c -> b s c", s=STEPS)).then_inc(out_copied, 16)

                def tile(t):
                    load_swa_next = not (isinstance(t, int) and t == TILES - 1)
                    if load_swa_next:
                        load_swa(t + 1)
                    if not (isinstance(t, int) and t == 0):
                        finish(t - 1)
                        load_gates(sp, T, bass.ds(t * P, P), P)
                    if load_swa_next:
                        load_gla(t + 1)
                        load_values(t + 1)
                        rows = bass.ds((t + 1) * P, P)
                        sp.wait_ge(T.oa_ready, t + 1)
                        load_vgate(sp, T, rows, P)

                tile(0)
                with sp.Fori(1, TILES - 1) as t:
                    tile(t)
                tile(TILES - 1)
                sp.wait_ge(S_ready, GLA_HEADS * TILES)
                sp.dma_start(ps_dram.rearrange("h d e -> d h e"), S[:, :, :]).then_inc(out_copied, 16)
                finish(TILES - 1)
                sp.wait_ge(out_copied, 16 * 7)
                sp.wait_ge(T.m_stored, 16 * TILES)

            @block.gpsimd
            def _(pool):
                pool.memset(ident[:, :], 0.0).then_inc(pstep, 1)
                pool.wait_ge(pstep, 1)
                pool.affine_select(out=ident[:, :], in_=ident[:, :], compare_op=ALU.not_equal, fill=1.0,
                                   base=0, pattern=[[-1, P]], channel_multiplier=1).then_inc(zeroed, 1)
                pool.memset(S[:, :, :], 0.0).then_inc(zeroed, 1)
                pool.memset(kk[:, :, 0, :], 0.0).then_inc(zeroed, 1)
                pool.memset(vv[:, 0, :], 0.0).then_inc(zeroed, 1)
                pool.wait_ge(consts, 16 * 4)
                gate_norm(pool, T, 0, P)
                with pool.Fori(1, TILES) as t:
                    gate_norm(pool, T, t, P)

            @block.scalar
            def _(act):
                chain = Chain(act, astep)
                act.wait_ge(zeroed, 4)

                def gla_exp(t, h):
                    i = GLA_HEADS * t + h
                    act.wait_ge(rel_ready, i + 1)
                    wait(act, T.o_done, i - 1)
                    chain.step(act.activation(rel[:, h % 2, :, :], rel[:, h % 2, :, :], ACT.Exp, scale=-1.0))
                    chain.step(act.activation(qt[:, h % 2, :], qt[:, h % 2, :], ACT.Exp))
                    chain.step(act.activation(eb[:, h % 2, :], b[:, h, :], ACT.Exp))
                    act.activation(kp[:, h % 2, :], b[:, h, :], ACT.Exp, bias=b[:, h, P - 1:P], scale=-1.0).then_inc(ex_done, 1)

                def tile(t):
                    gla_exp(t, 0)
                    gla_exp(t, 1)
                    act.wait_ge(neg_ready, t + 1)
                    for h in range(SWA_HEADS):
                        chain.step(act.activation(s[:, h, :], s[:, h, :], ACT.Exp, bias=m[:, 1, h:h + 1],
                                                  accum_out=e_sum[:, h:h + 1]))
                    act.activation(m[:, 2, :], m[:, 2, :], ACT.Exp).then_inc(e_done, 1)
                    for h in range(GLA_HEADS):
                        act.wait_ge(sc_done, GLA_HEADS * t + h + 1)
                        wait(act, su_done, GLA_HEADS * t + h - 1)
                        act.activation(kpT[:, h % 2, :], X[:, BANK + h * P:BANK + (h + 1) * P],
                                       ACT.Copy).then_inc(kpT_ready, 1)
                        if h < 2:
                            gla_exp(t, h + 2)
                    tail_norm_act(act, T, t, P)
                    for i in range(SWA_HEADS // 2):
                        act.wait_ge(pT_ps, 8 * t + i + 1)
                        act.activation(pT[:, i % 2, :, :], X[:, (i % 2) * BANK:(i % 2 + 1) * BANK].rearrange("p (a n) -> p a n", a=4),
                                       ACT.Copy).then_inc(pT_ready, 1)
                    tail_act(act, T, t, P)
                    chain.restart()

                tile(0)
                with act.Fori(1, TILES) as t:
                    tile(t)

            @block.vector
            def _(dve):
                chain = Chain(dve, vstep)
                dve.wait_ge(consts, 16 * 4)
                dve.wait_ge(zeroed, 4)

                def exponents(t, h):
                    i = GLA_HEADS * t + h
                    if h == 0:
                        dve.wait_ge(gla_in, 64 * (t + 1))
                    wait(dve, sc_done, i - 1)
                    for j in range(SUBS):
                        ref = b[:, h, j * SUB + SUB // 2:j * SUB + SUB // 2 + 1]
                        chain.step(dve.tensor_scalar(rel[:, h % 2, j, :], b[:, h, :], ref, -CLAMP, ALU.subtract, ALU.max))
                    blocks = b[:, h, :].rearrange("p (j i) -> p j i", j=SUBS)
                    view = qt[:, h % 2, :].rearrange("p (j i) -> p j i", j=SUBS)
                    chain.link(dve.tensor_tensor(view, blocks, blocks[:, :, SUB // 2:SUB // 2 + 1].to_broadcast([P, SUBS, SUB]),
                                                 ALU.subtract))
                    dve.tensor_scalar(qt[:, h % 2, :], qt[:, h % 2, :], CLAMP, None, ALU.min).then_inc(rel_ready, 1)

                def rescale(t, h):
                    i = GLA_HEADS * t + h
                    dve.wait_ge(ex_done, i + 1)
                    chain.step(dve.tensor_tensor(rel[:, h % 2, :, :], rel[:, h % 2, :, :],
                                                 k[:, h, :].unsqueeze(1).to_broadcast([P, SUBS, P]), ALU.mult))
                    wait(dve, T.o_done, i - 1)
                    chain.step(dve.scalar_tensor_tensor(out=qt[:, h % 2, :], in0=q[:, h, :], scalar=QSCALE,
                                                        in1=qt[:, h % 2, :], op0=ALU.mult, op1=ALU.mult))
                    chain.step(dve.scalar_tensor_tensor(out=qb[:, h % 2, :], in0=q[:, h, :], scalar=QSCALE,
                                                        in1=eb[:, h % 2, :], op0=ALU.mult, op1=ALU.mult))
                    dve.tensor_tensor(kp[:, h % 2, :], k[:, h, :], kp[:, h % 2, :], ALU.mult).then_inc(kq_ready, 1)

                def masked(t, h):
                    i = GLA_HEADS * t + h
                    dve.wait_ge(sc_done, i + 1)
                    dve.tensor_tensor(scm[:, h % 2, :], X[:, h * P:(h + 1) * P], causal[:, :], ALU.mult).then_inc(scm_ready, 1)

                def advance(t, h):
                    i = GLA_HEADS * t + h
                    dve.wait_ge(su_done, i + 1)
                    dve.scalar_tensor_tensor(out=S[:, h, :], in0=S[:, h, :], scalar=eb[:, h % 2, P - 1:P],
                                             in1=update(h), op0=ALU.mult, op1=ALU.add).then_inc(S_ready, 1)

                def tile(t):
                    first = isinstance(t, int) and t == 0

                    def tail(*steps):
                        for step in steps:
                            if not first:
                                tail_dve(dve, chain, T, t - 1, P, step)

                    exponents(t, 0)
                    exponents(t, 1)
                    for i in range(SWA_HEADS // 2):
                        wait_alone(dve, s_done, 8 * t + i + 1, tick)
                        if i == 0:
                            chain.settle()
                        for j in range(2):
                            h = 2 * i + j
                            last = dve.tensor_tensor_reduce(s[:, h, :], score_pair(i, j), mask[:, 0 if first else 1, :],
                                                            HD ** -0.5, sinks[:, h:h + 1], ALU.add, ALU.max,
                                                            m[:, 0, h:h + 1])
                            if j == 0:
                                chain.step(last)
                        last.then_inc(s_taken, 1)
                        if i == 1:
                            tail(0, 1)
                    dve.wait_ge(s_taken, 8 * (t + 1))
                    chain.step(dve.tensor_scalar(m[:, 1, :], m[:, 0, :], -1.0, None, ALU.mult))
                    dve.tensor_tensor(m[:, 2, :], sinks[:, :], m[:, 0, :], ALU.subtract).then_inc(neg_ready, 1)
                    rescale(t, 0)
                    rescale(t, 1)
                    tail(2)
                    masked(t, 0)
                    tail(3)
                    advance(t, 0)
                    exponents(t, 2)
                    masked(t, 1)
                    rescale(t, 2)
                    tail(4)
                    advance(t, 1)
                    exponents(t, 3)
                    dve.wait_ge(e_done, t + 1)
                    chain.link(dve.tensor_tensor(m[:, 3, :], e_sum[:, :], m[:, 2, :], ALU.add))
                    chain.link(dve.reciprocal(m[:, 3, :], m[:, 3, :]))
                    dve.tensor_tensor(s[:, :, :], s[:, :, :], m[:, 3, :].unsqueeze(2).to_broadcast([P, SWA_HEADS, 2 * P]),
                                      ALU.mult).then_inc(p_ready, 1)
                    masked(t, 2)
                    rescale(t, 3)
                    tail(5)
                    advance(t, 2)
                    masked(t, 3)
                    tail(6, 7)
                    advance(t, 3)
                    tail_oa_dve(dve, chain, T, t, P)
                    chain.restart()

                tile(0)
                tile(1)
                with dve.Fori(2, TILES) as t:
                    tile(t)
                for step in range(TAIL):
                    tail_dve(dve, chain, T, TILES - 1, P, step)

            @block.tensor
            def _(pe):
                pe.wait_ge(zeroed, 4)

                def gla_scores(t, h):
                    i = GLA_HEADS * t + h
                    pe.wait_ge(kq_ready, i + 1)
                    for j in range(SUBS):
                        pe.matmul(X[:, h * P + j * SUB:h * P + (j + 1) * SUB], rel[:, h % 2, j, :],
                                  qt[:, h % 2, j * SUB:(j + 1) * SUB], start=True, stop=True)
                    pe.transpose(X[:, BANK + h * P:BANK + (h + 1) * P], kp[:, h % 2, :], ident[:, :]).then_inc(sc_done, 1)

                def gla_out(t, h):
                    i = GLA_HEADS * t + h
                    vh = v[:, h * DV:(h + 1) * DV]
                    pe.wait_ge(scm_ready, i + 1)
                    wait(pe, S_ready, i - GLA_HEADS + 1)
                    pe.matmul(O[:, h * DV:(h + 1) * DV], scm[:, h % 2, :], vh, start=True, stop=False)
                    pe.matmul(O[:, h * DV:(h + 1) * DV], qb[:, h % 2, :], S[:, h, :], start=False, stop=True
                              ).then_inc(T.o_done, 1)
                    pe.wait_ge(kpT_ready, i + 1)
                    pe.wait_ge(T.o_done, i + 1)
                    if h >= 2:
                        pe.wait_ge(S_ready, i - 1)
                    pe.matmul(update(h), kpT[:, h % 2, :], vh, start=True, stop=True).then_inc(su_done, 1)

                def tile(t):
                    first = isinstance(t, int) and t == 0

                    def tail(*steps):
                        for step in steps:
                            if not first:
                                if step == 2 and isinstance(t, int):
                                    pe.wait_ge(weights, 32)
                                tail_pe(pe, T, t - 1, P, step)

                    pe.wait_ge(swa_in, 48 * (t + 1))
                    wait(pe, pT_ready, 8 * t)
                    wait(pe, T.oa_ready, t)
                    for i in range(SWA_HEADS // 2):
                        wait(pe, s_taken, 8 * t + i - 1)
                        for j in range(2):
                            half = j * HD
                            last = pe.matmul(score_pair(i, j), sq[half:half + HD, i, :],
                                             kk[half:half + HD, 2 * i // GROUP, :, :].rearrange("d a n -> d (a n)"),
                                             start=True, stop=True)
                        last.then_inc(s_done, 1)
                        if i == 1:
                            tail(0, 1)
                    tail(2)
                    pe.wait_ge(gla_in, 64 * (t + 1))
                    pe.wait_ge(s_taken, 8 * (t + 1))
                    wait(pe, T.obT_ready, t)
                    for h, steps in enumerate(((3,), (4,), (5,), (6, 7))):
                        gla_scores(t, h)
                        tail(*steps)
                        gla_out(t, h)
                    pe.wait_ge(p_ready, t + 1)
                    pe.wait_ge(vv_in, 16 * (t + 1))
                    pe.wait_ge(S_ready, GLA_HEADS * (t + 1))
                    for i in range(SWA_HEADS // 2 + 1):
                        if i < SWA_HEADS // 2:
                            wait(pe, pT_ready, 8 * t + i - 1)
                            for j in range(4):
                                last = pe.transpose(X[:, (i % 2) * BANK + j * P:(i % 2) * BANK + (j + 1) * P],
                                                    s[:, 2 * i + j // 2, (j % 2) * P:(j % 2 + 1) * P], ident[:, :])
                            last.then_inc(pT_ps, 1)
                        if i:
                            i -= 1
                            pe.wait_ge(pT_ready, 8 * t + i + 1)
                            g = 2 * i // GROUP
                            for j in range(2):
                                for a in range(2):
                                    last = pe.matmul(U[j * HD:(j + 1) * HD, i * P:(i + 1) * P], vv[:, a, g * HD:(g + 1) * HD],
                                                     pT[:, i % 2, 2 * j + a, :], start=(a == 0), stop=(a == 1))
                    last.then_inc(T.ob_done, 1)

                tile(0)
                tile(1)
                with pe.Fori(2, TILES) as t:
                    tile(t)
                for step in range(TAIL):
                    tail_pe(pe, T, TILES - 1, P, step)


        with ExitStack() as ctx:
            def sb(name, shape, dt=F32):
                return ctx.enter_context(nc.sbuf_tensor(name, shape, dt))

            N = NSAMP
            KEYS = WINDOW + STEPS
            T = Tail(sb, sem, "n_")
            q = sb("n_q", [P, GLA_HEADS, N])
            k = sb("n_k", [P, GLA_HEADS, N])
            b = sb("n_b", [P, GLA_HEADS, N])
            v = sb("n_v", [P, D])
            sq = sb("n_sq", [HD, SWA_HEADS, N])
            sq_seq = sb("n_sq_seq", [HD, SEQS, SWA_HEADS, STEPS])
            kk = sb("n_kk", [HD, SEQS, KV_HEADS, KEYS])
            vv = sb("n_vv", [P, SEQS, KV])
            v_new = sb("n_vnew", [STEPS, SEQS, KV])
            mask = sb("n_mask", [P, KEYS])
            causal = sb("n_causal", [N, N])
            seg_cols = sb("n_seg_cols", [P, SEQS, N])
            seg_rows = sb("n_seg_rows", [N, SEQS])
            sink = sb("n_sink", [P, 1])
            st = sb("n_st", [P, 2, SEQS, DV])
            kt = sb("n_kt", [P, 2, N])
            qt = sb("n_qt", [P, 2, N])
            kp = sb("n_kp", [P, 2, N])
            last_e = sb("n_last_e", [P, 2, SEQS])
            qm = sb("n_qm", [P, 2, SEQS, N])
            kpm = sb("n_kpm", [N, SEQS, P])
            scm = sb("n_scm", [N, N])
            s = sb("n_s", [P, SEQS, KEYS])
            m = sb("n_m", [P, 4, SEQS])
            e_sum = sb("n_e_sum", [P, SEQS])
            pT = sb("n_pT", [P, SEQS, P])
            pT_new = sb("n_pT_new", [STEPS, SEQS, P])

            gla_ins = sem("n_gla_ins")
            ins = sem("n_ins")
            sq_ready = sem("n_sq_ready")
            st_in = sem("n_st_in")
            st_out = sem("n_st_out")
            ex_in = sem("n_ex_in")
            ex_done = sem("n_ex_done")
            kq_ready = sem("n_kq_ready")
            sc_done = sem("n_sc_done")
            m_ready = sem("n_scm_ready")
            su_done = sem("n_su_done")
            st_ready = sem("n_st_ready")
            s_done = sem("n_s_done")
            neg_ready = sem("n_neg_ready")
            e_done = sem("n_e_done")
            p_ready = sem("n_p_ready")
            pT_ps = sem("n_pT_ps")
            pT_ready = sem("n_pT_ready")
            block = ctx.enter_context(nc.Block())
            PER_BANK = BANK // KEYS

            def score_place(seq):
                bank, at = seq // PER_BANK, (seq % PER_BANK) * KEYS
                tensor, base = ((X, 0), (X, BANK), (U, 0))[bank]
                return tensor, base + at

            @block.sync
            def _(sp):
                cols = slice(SEQ, TOK)
                for dst, src in ((b, z_b[:, :, cols]), (k, z_feat[4:8, :, cols]), (q, z_feat[0:4, :, cols])):
                    sp.dma_start(dst[:, :, :], src.rearrange("h p n -> p h n")).then_inc(gla_ins, 16)
                sp.dma_start(seg_cols[:, :, :], seg_cols_dram).then_inc(gla_ins, 16)
                sp.dma_start(causal[:, :], samp_causal_dram).then_inc(gla_ins, 16)
                sp.dma_start(seg_rows[:, :], seg_rows_dram).then_inc(gla_ins, 16)
                sp.dma_start(v[0:N, :], z_tok[cols, 0:D]).then_inc(gla_ins, 16)

                def load_state(h):
                    wait(sp, st_out, 16 * (h - 1))
                    sp.dma_start(st[:, h % 2, :, :], state_dram[:, h, :, :].rearrange("b d e -> d b e")).then_inc(st_in, 16)
                    sp.wait_ge(st_in, 16 * (h + 1))

                load_state(0)
                load_state(1)
                for half in range(2):
                    sp.dma_start(sq[:, half:SWA_HEADS:2, :],
                                 z_feat[8:16, half * HD:(half + 1) * HD, cols].rearrange("c d n -> d c n")).then_inc(ins, 16)
                for g in range(KV_HEADS):
                    sp.dma_start(kk[:, :, g, 0:WINDOW], cache_kT_dram[:, :, g, :]).then_inc(ins, 16)
                    sp.dma_start(kk[:, :, g, WINDOW:KEYS],
                                 z_kT[g * HD:(g + 1) * HD, cols].rearrange("d (b s) -> d b s", s=STEPS)).then_inc(ins, 16)
                sp.dma_start(vv[:, :, :], cache_v_dram).then_inc(ins, 16)
                sp.dma_start(v_new[:, :, :], z_kv[cols, KV:2 * KV].rearrange("(b s) c -> s b c", s=STEPS)).then_inc(ins, 16)
                sp.dma_start(mask[:, :], samp_mask_dram).then_inc(ins, 16)
                sp.dma_start(sink[:, :], sink_rows_dram).then_inc(ins, 16)
                load_vgate(sp, T, cols, N)
                load_gates(sp, T, cols, N)
                for h in range(GLA_HEADS):
                    sp.wait_ge(st_ready, SEQS * (h + 1))
                    sp.dma_start(ss_dram[:, h, :, :].rearrange("b d e -> d b e"), st[:, h % 2, :, :]).then_inc(st_out, 16)
                    sp.wait_ge(st_out, 16 * (h + 1))
                    if h + 2 < GLA_HEADS:
                        load_state(h + 2)
                sp.wait_ge(T.r_taken, TAIL)
                for start in (0, N):
                    sp.dma_start(m_dram[TILES].rearrange("p (k n) -> p k n", k=KT)[:, :, start:start + N],
                                 T.mT[:, :, 0:N]).then_inc(T.m_stored, 16)
                sp.wait_ge(T.m_stored, 32)

            @block.gpsimd
            def _(pool):
                pool.wait_ge(ins, 16 * 10)
                pool.tensor_copy(sq_seq[:, :, :, :], sq[:, :, :].rearrange("d h (b s) -> d b h s", s=STEPS)).then_inc(sq_ready, 1)
                gate_norm(pool, T, 0, N)

            @block.scalar
            def _(act):
                chain = Chain(act, astep)
                for h in range(GLA_HEADS):
                    act.wait_ge(ex_in, h + 1)
                    r = h % 2
                    wait(act, T.o_done, h - 1)
                    wait(act, st_ready, SEQS * (h - 1))
                    chain.step(act.activation(kt[:, r, :], kt[:, r, :], ACT.Exp, scale=-1.0))
                    chain.step(act.activation(qt[:, r, :], b[:, h, :], ACT.Exp))
                    chain.step(act.activation(kp[:, r, :], kp[:, r, :], ACT.Exp))
                    act.activation(last_e[:, r, :], b[:, h, STEPS - 1:N:STEPS], ACT.Exp).then_inc(ex_done, 1)
                tail_norm_act(act, T, 0, N)
                act.wait_ge(neg_ready, 1)
                for seq in range(SEQS):
                    chain.step(act.activation(s[:, seq, :], s[:, seq, :], ACT.Exp, bias=m[:, 1, seq:seq + 1],
                                              accum_out=e_sum[:, seq:seq + 1]))
                act.activation(m[:, 2, :], m[:, 2, :], ACT.Exp).then_inc(e_done, 1)
                for seq in range(SEQS):
                    r = seq % 2
                    act.wait_ge(pT_ps, seq + 1)
                    chain.step(act.activation(pT[:, seq, :], R[:, r, 0:P], ACT.Copy))
                    act.activation(pT_new[:, seq, :], R[0:STEPS, r, P:2 * P], ACT.Copy).then_inc(pT_ready, 1)
                tail_act(act, T, 0, N)

            @block.vector
            def _(dve):
                chain = Chain(dve, vstep)
                dve.wait_ge(gla_ins, 16 * 7)

                def exponents(h):
                    r = h % 2
                    blocks = b[:, h, :].rearrange("p (s i) -> p s i", s=SEQS)
                    wait(dve, sc_done, h - 1)
                    chain.step(dve.tensor_scalar(kt[:, r, :], b[:, h, :], -CLAMP, None, ALU.max))
                    dve.tensor_tensor(kp[:, r, :].rearrange("p (s i) -> p s i", s=SEQS),
                                      blocks[:, :, STEPS - 1:STEPS].to_broadcast([P, SEQS, STEPS]), blocks,
                                      ALU.subtract).then_inc(ex_in, 1)

                def rescale(h):
                    r = h % 2
                    dve.wait_ge(ex_done, h + 1)
                    chain.step(dve.tensor_tensor(kt[:, r, :], kt[:, r, :], k[:, h, :], ALU.mult))
                    chain.step(dve.tensor_tensor(kp[:, r, :], kp[:, r, :], k[:, h, :], ALU.mult))
                    chain.link(dve.scalar_tensor_tensor(out=qt[:, r, :], in0=q[:, h, :], scalar=QSCALE, in1=qt[:, r, :],
                                                        op0=ALU.mult, op1=ALU.mult))
                    dve.tensor_tensor(qm[:, r, :, :], qt[:, r, :].unsqueeze(1).to_broadcast([P, SEQS, N]), seg_cols[:, :, :],
                                      ALU.mult).then_inc(kq_ready, 1)

                exponents(0)
                rescale(0)
                for h in range(GLA_HEADS):
                    dve.wait_ge(sc_done, h + 1)
                    wait(dve, su_done, SEQS * h)
                    chain.step(dve.tensor_tensor(scm[:, :], R[0:N, 0, 0:N], causal[:, :], ALU.mult))
                    dve.tensor_tensor(kpm[:, :, :], R[0:N, 1, 0:P].unsqueeze(1).to_broadcast([N, SEQS, P]),
                                      seg_rows[:, :].unsqueeze(2).to_broadcast([N, SEQS, P]), ALU.mult).then_inc(m_ready, 1)
                    if h + 1 < GLA_HEADS:
                        exponents(h + 1)
                        rescale(h + 1)
                    dve.wait_ge(T.o_done, h + 1)
                    for seq in range(SEQS):
                        dve.wait_ge(su_done, SEQS * h + seq + 1)
                        at = (seq % 2) * BANK
                        dve.scalar_tensor_tensor(out=st[:, h % 2, seq, :], in0=st[:, h % 2, seq, :],
                                                 scalar=last_e[:, h % 2, seq:seq + 1], in1=U[:, at:at + DV],
                                                 op0=ALU.mult, op1=ALU.add).then_inc(st_ready, 1)
                tail_oa_dve(dve, chain, T, 0, N)
                dve.wait_ge(ins, 16 * 10)
                dve.wait_ge(s_done, 1)
                for seq in range(SEQS):
                    tensor, at = score_place(seq)
                    chain.step(dve.tensor_tensor_reduce(s[:, seq, :], tensor[:, at:at + KEYS], mask[:, :], HD ** -0.5, sink[:, :],
                                                        ALU.add, ALU.max, m[:, 0, seq:seq + 1]))
                chain.settle()
                chain.step(dve.tensor_scalar(m[:, 1, :], m[:, 0, :], -1.0, None, ALU.mult))
                dve.tensor_tensor(m[:, 2, :], sink[:, :].to_broadcast([P, SEQS]), m[:, 0, :], ALU.subtract).then_inc(neg_ready, 1)
                for step in range(2):
                    tail_dve(dve, chain, T, 0, N, step)
                dve.wait_ge(e_done, 1)
                chain.link(dve.tensor_tensor(m[:, 3, :], e_sum[:, :], m[:, 2, :], ALU.add))
                chain.link(dve.reciprocal(m[:, 3, :], m[:, 3, :]))
                dve.tensor_tensor(s[:, :, :], s[:, :, :], m[:, 3, :].unsqueeze(2).to_broadcast([P, SEQS, KEYS]),
                                  ALU.mult).then_inc(p_ready, 1)
                for step in range(2, TAIL):
                    tail_dve(dve, chain, T, 0, N, step)

            @block.tensor
            def _(pe):
                for h in range(GLA_HEADS):
                    vh = v[0:N, h * DV:(h + 1) * DV]
                    pe.wait_ge(kq_ready, h + 1)
                    wait(pe, m_ready, h)
                    if h == 0:
                        pe.wait_ge(gla_ins, 16 * 7)
                    pe.matmul(R[0:N, 0, 0:N], kt[:, h % 2, :], qt[:, h % 2, :], start=True, stop=True)
                    pe.transpose(R[0:N, 1, 0:P], kp[:, h % 2, :], ident[:, :]).then_inc(sc_done, 1)
                    pe.wait_ge(m_ready, h + 1)
                    pe.wait_ge(st_in, 16 * (h + 1))
                    pe.matmul(O[0:N, h * DV:(h + 1) * DV], scm[:, :], vh, start=True, stop=False)
                    for seq in range(SEQS):
                        last = pe.matmul(O[0:N, h * DV:(h + 1) * DV], qm[:, h % 2, seq, :], st[:, h % 2, seq, :],
                                         start=False, stop=(seq == SEQS - 1))
                    last.then_inc(T.o_done, 1)
                    for seq in range(SEQS):
                        at = (seq % 2) * BANK
                        wait(pe, st_ready, SEQS * h + seq - 1)
                        pe.matmul(U[:, at:at + DV], kpm[:, seq, :], vh, start=True, stop=True).then_inc(su_done, 1)
                pe.wait_ge(st_ready, SEQS * GLA_HEADS)
                pe.wait_ge(sq_ready, 1)
                pe.wait_ge(ins, 16 * 10)
                for seq in range(SEQS):
                    tensor, at = score_place(seq)
                    for g in range(KV_HEADS):
                        last = pe.matmul(tensor[g * HD:(g + 1) * HD, at:at + KEYS],
                                         sq_seq[:, seq, g * GROUP:(g + 1) * GROUP, :].rearrange("d h s -> d (h s)"),
                                         kk[:, seq, g, :], start=True, stop=True)
                last.then_inc(s_done, 1)
                for step in range(4):
                    tail_pe(pe, T, 0, N, step)
                pe.wait_ge(p_ready, 1)
                pe.wait_ge(T.r_taken, 4)

                def turn(seq):
                    r = seq % 2
                    wait(pe, pT_ready, seq - 1)
                    pe.transpose(R[:, r, 0:P], s[:, seq, 0:WINDOW], ident[:, :])
                    pe.transpose(R[0:STEPS, r, P:2 * P], s[:, seq, WINDOW:KEYS], ident[:, :]).then_inc(pT_ps, 1)

                turn(0)
                for seq in range(SEQS):
                    if seq + 1 < SEQS:
                        turn(seq + 1)
                    pe.wait_ge(pT_ready, seq + 1)
                    for g in range(KV_HEADS):
                        for j in range(2):
                            rows = lambda t: t[:, seq, g * HD:(g + 1) * HD].rearrange("k (h s) -> k h s", s=STEPS)[:, j:GROUP:2, :]
                            out = U[j * HD:(j + 1) * HD, 0:KT * N].rearrange("d (c n) -> d c n", c=KT)[
                                :, g * (GROUP // 2):(g + 1) * (GROUP // 2), seq * STEPS:(seq + 1) * STEPS]
                            pe.matmul(out, vv[:, seq, g * HD:(g + 1) * HD], rows(pT), start=True, stop=False)
                            last = pe.matmul(out, v_new[:, seq, g * HD:(g + 1) * HD], rows(pT_new), start=False, stop=True)
                last.then_inc(T.ob_done, 1)
                for step in range(4, TAIL):
                    tail_pe(pe, T, 0, N, step)


def peer_stage(nc, sem, x_dram, m_dram, wo_dram, wq_dram, keys_dram, u_dram, v_dram, g_ffn_dram, g_final_dram, y_dram):
    U_RING, V_RING = 8, 8
    IDX = 4
    WQ_PARTS = 2
    DIAGS = 8
    W_OUT = {2: (0,), 3: (1,), 4: (2, 3)}
    RESIDUAL = (4, 5)
    with ExitStack() as ctx:
        def sb(name, shape, dt=F32):
            return ctx.enter_context(nc.sbuf_tensor(name, shape, dt))

        def pb(name, shape):
            return ctx.enter_context(nc.psum_tensor(name, shape, F32))

        wq = sb("e_wq", [P, KT, QD])
        keys = sb("e_keys", [P, 2 * HEADS, NKEYS])
        g_ffn = sb("e_g_ffn", [P, D])
        g_final = sb("e_g_final", [P, D])
        ident = sb("e_ident", [P, P])
        ident_pair = sb("e_ident_pair", [P, NSAMP])
        iota16 = sb("e_iota16", [P, TOPK])
        u_rows = sb("e_u_rows", [P, U_RING, D])
        v_rows = sb("e_v_rows", [P, V_RING, D])
        wo = sb("e_wo", [P, KT, D])
        h_next = sb("e_h_next", [P, D])
        room = sb("e_room", [P, D])
        xn_next = y = room
        mT = room[:, :].rearrange("p (k n) -> p k n", k=KT)
        xn = sb("e_xn", [P, D])
        xnT = sb("e_xnT", [P, KT, P])
        q_sb = sb("e_q_sb", [P, 2, P])
        s_sb = sb("e_s_sb", [P, 2, NKEYS])
        top_val = sb("e_top_val", [P, 2, TOPK])
        top_idx = sb("e_top_idx", [P, 2, TOPK], U32)
        top_idxf = sb("e_top_idxf", [P, 2, TOPK])
        pairs = sb("e_pairs", [P, 2 * TOPK * TOPK])
        cand, cand_rest = pairs[:, 0:TOPK * TOPK], pairs[:, TOPK * TOPK:]
        s_rest = cand_rest.rearrange("p (s n) -> p s n", s=2)
        hot = pairs[:, :].rearrange("p (s a b) -> p s a b", s=2, a=TOPK)
        best = sb("e_best", [P, IDX, TOPK])
        pos = sb("e_pos", [P, TOPK], U32)
        pos_ab = sb("e_pos_ab", [P, 2, TOPK], U32)
        pos_abf = sb("e_pos_abf", [P, 2, TOPK])
        picked = sb("e_picked", [P, 2, TOPK])
        expert = sb("e_expert", [P, IDX, TOPK], U32)
        expert_pair = sb("e_expert_pair", [P, IDX, TOPK // 2], U32)
        neg_best = sb("e_neg_best", [P, IDX])
        e_top = sb("e_e_top", [P, IDX, TOPK])
        e_sum = sb("e_e_sum", [P, IDX])
        e_rec = sb("e_e_rec", [P, IDX])
        dots = sb("e_dots", [P, 2, TOPK])
        gelus = sb("e_gelus", [P, 2, TOPK])
        weight = sb("e_weight", [P, 2, TOPK])
        diag = sb("e_diag", [P, DIAGS, P])
        stat = sb("e_stat", [P, 8])
        q_ps = pb("e_q_ps", [P, 2, P])
        s_ps = pb("e_s_ps", [P, 2, NKEYS])
        t_ps = [pb(f"e_t_ps{i}", [P, 4, P]) for i in range(2)]
        o_ps = pb("e_o_ps", [P, D])
        w_ps = pb("e_w_ps", [P, D])

        norm_in = sem("e_norm_in")
        keys_in = sem("e_keys_in")
        wq_in = [sem(f"e_wq_in{i}") for i in range(WQ_PARTS)]
        consts = sem("e_consts")
        made = sem("e_made")
        wo_in = [sem(f"e_wo_in{c}") for c in range(2)]
        m_in = sem("e_m_in")
        x_in = sem("e_x_in")
        wo_done = sem("e_wo_done")
        h_ready = sem("e_h_ready")
        h_used = sem("e_h_used")
        moved = sem("e_moved")
        sq_done = sem("e_sq_done")
        rt_in = sem("e_rt_in")
        rt_done = sem("e_rt_done")
        xn_ready = sem("e_xn_ready")
        xnT_ps = sem("e_xnT_ps")
        xnT_ready = sem("e_xnT_ready")
        q_done = sem("e_q_done")
        q_ready = sem("e_q_ready")
        s_done = sem("e_s_done")
        s_taken = sem("e_s_taken")
        picked_ready = sem("e_picked_ready")
        paired = sem("e_paired")
        e_done = sem("e_e_done")
        u_got = [sem(f"e_u_got{i}") for i in range(U_RING)]
        v_got = [sem(f"e_v_got{i}") for i in range(V_RING)]
        u_used = sem("e_u_used")
        v_used = sem("e_v_used")
        gelu_done = sem("e_gelu_done")
        w_ready = sem("e_w_ready")
        diag_ready = sem("e_diag_ready")
        acc_ready = sem("e_acc_ready")
        out_sq = sem("e_out_sq")
        out_ms = sem("e_out_ms")
        out_rt = sem("e_out_rt")
        y_ready = sem("e_y_ready")
        y_stored = sem("e_y_stored")
        vstep = sem("e_vstep")
        tick = sem("tick")
        pstep = sem("e_pstep")
        block = ctx.enter_context(nc.Block())
        LAST = TILES

        def rows(t):
            return NSAMP if isinstance(t, int) and t == LAST else P

        def slots(t, h=0):
            return TOPK // 2 if isinstance(t, int) and t == LAST and h >= 0 else TOPK

        def slots_before(unit):
            if isinstance(unit, int) and unit > LAST * HEADS:
                return LAST * HEADS * TOPK + (unit - LAST * HEADS) * (TOPK // 2)
            return unit * TOPK

        def rounds(unit, k, ring):
            if isinstance(unit, int):
                return slots_before(unit) // ring + k // ring + 1
            return unit * (TOPK // ring) + k // ring + 1

        @block.sync
        def _(sp):

            def load_merge(t):
                wait_alone(sp, moved, t, tick)
                wait_alone(sp, xnT_ps, 2 * t, tick)
                wait_alone(sp, y_stored, 16 * (t - 1), tick)
                sp.dma_start(room[:, :], m_dram[bass.ds(t, 1), :, :].rearrange("o p n -> p (o n)")).then_inc(m_in, 16)

            def load_x(t):
                wait_alone(sp, sq_done, t, tick)
                wait_alone(sp, h_used, t, tick)
                sp.dma_start(h_next[:, :], x_dram[bass.ds(t * P, P), :]).then_inc(x_in, 16)

            def store(t):
                wait_alone(sp, y_ready, t + 1, tick)
                sp.dma_start(y_dram[bass.ds(t * P, rows(t)), :], y[0:rows(t), :]).then_inc(y_stored, 16)

            for c in range(2):
                sp.dma_start(wo[:, :, c * BANK:(c + 1) * BANK], wo_dram[:, :, c * BANK:(c + 1) * BANK]).then_inc(wo_in[c], 16)
                if c == 0:
                    load_merge(0)
                    load_x(0)
            sp.dma_start(g_ffn[:, :], g_ffn_dram.to_broadcast([P, D])).then_inc(norm_in, 16)
            part = QD // WQ_PARTS
            for i in range(WQ_PARTS):
                sp.dma_start(wq[:, :, i * part:(i + 1) * part], wq_dram[:, :, i * part:(i + 1) * part]).then_inc(wq_in[i], 16)
                if i == 0:
                    sp.dma_start(keys[:, :, :], keys_dram).then_inc(keys_in, 16)
            sp.dma_start(g_final[:, :], g_final_dram.to_broadcast([P, D])).then_inc(consts, 16)

            def tile(t):
                if not (isinstance(t, int) and t == 0):
                    store(t - 1)
                if not (isinstance(t, int) and t == LAST):
                    load_x(t + 1)
                    load_merge(t + 1)

            tile(0)
            with sp.Fori(1, LAST) as t:
                tile(t)
            tile(LAST)
            store(LAST)
            sp.wait_ge(y_stored, 16 * (LAST + 1))

        @block.gpsimd
        def _(pool):
            pool.memset(ident[:, :], 0.0).then_inc(pstep, 1)
            pool.wait_ge(pstep, 1)
            pool.affine_select(out=ident[:, :], in_=ident[:, :], compare_op=ALU.not_equal, fill=1.0,
                               base=0, pattern=[[-1, P]], channel_multiplier=1).then_inc(made, 1)
            pool.memset(ident_pair[:, :], 0.0).then_inc(pstep, 1)
            for i in range(2):
                pool.wait_ge(pstep, 2 + i)
                pool.affine_select(out=ident_pair[:, :], in_=ident_pair[:, :], compare_op=ALU.not_equal, fill=1.0,
                                   base=-i * NSAMP, pattern=[[-1, NSAMP]], channel_multiplier=1
                                   ).then_inc(made if i else pstep, 1)
            pool.iota(iota16[:, :], [[1, TOPK]], base=0, channel_multiplier=0,
                      allow_small_or_imprecise_dtypes=True).then_inc(made, 1)

            def gather(table, ring, got, used, t, h, k):
                size = len(got)
                wait_alone(pool, used, slots_before(t * HEADS + h) + k - size + 1, tick)
                index = expert if slots(t, h) == TOPK else expert_pair
                pool.indirect_dma_start(ring[:, k % size, :], None, table,
                                        bass.IndirectOffsetOnAxis(ap=index[:, h % IDX, k:k + 1], axis=0)
                                        ).then_inc(got[k % size], 16)

            def u_gather(t, h, k):
                gather(u_dram, u_rows, u_got, u_used, t, h, k)

            def v_gather(t, h, k):
                gather(v_dram, v_rows, v_got, v_used, t, h, k)

            def tile(t):
                for h in range(HEADS):
                    early = 0
                    if slots(t) == TOPK:
                        wait_alone(pool, picked_ready, t * HEADS + h + 1, tick)
                    else:
                        if h == 0:
                            early = V_RING
                            for k in range(early):
                                v_gather(t, -1, k)
                        pool.wait_ge(paired, h + 1)
                    for k in range(TOPK):
                        if k < slots(t):
                            u_gather(t, h, k)
                        if early + k < slots(t, h - 1) and not (isinstance(t, int) and t == 0 and h == 0):
                            v_gather(t, h - 1, early + k)

            tile(0)
            with pool.Fori(1, LAST) as t:
                tile(t)
            tile(LAST)
            for k in range(slots(LAST)):
                v_gather(LAST, HEADS - 1, k)

        @block.scalar
        def _(act):
            def norm(t):
                act.wait_ge(h_ready, 2 * (t + 1))
                act.wait_ge(wo_done, 2 * (t + 1))
                act.activation(xn_next[:, :], h_next[:, :], ACT.Square, accum_out=stat[:, 0:1]).then_inc(sq_done, 1)
                act.wait_ge(rt_in, t + 1)
                act.activation(stat[:, 2:3], stat[:, 1:2], ACT.Sqrt).then_inc(rt_done, 1)
                for i in range(2):
                    act.wait_ge(xnT_ps, 2 * t + i + 1)
                    act.activation(xnT[:, 4 * i:4 * i + 4, :], t_ps[i][:, :, :], ACT.Copy).then_inc(xnT_ready, 1)

            def queries(unit):
                act.wait_ge(q_done, unit + 1)
                wait(act, s_done, unit)
                act.activation(q_sb[:, :, :], q_ps[:, :, :], ACT.Copy).then_inc(q_ready, 1)

            def exponentials(unit, h):
                b = h % IDX
                act.wait_ge(picked_ready, unit + 1)
                act.activation(e_top[:, b, :], best[:, b, :], ACT.Exp, bias=neg_best[:, b:b + 1],
                               accum_out=e_sum[:, b:b + 1]).then_inc(e_done, 1)

            def gelu(t, h):
                unit, n = t * HEADS + h, slots(t, h)
                act.wait_ge(u_used, slots_before(unit + 1))
                wait(act, w_ready, unit - 1)
                act.activation(gelus[:, h % 2, 0:n], dots[:, h % 2, 0:n], ACT.Gelu).then_inc(gelu_done, 1)

            def diagonals(t, h):
                unit = t * HEADS + h
                act.wait_ge(w_ready, unit + 1)
                eye = ident if slots(t, h) == TOPK else ident_pair
                for k in range(slots(t, h)):
                    wait(act, v_used, slots_before(unit) + k - DIAGS + 1)
                    act.activation(diag[:, k % DIAGS, 0:eye.shape[1]], eye[:, :], ACT.Copy,
                                   scale=weight[:, h % 2, k:k + 1]).then_inc(diag_ready, 1)

            def evacuate(t):
                act.wait_ge(v_used, slots_before((t + 1) * HEADS))
                if isinstance(t, int) and t == LAST:
                    act.wait_ge(y_stored, 16 * LAST)
                else:
                    act.wait_ge(moved, t + 2)
                    act.wait_ge(xnT_ps, 2 * (t + 2))
                n = rows(t)
                act.activation(y[0:n, :], o_ps[0:n, :], ACT.Square, accum_out=stat[0:n, 4:5]).then_inc(out_sq, 1)
                act.wait_ge(out_sq, t + 1)
                act.activation(y[0:n, :], o_ps[0:n, :], ACT.Copy).then_inc(acc_ready, 1)

            def out_root(t):
                act.wait_ge(out_ms, t + 1)
                act.activation(stat[0:rows(t), 6:7], stat[0:rows(t), 5:6], ACT.Sqrt).then_inc(out_rt, 1)

            act.wait_ge(made, 3)
            norm(0)
            queries(0)
            queries(1)
            exponentials(0, 0)
            exponentials(1, 1)

            def tile(t):
                first = isinstance(t, int) and t == 0
                last = isinstance(t, int) and t == LAST
                for h in range(HEADS):
                    unit = t * HEADS + h
                    if h == 1 and not first:
                        out_root(t - 1)
                    if h == HEADS - 2 and not last:
                        norm(t + 1)
                    if not (first and h == 0):
                        diagonals(t, h - 1)
                    if h < HEADS - 2 or not last:
                        queries(unit + 2)
                    gelu(t, h)
                    if h < HEADS - 2 or not last:
                        exponentials(unit + 2, (h + 2) % HEADS)
                    if h == 0 and not first:
                        evacuate(t - 1)

            tile(0)
            with act.Fori(1, LAST) as t:
                tile(t)
            tile(LAST)
            diagonals(LAST, HEADS - 1)
            evacuate(LAST)
            out_root(LAST)

        @block.vector
        def _(dve):
            chain = Chain(dve, vstep)

            def residual(t, c):
                dve.wait_ge(x_in, 16 * (t + 1))
                dve.wait_ge(wo_done, 2 * t + c + 1)
                cols = slice(c * BANK, (c + 1) * BANK)
                dve.tensor_tensor(h_next[:, cols], h_next[:, cols], w_ps[:, cols], ALU.add).then_inc(h_ready, 1)

            def norm(t):
                dve.wait_ge(sq_done, t + 1)
                dve.tensor_scalar(stat[:, 1:2], stat[:, 0:1], 1.0 / D, EPS, ALU.mult, ALU.add).then_inc(rt_in, 1)
                dve.wait_ge(rt_done, t + 1)
                chain.link(dve.reciprocal(stat[:, 3:4], stat[:, 2:3]))
                dve.scalar_tensor_tensor(out=xn_next[:, :], in0=h_next[:, :], scalar=stat[:, 3:4],
                                         in1=g_ffn[:, :], op0=ALU.mult, op1=ALU.mult).then_inc(xn_ready, 1)

            def take(t):
                dve.wait_ge(xn_ready, t + 1)
                wait(dve, u_used, t * HEADS * TOPK)
                dve.tensor_copy(xn[:, :], xn_next[:, :]).then_inc(moved, 1)
                dve.wait_ge(moved, t + 1)

            def top16(values, indices, source, rest):
                chain.link(dve.max(values[:, 0:8], source))
                chain.step(dve.max_index(indices[:, 0:8], values[:, 0:8], source))
                chain.link(dve.match_replace(rest, values[:, 0:8], source, LOWEST))
                chain.link(dve.max(values[:, 8:16], rest))
                chain.step(dve.max_index(indices[:, 8:16], values[:, 8:16], rest))

            def select(unit, h):
                b = h % IDX
                dve.wait_ge(s_done, unit + 1)
                dve.tensor_copy(s_sb[:, :, :], s_ps[:, :, :]).then_inc(s_taken, 1)
                dve.wait_ge(s_taken, unit + 1)
                wait(dve, v_used, slots_before(unit - IDX + 1))
                chain.step(dve.tensor_copy(stat[:, 7:8], stat[:, 3:4]))
                for half in range(2):
                    top16(top_val[:, half, :], top_idx[:, half, :], s_sb[:, half, :], s_rest[:, half, :])
                chain.settle()
                chain.step(dve.tensor_copy(top_idxf[:, :, :], top_idx[:, :, :]))
                chain.link(dve.tensor_tensor(cand.rearrange("p (a b) -> p a b", a=TOPK),
                                             top_val[:, 0, :].unsqueeze(2).to_broadcast([P, TOPK, TOPK]),
                                             top_val[:, 1, :].unsqueeze(1).to_broadcast([P, TOPK, TOPK]), ALU.add))
                top16(best[:, b, :], pos[:, :], cand, cand_rest)
                chain.settle()
                chain.step(dve.tensor_scalar(pos_ab[:, 0, :], pos[:, :], 4, None, ALU.logical_shift_right))
                chain.step(dve.tensor_scalar(pos_ab[:, 1, :], pos[:, :], TOPK - 1, None, ALU.bitwise_and))
                chain.link(dve.tensor_scalar(neg_best[:, b:b + 1], best[:, b, 0:1], -1.0, None, ALU.mult))
                chain.link(dve.tensor_copy(pos_abf[:, :, :], pos_ab[:, :, :]))
                chain.link(dve.tensor_tensor(
                    hot[:, :, :, :].rearrange("p s a b -> p (s a) b"),
                    pos_abf[:, :, :].rearrange("p s a -> p (s a)").unsqueeze(2).to_broadcast([P, 2 * TOPK, TOPK]),
                    iota16[:, :].unsqueeze(1).to_broadcast([P, 2 * TOPK, TOPK]), ALU.is_equal))
                chain.link(dve.tensor_tensor(hot[:, :, :, :], hot[:, :, :, :],
                                             top_idxf[:, :, :].unsqueeze(2).to_broadcast([P, 2, TOPK, TOPK]), ALU.mult))
                chain.link(dve.tensor_reduce(picked[:, :, :], hot[:, :, :, :], AX_X, ALU.add))
                dve.scalar_tensor_tensor(out=expert[:, b, :], in0=picked[:, 0, :], scalar=float(NKEYS),
                                         in1=picked[:, 1, :], op0=ALU.mult, op1=ALU.add).then_inc(picked_ready, 1)

            def pair(h):
                b = h % IDX
                dve.wait_ge(picked_ready, LAST * HEADS + h + 1)
                chain.step(dve.tensor_copy(expert_pair[0:NSAMP, b, :], expert[0:NSAMP, b, 0:TOPK:2]))
                dve.tensor_copy(expert_pair[NSAMP:P, b, :], expert[NSAMP:P, b, 1:TOPK:2]).then_inc(paired, 1)

            def u_dots(t, h):
                unit = t * HEADS + h
                wait(dve, gelu_done, unit - 1)
                for k in range(slots(t, h)):
                    dve.wait_ge(u_got[k % U_RING], 16 * rounds(unit, k, U_RING))
                    dve.tensor_tensor_reduce(u_rows[:, k % U_RING, :], u_rows[:, k % U_RING, :], xn[:, :], 1.0, 0.0,
                                             ALU.mult, ALU.add, dots[:, h % 2, k:k + 1]).then_inc(u_used, 1)

            def weights(t, h):
                unit, b = t * HEADS + h, h % IDX
                dve.wait_ge(e_done, unit + 1)
                chain.link(dve.reciprocal(e_rec[:, b:b + 1], e_sum[:, b:b + 1]))
                dve.wait_ge(gelu_done, unit + 1)
                wait(dve, diag_ready, slots_before(unit - 1))

                def product(p0, p1, first, stride, n):
                    return dve.scalar_tensor_tensor(out=weight[p0:p1, h % 2, 0:n], in0=gelus[p0:p1, h % 2, 0:n],
                                                    scalar=e_rec[p0:p1, b:b + 1], in1=e_top[p0:p1, b, first:TOPK:stride],
                                                    op0=ALU.mult, op1=ALU.mult)

                if slots(t, h) == TOPK:
                    product(0, P, 0, 1, TOPK).then_inc(w_ready, 1)
                else:
                    chain.step(product(0, NSAMP, 0, 2, TOPK // 2))
                    product(NSAMP, P, 1, 2, TOPK // 2).then_inc(w_ready, 1)

            def out_mean(t):
                n = rows(t)
                dve.wait_ge(out_sq, t + 1)
                dve.tensor_scalar(stat[0:n, 5:6], stat[0:n, 4:5], 1.0 / D, EPS, ALU.mult, ALU.add).then_inc(out_ms, 1)

            def out_norm(t):
                n = rows(t)
                dve.wait_ge(out_rt, t + 1)
                dve.wait_ge(consts, 16)
                chain.link(dve.reciprocal(stat[0:n, 6:7], stat[0:n, 6:7]))
                dve.wait_ge(acc_ready, t + 1)
                dve.scalar_tensor_tensor(out=y[0:n, :], in0=y[0:n, :], scalar=stat[0:n, 6:7],
                                         in1=g_final[0:n, :], op0=ALU.mult, op1=ALU.mult).then_inc(y_ready, 1)

            dve.wait_ge(norm_in, 16)
            dve.wait_ge(made, 3)
            for c in range(2):
                residual(0, c)
            norm(0)
            take(0)
            select(0, 0)
            select(1, 1)
            chain.restart()

            def tile(t):
                first = isinstance(t, int) and t == 0
                last = isinstance(t, int) and t == LAST
                if last:
                    pair(0)
                    pair(1)
                for h in range(HEADS):
                    unit = t * HEADS + h
                    if h == 1 and not first:
                        out_mean(t - 1)
                    if h in RESIDUAL and not last:
                        residual(t + 1, RESIDUAL.index(h))
                    if h == HEADS - 2 and not last:
                        norm(t + 1)
                    u_dots(t, h)
                    if h == HEADS - 1 and not last:
                        take(t + 1)
                    if h < HEADS - 2 or not last:
                        select(unit + 2, (h + 2) % HEADS)
                    if h < HEADS - 2 and last:
                        pair(h + 2)
                    weights(t, h)
                    if h == 1 and not first:
                        out_norm(t - 1)
                chain.restart()

            tile(0)
            with dve.Fori(1, LAST) as t:
                tile(t)
            tile(LAST)
            out_mean(LAST)
            out_norm(LAST)

        @block.tensor
        def _(pe):
            def transposes(t):
                pe.wait_ge(xn_ready, t + 1)
                for i in range(2):
                    wait(pe, xnT_ready, 2 * (t - 1) + i + 1)
                    for j in range(4):
                        k = 4 * i + j
                        last = pe.transpose(t_ps[i][:, j, :], xn_next[:, k * P:(k + 1) * P], ident[:, :])
                    last.then_inc(xnT_ps, 1)

            def w_out(t, part):
                c, late = divmod(part, 2)
                if isinstance(t, int) and t == 0:
                    pe.wait_ge(wo_in[c], 16)
                if part == 0:
                    pe.wait_ge(m_in, 16 * (t + 1))
                    wait(pe, h_ready, 2 * t)
                for k in range(4 * late, 4 * late + 4):
                    last = pe.matmul(w_ps[:, c * BANK:(c + 1) * BANK], mT[:, k, :], wo[:, k, c * BANK:(c + 1) * BANK],
                                     start=(k == 0), stop=(k == KT - 1))
                if late:
                    last.then_inc(wo_done, 1)

            def query(unit, h, t, half):
                if isinstance(unit, int) and unit < HEADS:
                    pe.wait_ge(wq_in[h * WQ_PARTS // HEADS], 16)
                pe.wait_ge(xnT_ready, 2 * (t + 1))
                wait(pe, q_ready, unit)
                j = 2 * h + half
                for k in range(KT):
                    last = pe.matmul(q_ps[:, half, :], wq[:, k, j * P:(j + 1) * P], xnT[:, k, :],
                                     start=(k == 0), stop=(k == KT - 1))
                if half:
                    last.then_inc(q_done, 1)

            def scores(unit, h):
                pe.wait_ge(q_ready, unit + 1)
                if isinstance(unit, int) and unit == 0:
                    pe.wait_ge(keys_in, 16)
                wait(pe, s_taken, unit)
                for half in range(2):
                    last = pe.matmul(s_ps[:, half, :], q_sb[:, half, :], keys[:, 2 * h + half, :],
                                     start=True, stop=True)
                last.then_inc(s_done, 1)

            def carry(t):
                n = rows(t)
                wait(pe, acc_ready, t)
                for c in range(D // BANK):
                    last = pe.matmul(o_ps[0:n, c * BANK:(c + 1) * BANK], ident[0:n, 0:n],
                                     h_next[0:n, c * BANK:(c + 1) * BANK], start=True, stop=False)
                last.then_inc(h_used, 1)

            def v_sum(t, h, part):
                unit, count = t * HEADS + h, slots(t, h)
                n = P if count == TOPK else NSAMP
                for k in range(part * count // 4, (part + 1) * count // 4):
                    pe.wait_ge(diag_ready, slots_before(unit) + k + 1)
                    pe.wait_ge(v_got[k % V_RING], 16 * rounds(unit, k, V_RING))
                    for c in range(D // BANK):
                        last = pe.matmul(o_ps[0:n, c * BANK:(c + 1) * BANK], diag[:, k % DIAGS, 0:n],
                                         v_rows[:, k % V_RING, c * BANK:(c + 1) * BANK],
                                         start=False, stop=(h % HEADS == HEADS - 1 and k == count - 1))
                    last.then_inc(v_used, 1)

            pe.wait_ge(made, 3)
            for part in range(4):
                w_out(0, part)
            transposes(0)
            for h in range(2):
                for half in range(2):
                    query(h, h, 0, half)
                scores(h, h)

            def tile(t):
                first = isinstance(t, int) and t == 0
                last = isinstance(t, int) and t == LAST
                for h in range(HEADS):
                    unit = t * HEADS + h
                    if h == HEADS - 2 and not last:
                        transposes(t + 1)
                    ahead = h < HEADS - 2 or not last
                    if h == 1:
                        carry(t)
                    for part in range(4):
                        if ahead and part < 2:
                            query(unit + 2, (h + 2) % HEADS, t + (h + 2) // HEADS, part)
                        if ahead and part == 2:
                            scores(unit + 2, (h + 2) % HEADS)
                        if part == 3 and not last:
                            for quarter in W_OUT.get(h, ()):
                                w_out(t + 1, quarter)
                        if not first or h:
                            v_sum(t, h - 1, part)

            tile(0)
            with pe.Fori(1, LAST) as t:
                tile(t)
            tile(LAST)
            for part in range(4):
                v_sum(LAST, HEADS - 1, part)


def build(nc, i, o):
    with ExitStack() as ctx:
        named = {}

        def sem(name):
            if name not in named:
                named[name] = ctx.enter_context(nc.semaphore(name))
            return named[name]

        stages(nc, sem, i, o)


def stages(nc, sem, i, o):
    scratch = lambda name, shape: nc.dram_tensor(name, shape, F32, kind="Internal").ap()
    z_tok = scratch("z_tok", (TOK, 4 * D))
    z_feat = scratch("z_feat", (16, P, TOK))
    z_kv = scratch("z_kv", (TOK, 2 * KV))
    z_kT = scratch("z_kT", (KV, TOK))
    z_b = scratch("z_b", (GLA_HEADS, P, TOK))
    merged = scratch("merged", (TILES + 1, P, D))
    project_stage(nc, sem, i("x"), i("g_mix"), i("w_big"), i("w_small"), i("w_decay"), i("b_decay"),
                  z_tok, z_feat, z_kv, z_kT, z_b)
    mix_stage(nc, sem, i("wa"), i("wb"), i("gla_norm"), i("sinks"), i("sink_rows"), i("mask"),
              i("causal"), i("samp_mask"), i("samp_causal"), i("seg_cols"), i("seg_rows"), i("cache_kT"),
              i("cache_v"), i("cache_k_rows"), i("cache_v_rows"), i("state"), z_tok, z_feat, z_kv, z_kT, z_b, merged,
              o["pk"], o["pv"], o["ps"], o["sk"], o["sv"], o["ss"])
    peer_stage(nc, sem, i("x"), merged, i("wo"), i("wq"), i("keys"), i("u"), i("v"), i("g_ffn"), i("g_final"), o["y"])


OUTPUTS = [("y", (TOK, D)), ("pk", (WINDOW, KV)), ("pv", (WINDOW, KV)), ("ps", (GLA_HEADS, DK, DV)),
           ("sk", (SEQS, WINDOW, KV)), ("sv", (SEQS, WINDOW, KV)), ("ss", (SEQS, GLA_HEADS, DK, DV))]


def kernel(**inputs):
    import numpy as np
    import concourse.bacc as bacc
    from concourse.bass_utils import run_bass_kernel_spmd as run

    a = {name: np.asarray(value) for name, value in inputs.items()}
    w_in = a["w_in"][0]

    def tiled(w):
        return w.reshape(-1, P, w.shape[1]).transpose(1, 0, 2)

    gq, gk, gv, gg, glr, sq, sk, ga, gb = 0, 512, 1024, 2048, 3072, 3088, 4112, 4368, 5392
    starts = [c + d for c in (gv, gg, ga, gb) for d in (0, CHUNK)] + [gq, gk, sq, sq + CHUNK]
    token, key = np.arange(P)[:, None], np.arange(P)[None, :]
    window = np.concatenate([np.where(key > token, 0.0, MASKED), np.where(key <= token, 0.0, MASKED)], 1)
    first = np.concatenate([np.full((P, P), MASKED), window[:, P:]], 1)
    step = np.arange(P)[:, None] % STEPS
    late = np.arange(WINDOW + STEPS)[None, :]
    samp = np.where((late > step) & (late <= WINDOW + step), 0.0, MASKED)
    row, col = np.arange(NSAMP)[:, None], np.arange(NSAMP)[None, :]
    same = row // STEPS == col // STEPS
    seg = np.arange(SEQS)[:, None] == col // STEPS
    f32 = np.float32
    arrays = {
        "x": np.concatenate([a["x_prompt"].reshape(SEQ, D)] + 2 * [a["x_sample"].reshape(NSAMP, D)]),
        "g_mix": a["norm_mix"], "g_ffn": a["norm_ffn"], "g_final": a["norm_final"][None],
        "w_big": np.stack([tiled(w_in[:, c:c + CHUNK]).reshape(P, KT * CHUNK) for c in starts]),
        "w_small": tiled(np.concatenate([w_in[:, glr:glr + RANK], w_in[:, sk:sk + 2 * KV]], 1)),
        "w_decay": a["gla_w_decay"][0], "b_decay": a["gla_b_decay"].reshape(GLA_HEADS, DK).T,
        "wa": tiled(a["w_branch_a"][0]), "wb": tiled(a["w_branch_b"][0]), "wo": tiled(a["w_out"][0]),
        "gla_norm": a["gla_norm"], "sinks": a["swa_sinks"],
        "sink_rows": np.repeat(a["swa_sinks"][0], STEPS)[:, None],
        "mask": np.stack([first, window], 1).astype(f32), "causal": (token <= key).astype(f32),
        "samp_mask": samp.astype(f32), "samp_causal": (same & (row <= col)).astype(f32),
        "seg_cols": np.broadcast_to(seg, (P, SEQS, NSAMP)).astype(f32), "seg_rows": seg.T.astype(f32),
        "cache_kT": a["cache_win_k"][0].transpose(3, 0, 2, 1),
        "cache_v": a["cache_win_v"][0].transpose(1, 0, 2, 3).reshape(WINDOW, SEQS, KV),
        "cache_k_rows": a["cache_win_k"][0].reshape(SEQS, WINDOW, KV),
        "cache_v_rows": a["cache_win_v"][0].reshape(SEQS, WINDOW, KV),
        "state": a["state_gla"][0],
        "wq": tiled(a["peer_w_q"][0]),
        "keys": np.stack([a["peer_keys1"][0], a["peer_keys2"][0]], 1).reshape(2 * HEADS, NKEYS, HALF).transpose(2, 0, 1),
        "u": a["peer_u"][0], "v": a["peer_v"][0],
    }
    nc = bacc.Bacc("TRN2", target_bir_lowering=False, num_devices=1)
    given, feeds = {}, {}
    for name, value in arrays.items():
        feeds[f"in_{name}"] = np.ascontiguousarray(value)
        given[name] = nc.dram_tensor(f"in_{name}", value.shape, F32, kind="ExternalInput").ap()
    outs = {name: nc.dram_tensor(f"out_{name}", shape, F32, kind="ExternalOutput").ap() for name, shape in OUTPUTS}
    build(nc, given.__getitem__, outs)
    result = run(nc, [feeds], core_ids=[0]).results[0]
    r = {name: result[f"out_{name}"] for name, _ in OUTPUTS}
    win = (1, 1, WINDOW, KV_HEADS, HD)
    return (r["y"][:SEQ].reshape(1, SEQ, D), r["y"][SEQ:].reshape(SEQS, STEPS, D),
            r["pk"].reshape(win), r["pv"].reshape(win), r["ps"].reshape(1, 1, GLA_HEADS, DK, DV),
            r["sk"].reshape(1, SEQS, WINDOW, KV_HEADS, HD), r["sv"].reshape(1, SEQS, WINDOW, KV_HEADS, HD),
            r["ss"].reshape(1, SEQS, GLA_HEADS, DK, DV))
```
